# Optimizing a Trainium2 kernel written in Bass

```python
import math
import jax, jax.numpy as jnp
from jax import lax
import numpy as np

D_MODEL = 1024
BATCH = 1
SEQ = 1024
DEPTH = 2

CHUNK = 64
N_META = 16
CONV_W = 3
N_HEADS = 8
HEAD_DIM = D_MODEL // N_HEADS // 2
V_DIM = 2 * HEAD_DIM
Q_BLOCK = 128
N_A = max(1, DEPTH // 2)
N_B = DEPTH - N_A
EPS = 1e-6

kernel_name = "yoco_shortconv_diffattn_meta"

def rmsnorm(x, g):
    xf = x.astype(jnp.float32)
    y = xf * lax.rsqrt(jnp.mean(xf * xf, axis=-1, keepdims=True) + EPS)
    return (y * g.astype(jnp.float32)).astype(x.dtype)

def chunk_ids(n):
    p = jnp.arange(n)
    return jnp.where(p < N_META, 0, 1 + (p - N_META) // CHUNK)

def lambda_init_fn(depth):
    return 0.8 - 0.6 * math.exp(-0.3 * depth)

def short_conv_mixer(h, g, w_in, conv_w, conv_b, w_out):
    L = h.shape[1]
    u = rmsnorm(h, g) @ w_in
    b_gate, c_gate, h_in, z = jnp.split(u, 4, axis=-1)
    v = c_gate * h_in
    vp = jnp.pad(v, ((0, 0), (CONV_W - 1, 0), (0, 0)))
    conv = conv_w[0] * vp[:, 0:L]
    for j in range(1, CONV_W):
        conv = conv + conv_w[j] * vp[:, j:j + L]
    conv = conv + conv_b
    y = b_gate * conv * jax.nn.silu(z)
    return y @ w_out

def diff_attention_core(q, k, v, lam):
    bsz, L = q.shape[0], q.shape[1]
    n_blocks = -(-L // Q_BLOCK)
    Lp = n_blocks * Q_BLOCK
    qp = jnp.pad(q, ((0, 0), (0, Lp - L), (0, 0), (0, 0), (0, 0)))
    qb = qp.reshape(bsz, n_blocks, Q_BLOCK, N_HEADS, 2, HEAD_DIM).transpose(1, 0, 2, 3, 4, 5)
    qcid = chunk_ids(Lp).reshape(n_blocks, Q_BLOCK)
    kcid = chunk_ids(L)
    kf = k.astype(jnp.float32)
    vf = v.astype(jnp.float32)
    scale = HEAD_DIM ** -0.5

    def block(args):
        qi, ci = args
        s = jnp.einsum('bqhcd,bkhcd->bhcqk', qi.astype(jnp.float32), kf) * scale
        mask = ci[:, None] >= kcid[None, :]
        s = jnp.where(mask[None, None, None], s, -jnp.inf)
        p = jax.nn.softmax(s, axis=-1)
        attn = p[:, :, 0] - lam * p[:, :, 1]
        return jnp.einsum('bhqk,bkhe->bqhe', attn, vf)

    o = lax.map(block, (qb, qcid))
    o = o.transpose(1, 0, 2, 3, 4).reshape(bsz, Lp, N_HEADS, V_DIM)
    return o[:, :L]

def diff_attn_mixer(h, g, w_in, lq1, lk1, lq2, lk2, subln_g, w_out, k, v, lambda_init):
    bsz, L, _ = h.shape
    u = rmsnorm(h, g) @ w_in
    q, z = jnp.split(u, 2, axis=-1)
    q = q.reshape(bsz, L, N_HEADS, 2, HEAD_DIM)
    lam = (jnp.exp(jnp.sum(lq1.astype(jnp.float32) * lk1.astype(jnp.float32)))
           - jnp.exp(jnp.sum(lq2.astype(jnp.float32) * lk2.astype(jnp.float32)))
           + lambda_init)
    o = diff_attention_core(q, k, v, lam)
    o = rmsnorm(o, subln_g) * (1.0 - lambda_init)
    o = o.reshape(bsz, L, N_HEADS * V_DIM).astype(h.dtype) * jax.nn.silu(z)
    return o @ w_out

def setup_inputs(seed: int = 0) -> dict:
    key = jax.random.key(seed)
    ks = jax.random.split(key, 20)
    D = D_MODEL
    s = D ** -0.5
    nrm = lambda k, shp, sc: jax.random.normal(k, shp, jnp.float32) * sc
    return {
        "x": nrm(ks[0], (BATCH, SEQ, D), 1.0),
        "meta_tokens": nrm(ks[1], (N_META, D), 1.0),
        "a_norm_g": 1.0 + nrm(ks[2], (N_A, D), 0.02),
        "a_w_in": nrm(ks[3], (N_A, D, 4 * D), s),
        "a_conv_w": nrm(ks[4], (N_A, CONV_W, D), CONV_W ** -0.5),
        "a_conv_b": nrm(ks[5], (N_A, D), 0.02),
        "a_w_out": nrm(ks[6], (N_A, D, D), s),
        "kv_norm_g": 1.0 + nrm(ks[7], (D,), 0.02),
        "w_kv": nrm(ks[8], (D, 2 * D), s),
        "b_norm_g": 1.0 + nrm(ks[9], (N_B, D), 0.02),
        "b_w_in": nrm(ks[10], (N_B, D, 2 * D), s),
        "b_lambda_q1": nrm(ks[11], (N_B, HEAD_DIM), 0.1),
        "b_lambda_k1": nrm(ks[12], (N_B, HEAD_DIM), 0.1),
        "b_lambda_q2": nrm(ks[13], (N_B, HEAD_DIM), 0.1),
        "b_lambda_k2": nrm(ks[14], (N_B, HEAD_DIM), 0.1),
        "b_subln_g": 1.0 + nrm(ks[15], (N_B, V_DIM), 0.02),
        "b_w_out": nrm(ks[16], (N_B, D, D), s),
        "final_norm_g": 1.0 + nrm(ks[17], (D,), 0.02),
    }

def reference(x, meta_tokens, a_norm_g, a_w_in, a_conv_w, a_conv_b, a_w_out,
              kv_norm_g, w_kv, b_norm_g, b_w_in, b_lambda_q1, b_lambda_k1,
              b_lambda_q2, b_lambda_k2, b_subln_g, b_w_out, final_norm_g):
    bsz = x.shape[0]
    meta = jnp.broadcast_to(meta_tokens[None].astype(x.dtype), (bsz, N_META, D_MODEL))
    h = jnp.concatenate([meta, x], axis=1)
    L = h.shape[1]
    k_sh = None
    v_sh = None
    for i in range(DEPTH):
        if i < N_A:
            h = h + short_conv_mixer(h, a_norm_g[i], a_w_in[i], a_conv_w[i],
                                     a_conv_b[i], a_w_out[i])
            if i == N_A - 1:
                kv = rmsnorm(h, kv_norm_g) @ w_kv
                k_sh = kv[..., :D_MODEL].reshape(bsz, L, N_HEADS, 2, HEAD_DIM)
                v_sh = kv[..., D_MODEL:].reshape(bsz, L, N_HEADS, V_DIM)
        else:
            j = i - N_A
            h = h + diff_attn_mixer(h, b_norm_g[j], b_w_in[j], b_lambda_q1[j],
                                    b_lambda_k1[j], b_lambda_q2[j], b_lambda_k2[j],
                                    b_subln_g[j], b_w_out[j], k_sh, v_sh,
                                    lambda_init_fn(i))
    h = rmsnorm(h, final_norm_g)
    return h[:, N_META:]


_drawn_inputs = setup_inputs


def setup_inputs(seed=0):
    import zlib

    import numpy as np

    out = dict(_drawn_inputs(seed))
    spreads = {}
    factors = {'a_conv_b': 4.561,
     'kv_norm_g': 5.598,
     'b_norm_g': 5.96,
     'b_lambda_k1': 3.255,
     'b_lambda_q2': 3.132,
     'b_lambda_k2': 4.716,
     'b_subln_g': 8.0,
     'final_norm_g': 2.875}
    for name, (base, spread) in spreads.items():
        noise = np.random.default_rng([zlib.crc32(name.encode()), seed]).standard_normal(out[name].shape)
        drawn = base * np.exp(spread * noise) if base else spread * noise
        out[name] = __import__('jax').numpy.asarray(drawn.astype(out[name].dtype))
    for name, factor in factors.items():
        out[name] = (out[name] * factor).astype(out[name].dtype)
    return out
```

```python
import math
from contextlib import ExitStack

import concourse.bass as bass
from concourse import mybir

P = 128
EPS = 1e-6
LAMBDA_INIT = 0.8 - 0.6 * math.exp(-0.3 * 1)

ALU = mybir.AluOpType
ACT = mybir.ActivationFunctionType
F32 = mybir.dt.float32
F32R = mybir.dt.float32r
BF16 = mybir.dt.bfloat16
AX_X = mybir.AxisListType.X
MASKED = -1.0e30


def yoco_kernel(nc, x, meta_tokens, a_norm_g, a_w_in, a_conv_w, a_conv_b, a_w_out, kv_norm_g, w_kv,
                b_norm_g, b_w_in, b_lambda_q1, b_lambda_k1, b_lambda_q2, b_lambda_k2, b_subln_g,
                b_w_out, final_norm_g, out):
    _, T, D = x.shape
    M = meta_tokens.shape[0]
    L = T + M
    KT = D // P
    NT = T // P
    CW = 348
    LP = 3 * CW
    NH = KT
    HD = P // 2
    QW = 512
    SCALE = HD ** -0.5
    assert L <= LP and T == 2 * QW and NH * P == D and a_conv_w.shape[1] == 3

    x_rows = x[0]
    out_rows = out[0]
    w_in_a = a_w_in[0].rearrange("(k p) n -> p k n", p=P)
    w_out_a = a_w_out[0].rearrange("(k p) n -> p k n", p=P)
    w_kv_v = w_kv.rearrange("(k p) n -> p k n", p=P)
    w_in_b = b_w_in[0].rearrange("(k p) n -> p k n", p=P)
    w_out_b = b_w_out[0].rearrange("(k p) n -> p k n", p=P)
    h1_dram = nc.dram_tensor("h1_scratch", [T, D], F32, kind="Internal").ap()
    y_dram = nc.dram_tensor("y_scratch", [P, NH, T], F32, kind="Internal").ap()

    with ExitStack() as ctx:
        def sb(name, shape, dt):
            return ctx.enter_context(nc.sbuf_tensor(name, shape, dt))

        def sem(name):
            return ctx.enter_context(nc.semaphore(name))

        X_hi = sb("X_hi", [P, KT, LP], F32R)
        X_lo = sb("X_lo", [P, KT, LP], F32R)
        ring = sb("ring", [P, 2, 2, KT, P], F32R)
        BIGW = 2 * KT * D
        big = sb("big", [P, BIGW], F32R)
        wo_hi = big[:, 0:KT * D].rearrange("p (k n) -> p k n", k=KT)
        wo_lo = big[:, KT * D:2 * KT * D].rearrange("p (k n) -> p k n", k=KT)
        keys = [big[:, 2 * LP * c:2 * LP * (c + 1)].rearrange("p (s n) -> p s n", s=2) for c in range(2)]
        at = 4 * LP
        queries = [big[:, at + T * c:at + T * (c + 1)] for c in range(2)]
        at += 2 * T
        NK = NT + 1
        V = big[:, at:at + 2 * NK * P].rearrange("p (s j v) -> p s j v", s=2, j=NK)
        at += 2 * NK * P
        attn_t = big[:, at:at + 2 * NK * 2 * P].rearrange("p (s j q) -> p s j q", s=2, j=NK)
        assert at + 4 * NK * P <= BIGW

        WORK = KT * LP + 2 * D + D + 3 * LP + 16
        work = sb("work", [P, WORK], F32)
        raw_at = KT * LP
        misc_at = raw_at + 2 * D
        raw = [work[:, raw_at + D * s:raw_at + D * (s + 1)].rearrange("p (k n) -> p k n", k=KT) for s in range(2)]
        x0 = [work[:, D * s:D * (s + 1)] for s in range(2)]
        Y = work[:, 0:KT * LP].rearrange("p (k n) -> p k n", k=KT)
        raw_o = work[:, misc_at:misc_at + D].rearrange("p (k n) -> p k n", k=KT)
        cz = work[:, misc_at + D:misc_at + D + LP]
        vpad = work[:, misc_at + D + LP:misc_at + D + 2 * LP + 2]
        conv = work[:, misc_at + D + 2 * LP + 2:misc_at + D + 3 * LP + 2]
        xt = [work[:, misc_at + D * s:misc_at + D * (s + 1)] for s in range(2)]
        ht = [work[:, misc_at + D * (2 + s):misc_at + D * (3 + s)] for s in range(2)]
        E = [[work[:, LP * (2 * s + c):LP * (2 * s + c + 1)] for c in range(2)] for s in range(2)]
        v_t = work[:, 4 * LP:5 * LP]
        z_act = work[:, 5 * LP:5 * LP + T]
        o_t = work[:, 6 * LP:6 * LP + T]
        r_o = work[:, 7 * LP:7 * LP + T]
        y_o = work[:, misc_at:misc_at + T]
        o_sq = work[:, misc_at + T:misc_at + T + 2 * P]
        y4 = [work[:, D * s:D * (s + 1)].rearrange("p (k n) -> p k n", k=NH) for s in range(2)]
        h4 = [work[:, D * (2 + s):D * (3 + s)] for s in range(2)]
        o4 = [work[:, D * (4 + s):D * (5 + s)] for s in range(2)]
        g_final = work[:, 7 * D:8 * D]

        ident = sb("ident", [P, P], F32)
        ones = sb("ones", [P, P], F32)
        mask_q = sb("mask_q", [P, P], BF16)
        mask_k = sb("mask_k", [P, HD + LP - L], BF16)
        gain_rows = work[:, misc_at + D:misc_at + D + P]
        gains = sb("gains", [P, 8 * KT], F32)
        g_a = gains[:, 0:KT]
        g_kv = gains[:, KT:2 * KT]
        g_b = gains[:, 2 * KT:3 * KT]
        conv_b = gains[:, 3 * KT:4 * KT]
        conv_w = gains[:, 4 * KT:7 * KT].rearrange("p (j k) -> p j k", j=3)
        g_sub = sb("g_sub", [P, 2], F32)
        lam_in = sb("lam_in", [P, 4, HD], F32)
        lam_s = sb("lam_s", [P, 8], F32)
        eps = sb("eps", [P, 1], F32)
        stat = sb("stat", [P, 2, 8], F32)
        neg_max = sb("neg_max", [P, 2, 2], F32)
        z_sum = sb("z_sum", [P, 2, 2], F32)
        z_inv = sb("z_inv", [P, 2, 3], F32)
        ps = ctx.enter_context(nc.psum_tensor("ps", [P, 8, 512], F32))

        def flat(bank, width):
            return ps[:].rearrange("p b n -> p (b n)")[:, bank * 512:bank * 512 + width]

        const_in = sem("const_in")
        rows_zero = sem("rows_zero")
        gains_mm = sem("gains_mm")
        gains_done = sem("gains_done")
        ident_made = sem("ident_made")
        masks_made = sem("masks_made")
        pads_zero = sem("pads_zero")
        lam_step = sem("lam_step")
        lam_exp = sem("lam_exp")
        lam_done = sem("lam_done")
        x_in = [sem(f"x_in{s}") for s in range(2)]
        sq_done = sem("sq_done")
        ln_done = sem("ln_done")
        r0_done = sem("r0_done")
        newton = sem("newton")
        xn_done = sem("xn_done")
        tr_done = sem("tr_done")
        xh_done = sem("xh_done")
        xl_done = sem("xl_done")
        raw_in = [sem(f"raw_in{s}") for s in range(2)]
        w_scaled = sem("w_scaled")
        w_hi = sem("w_hi")
        w_lo = sem("w_lo")
        c_done = sem("c_done")
        v_done = sem("v_done")
        conv_step = sem("conv_step")
        b_done = sem("b_done")
        z_done = sem("z_done")
        y_done = sem("y_done")
        o_in = sem("o_in")
        o_hi = sem("o_hi")
        o_lo = sem("o_lo")
        y_hi = sem("y_hi")
        y_lo = sem("y_lo")
        out_mm = sem("out_mm")
        h1_done = sem("h1_done")
        vpad_zero = sem("vpad_zero")
        v_zero = sem("v_zero")
        h1_stored = [sem(f"h1_stored{s}") for s in range(2)]
        unit_mm = sem("unit_mm")
        chunk_mm = sem("chunk_mm")
        chunk_hi = sem("chunk_hi")
        kq_out = sem("kq_out")
        vz_out = sem("vz_out")
        keys_dup = sem("keys_dup")
        s_mm = sem("s_mm")
        s_out = sem("s_out")
        exp_done = sem("exp_done")
        recip_done = sem("recip_done")
        inv_done = sem("inv_done")
        e1_scaled = sem("e1_scaled")
        attn_done = sem("attn_done")
        round_mm = sem("round_mm")
        round_hi = sem("round_hi")
        round_lo = sem("round_lo")
        pv_mm = sem("pv_mm")
        o_copied = sem("o_copied")
        o_squared = sem("o_squared")
        ms_mm = sem("ms_mm")
        ms_ln = sem("ms_ln")
        r_done = sem("r_done")
        or_done = sem("or_done")
        y_head = sem("y_head")
        y_stored = sem("y_stored")
        wb_in = [sem(f"wb_in{s}") for s in range(2)]
        wb_hi = sem("wb_hi")
        wb_lo = sem("wb_lo")
        y4_in = [sem(f"y4_in{s}") for s in range(2)]
        h4_in = [sem(f"h4_in{s}") for s in range(2)]
        gf_in = sem("gf_in")
        y4_hi = sem("y4_hi")
        y4_lo = sem("y4_lo")
        out4_mm = sem("out4_mm")
        h2_done = sem("h2_done")
        o4_done = sem("o4_done")
        o4_stored = [sem(f"o4_stored{s}") for s in range(2)]

        NCONST = 14
        U1 = 4 * KT
        UH = 4
        CHUNKS = 10
        CHUNK_OF = {"V": 0, "K": 3, "Q": 6, "Z": 8}
        RH = 18
        RP = 4
        SLOT = {"V": 1, "K": 0, "Q": 1, "Z": 0}

        def rounds_of(i):
            tiles = list(range(1, i + 2)) + [0]
            return [tiles[a:a + 4] for a in range(0, len(tiles), 4)]

        ROUND_AT = [sum(len(rounds_of(a)) for a in range(i)) for i in range(NT)]
        V_ROUNDS = [[1, 2, 3], [4, 5, 6], [7, 8], [0]]
        assert ROUND_AT[-1] + len(rounds_of(NT - 1)) + len(V_ROUNDS) == RH

        def round_bank(n):
            return 5 + n % 2

        def chunk_bank(kind, c):
            return 3 + (CHUNK_OF[kind] + c) % 2

        def tr_bank(slot):
            return 6 - 2 * slot

        def s_shape(i):
            n = M + P * (i + 1)
            if n <= 512:
                return 1, n
            if n <= 1024:
                return 2, n // 2
            return 3, CW

        def key_col(j):
            return 0 if j == 0 else M + P * (j - 1)

        block = ctx.enter_context(nc.Block())

        @block.sync
        def _(sp):
            def load_x(t, slot, dst, sems):
                if t is None:
                    sp.dma_start(dst[slot][0:M, :], meta_tokens).then_inc(sems[slot], 16)
                    sp.dma_start(dst[slot][M:P, :], x_rows[0:P - M, :]).then_inc(sems[slot], 16)
                else:
                    sp.dma_start(dst[slot], x_rows[bass.ds(t * P, P), :]).then_inc(sems[slot], 16)

            load_x(None, 0, x0, x_in)
            load_x(0, 1, x0, x_in)
            for r, v in enumerate((a_norm_g[0], kv_norm_g, b_norm_g[0], a_conv_b[0], a_conv_w[0, 0], a_conv_w[0, 1],
                                   a_conv_w[0, 2])):
                sp.dma_start(gain_rows[KT * r:KT * (r + 1), :], v.rearrange("(k p) -> k p", p=P)).then_inc(const_in, 16)
            sp.dma_start(gain_rows[7 * KT:8 * KT, :], b_subln_g[0:1, :].to_broadcast([KT, P])).then_inc(const_in, 16)
            for j, v in enumerate((b_lambda_q1, b_lambda_k1, b_lambda_q2, b_lambda_k2)):
                sp.dma_start(lam_in[:, j, :], v[0:1, :].to_broadcast([P, HD])).then_inc(const_in, 16)

            def load_unit(u, slot, w, col):
                sp.wait_ge(w_hi, u - 1)
                sp.wait_ge(w_lo, u - 1)
                sp.dma_start(raw[slot], w[:, :, bass.ds(col, P)]).then_inc(raw_in[slot], 16)

            ORDER = (1, 2, 0, 3)
            for n in range(2):
                sp.dma_start(raw[n], w_in_a[:, :, ORDER[n] * D:ORDER[n] * D + P]).then_inc(raw_in[n], 16)
            for t in range(2, NT + 1):
                sp.wait_ge(tr_done, t - 1)
                load_x(t - 1, t % 2, x0, x_in)
            sp.dma_start(raw_o, w_out_a[:, :, 0:P]).then_inc(o_in, 16)
            for n in (2, 3):
                load_unit(n, n % 2, w_in_a, ORDER[n] * D)
            with sp.Fori(1, KT) as f:
                sp.wait_ge(o_hi, f)
                sp.wait_ge(o_lo, f)
                sp.dma_start(raw_o, w_out_a[:, :, bass.ds(f * P, P)]).then_inc(o_in, 16)
                for n in range(4):
                    load_unit(4 * f + n, n % 2, w_in_a, f * P + ORDER[n] * D)

            sp.wait_ge(o_hi, KT)
            sp.wait_ge(o_lo, KT)
            sp.wait_ge(y_done, KT)
            load_x(None, 0, xt, x_in)
            load_x(0, 1, xt, x_in)
            def load_head_unit(u, kind, h, ahead=0):
                slot = SLOT[kind]
                w, col = {"V": (w_kv_v, D), "K": (w_kv_v, 0), "Q": (w_in_b, 0), "Z": (w_in_b, D)}[kind]
                load_unit(u, slot, w, h * P + (col + ahead * P))

            sp.wait_ge(w_hi, U1)
            sp.wait_ge(w_lo, U1)
            load_head_unit(U1, "V", 0)
            sp.dma_start(raw[SLOT["K"]], w_kv_v[:, :, 0:P]).then_inc(raw_in[SLOT["K"]], 16)

            def store_h1(t, slot):
                sp.wait_ge(h1_done, t + 1)
                sp.dma_start(h1_dram[bass.ds((t - 1) * P, P), :], ht[slot]).then_inc(h1_stored[slot], 16)

            def step2(t, slot):
                sp.wait_ge(tr_done, NT + 1 + t)
                load_x(t, 1 - slot, xt, x_in)
                store_h1(t, slot)

            with sp.Fori(0, (NT - 2) // 2) as i:
                step2(2 * i + 1, 1)
                step2(2 * i + 2, 0)
            step2(NT - 1, 1)
            store_h1(NT, 0)

            def dup_keys(h):
                sp.wait_ge(kq_out, 5 * h + 3)
                sp.dma_start(keys[0][HD:P].bitcast(F32), keys[0][0:HD].bitcast(F32)).then_inc(keys_dup, 16)
                sp.dma_start(keys[1][0:HD].bitcast(F32), keys[1][HD:P].bitcast(F32)).then_inc(keys_dup, 16)

            load_head_unit(U1 + 2, "Q", 0)
            load_head_unit(U1 + 3, "Z", 0)

            def store_y(h):
                sp.wait_ge(y_head, h + 1)
                sp.dma_start(y_dram[:, bass.ds(h, 1), :], y_o.rearrange("p (a n) -> p a n", a=1)).then_inc(y_stored, 16)

            def head(h, ahead):
                u = U1 + 4 + UH * h
                load_head_unit(u + 2, "Q", h + 1)
                load_head_unit(u + 3, "Z", h + 1)
                if ahead:
                    load_head_unit(u + 4, "V", h + 1, 1)
                dup_keys(h + 1)
                if ahead:
                    load_head_unit(u + 5, "K", h + 1, 1)
                store_y(h)

            load_head_unit(U1 + 4, "V", 1)
            dup_keys(0)
            load_head_unit(U1 + 5, "K", 1)
            with sp.Fori(0, NH - 2) as h:
                head(h, True)
            head(NH - 2, False)
            UL = U1 + 4 + UH * (NH - 1)
            sp.wait_ge(w_hi, UL)
            sp.wait_ge(w_lo, UL)
            for j in range(KT):
                if j >= 2:
                    sp.wait_ge(wb_hi, j - 1)
                    sp.wait_ge(wb_lo, j - 1)
                sp.dma_start(raw[j % 2], w_out_b[:, :, j * P:(j + 1) * P]).then_inc(wb_in[j % 2], 16)
            store_y(NH - 1)

            sp.dma_start(g_final, final_norm_g.rearrange("(a n) -> a n", a=1).to_broadcast([P, D])).then_inc(gf_in, 16)
            for s in range(2):
                sp.wait_ge(h1_stored[s], 16 * (NT // 2))
            sp.wait_ge(y_stored, 16 * NH)

            def load4(t, slot):
                sp.dma_start(y4[slot], y_dram[:, :, bass.ds(t * P, P)]).then_inc(y4_in[slot], 16)
                sp.dma_start(h4[slot], h1_dram[bass.ds(t * P, P), :]).then_inc(h4_in[slot], 16)

            def store4(t, slot):
                sp.wait_ge(o4_done, t + 1)
                sp.dma_start(out_rows[bass.ds(t * P, P), :], o4[slot]).then_inc(o4_stored[slot], 16)

            load4(0, 0)
            load4(1, 1)
            with sp.Fori(0, NT // 2 - 1) as i:
                for s in range(2):
                    t = 2 * i + s
                    store4(t, s)
                    sp.wait_ge(y4_lo, t + 1)
                    load4(t + 2, s)
            for s in range(2):
                store4(NT - 2 + s, s)
            for s in range(2):
                sp.wait_ge(o4_stored[s], 16 * (NT // 2))

        @block.gpsimd
        def _(pool):
            nc.gpsimd.memset(ident[:], 0.0).then_inc(ident_made, 1)
            nc.gpsimd.memset(ones[:], 1.0).then_inc(ident_made, 1)
            nc.gpsimd.memset(eps[:], EPS).then_inc(ident_made, 1)
            pool.wait_ge(ident_made, 3)
            nc.gpsimd.affine_select(out=ident[:], in_=ident[:], compare_op=ALU.not_equal, fill=1.0, base=0,
                                    pattern=[[-1, P]], channel_multiplier=1).then_inc(ident_made, 1)
            pool.wait_ge(ident_made, 4)
            nc.gpsimd.memset(gain_rows[8 * KT:P, :], 0.0).then_inc(rows_zero, 1)
            pool.wait_ge(rows_zero, 1)
            nc.gpsimd.memset(X_hi[:, :, L:LP].bitcast(F32), 0.0).then_inc(pads_zero, 1)
            nc.gpsimd.memset(X_lo[:, :, L:LP].bitcast(F32), 0.0).then_inc(pads_zero, 1)
            nc.gpsimd.memset(mask_q[:], 0.0).then_inc(masks_made, 1)
            nc.gpsimd.memset(mask_k[:], 0.0).then_inc(masks_made, 1)
            pool.wait_ge(masks_made, 2)
            for n, (rows, value) in enumerate((
                    (mask_q[0:2, :], 1.0), (mask_k[0:2, HD:], MASKED), (mask_q[0:1, HD:P], 0.0),
                    (mask_k[0:1, 0:HD], MASKED), (mask_k[0:1, HD:], 0.0))):
                nc.gpsimd.memset(rows, value).then_inc(masks_made, 1)
                pool.wait_ge(masks_made, n + 3)

            def scale_unit(u, slot, count, g):
                pool.wait_ge(raw_in[slot], count)
                nc.gpsimd.tensor_tensor(raw[slot], raw[slot], g.unsqueeze(2).to_broadcast([P, KT, P]),
                                        ALU.mult).then_inc(w_scaled, 1)

            pool.wait_ge(gains_done, 1)
            with pool.Fori(0, KT) as f:
                for n in range(4):
                    scale_unit(4 * f + n, n % 2, 32 * f + 16 * (n // 2 + 1), g_a)
            R1 = 16 * (U1 // 2)
            scale_unit(U1, 1, R1 + 16, g_kv)
            scale_unit(U1 + 1, 0, R1 + 16, g_kv)
            scale_unit(U1 + 2, 1, R1 + 32, g_b)
            scale_unit(U1 + 3, 0, R1 + 32, g_b)

            def scale_e1(h, i):
                pool.wait_ge(inv_done, NT * h + i + 1)
                nb, w = s_shape(i)
                e1 = E[i % 2][1][:, 0:nb * w]
                nc.gpsimd.tensor_tensor(e1, e1, z_inv[:, i % 2, 2:3].to_broadcast([P, nb * w]),
                                        ALU.mult).then_inc(e1_scaled, 1)

            def head(h, last):
                for i in range(NT):
                    if not last:
                        u = U1 + 4 + UH * h
                        at = R1 + 32 + 32 * h
                        if i == 0:
                            scale_unit(u, 1, at + 16, g_kv)
                        if i == 2:
                            scale_unit(u + 1, 0, at + 16, g_kv)
                        if i == 5:
                            scale_unit(u + 2, 1, at + 32, g_b)
                        if i == 7:
                            scale_unit(u + 3, 0, at + 32, g_b)
                    scale_e1(h, i)
                pool.wait_ge(r_done, h + 1)
                nc.gpsimd.tensor_tensor(o_t, o_t, r_o, ALU.mult).then_inc(or_done, 1)

            with pool.Fori(0, NH - 1) as h:
                head(h, False)
            head(NH - 1, True)

        @block.scalar
        def _(act):
            def unit_hi(u, slot, sem_used, used):
                act.wait_ge(w_scaled, u + 1)
                if used is not None:
                    act.wait_ge(sem_used, used)
                nc.scalar.activation(ring[:, slot, 0], raw[slot], ACT.Copy).then_inc(w_hi, 1)

            def stats(n, slot, src):
                s = stat[:, slot]
                nc.scalar.activation(flat(tr_bank(slot), D), src, ACT.Square, accum_out=s[:, 0:1]).then_inc(sq_done, 1)
                act.wait_ge(sq_done, n + 1)
                nc.scalar.activation(s[:, 2:3], s[:, 0:1], ACT.Ln, bias=eps[:], scale=1.0 / D).then_inc(ln_done, 1)
                act.wait_ge(ln_done, n + 1)
                nc.scalar.activation(s[:, 3:4], s[:, 2:3], ACT.Exp, scale=-0.5).then_inc(r0_done, 1)

            def x_hi(n, slot, col, width):
                act.wait_ge(tr_done, n + 1)
                nc.scalar.activation(X_hi[:, :, bass.ds(col, width)],
                                     flat(tr_bank(slot), D).rearrange("p (k n) -> p k n", k=KT)[:, :, 0:width],
                                     ACT.Copy).then_inc(xh_done, 1)

            nc.scalar.preload_act_table_set("natural_log_exp_and_others")
            act.wait_ge(ident_made, 3)
            act.wait_ge(x_in[0], 32)
            stats(0, 0, x0[0])
            for t in range(1, NT + 1):
                act.wait_ge(x_in[t % 2], 32 + 16 * (t // 2) if t % 2 == 0 else 16 * (t // 2 + 1))
                pass
                if t >= 2:
                    act.wait_ge(xn_done, t - 1)
                    act.wait_ge(xl_done, t - 1)
                stats(t, t % 2, x0[t % 2])
                x_hi(t - 1, (t - 1) % 2, key_col(t - 1), M if t == 1 else P)
            act.wait_ge(gains_mm, 1)
            nc.scalar.activation(gains[:], ps[:, 0, 0:8 * KT], ACT.Copy).then_inc(gains_done, 1)
            act.wait_ge(lam_step, 4)
            nc.scalar.activation(lam_s[:, 2:4], lam_s[:, 0:2], ACT.Exp).then_inc(lam_exp, 1)
            unit_hi(0, 0, None, None)
            x_hi(NT, NT % 2, key_col(NT), P)

            def feature(f, last):
                unit_hi(4 * f + 1, 1, unit_mm, 4 * f)
                act.wait_ge(unit_mm, 4 * f + 1)
                act.wait_ge(y_done, f)
                nc.scalar.activation(cz.rearrange("p (b n) -> p b n", b=3), ps[:, 0:3, 0:CW], ACT.Copy).then_inc(c_done, 1)
                unit_hi(4 * f + 2, 0, unit_mm, 4 * f + 1)
                unit_hi(4 * f + 3, 1, unit_mm, 4 * f + 2)
                act.wait_ge(o_in, 16 * f + 16)
                nc.scalar.activation(wo_hi[:, :, bass.ds(f * P, P)], raw_o, ACT.Copy).then_inc(o_hi, 1)
                if not last:
                    unit_hi(4 * f + 4, 0, unit_mm, 4 * f + 3)
                act.wait_ge(unit_mm, 4 * f + 4)
                act.wait_ge(v_done, f + 1)
                nc.scalar.activation(cz.rearrange("p (b n) -> p b n", b=3), ps[:, 3:6, 0:CW], ACT.Silu).then_inc(z_done, 1)

            with act.Fori(0, KT - 1) as f:
                feature(f, False)
            feature(KT - 1, True)

            nc.scalar.preload_act_table_set("natural_log_exp_and_others")

            def y_tile_hi(t, slot, col):
                act.wait_ge(y_done, KT)
                nc.scalar.activation(ring[:, slot, 0], Y[:, :, bass.ds(col, P)], ACT.Copy).then_inc(y_hi, 1)

            N2 = NT + 1

            def step2(t, par, nxt=True, prev=True, prev2=True, meta2=False):
                if nxt:
                    act.wait_ge(out_mm, t)
                    y_tile_hi(t + 1, 1 - par, M + t * P)
                if prev2:
                    x_hi(N2 + t - 2, par, 0 if meta2 else M + (t - 3) * P, M if meta2 else P)
                if prev:
                    act.wait_ge(h1_done, t)
                    act.wait_ge(xn_done, N2 + t - 2)
                    act.wait_ge(xl_done, N2 + t - 2)
                    stats(N2 + t - 1, 1 - par, ht[1 - par])

            act.wait_ge(unit_mm, U1 - 1)
            y_tile_hi(0, 0, 0)
            act.wait_ge(unit_mm, U1)
            y_tile_hi(1, 1, M)
            step2(1, 1, prev2=False)
            step2(2, 0, meta2=True)
            with act.Fori(0, (NT - 4) // 2) as i:
                step2(2 * i + 3, 1)
                step2(2 * i + 4, 0)
            step2(NT - 1, 1)
            unit_hi(U1, SLOT["V"], out_mm, NT)
            step2(NT, 0, nxt=False)
            step2(NT + 1, 1, nxt=False)
            unit_hi(U1 + 1, SLOT["K"], out_mm, NT + 1)
            x_hi(N2 + NT, 0, M + (NT - 1) * P, P)

            def chunk(kind, h, c):
                act.wait_ge(chunk_mm, CHUNKS * h + CHUNK_OF[kind] + c + 1)
                return ps[:, chunk_bank(kind, c), 0:CW if kind in "VK" else QW]

            def v_chunk(h, c):
                b = chunk("V", h, c)
                nc.scalar.activation(v_t[:, CW * c:CW * (c + 1)], b, ACT.Copy).then_inc(vz_out, 1)

            def k_chunk_hi(h, c, scores=None):
                b = chunk("K", h, c)
                if scores is not None:
                    act.wait_ge(s_mm, scores)
                nc.scalar.activation(keys[0][0:HD, 0, CW * c:CW * (c + 1)], b[0:HD], ACT.Copy)
                nc.scalar.activation(keys[1][HD:P, 0, CW * c:CW * (c + 1)], b[HD:P], ACT.Copy).then_inc(chunk_hi, 1)

            def q_chunk_hi(h, c):
                b = chunk("Q", h, c)
                nc.scalar.activation(queries[0][0:HD, QW * c:QW * (c + 1)], b[0:HD], ACT.Copy)
                nc.scalar.activation(queries[1][HD:P, QW * c:QW * (c + 1)], b[HD:P], ACT.Copy).then_inc(chunk_hi, 1)

            def z_chunk(h, c):
                b = chunk("Z", h, c)
                nc.scalar.activation(z_act[:, QW * c:QW * (c + 1)], b, ACT.Silu).then_inc(vz_out, 1)

            def round_hi_v(n, par, tiles, pvs):
                act.wait_ge(round_mm, n + 1)
                if pvs is not None:
                    act.wait_ge(pv_mm, pvs)
                b = ps[:, round_bank(par), 0:P * len(tiles)]
                if tiles == [0]:
                    nc.scalar.activation(V[0:M, 0, 0, :], b[0:M], ACT.Copy).then_inc(round_hi, 1)
                else:
                    nc.scalar.activation(V[:, 0, tiles[0]:tiles[-1] + 1, :], b.rearrange("p (j v) -> p j v", v=P),
                                         ACT.Copy).then_inc(round_hi, 1)

            def round_hi_a(n, par, tiles, half, pvs):
                act.wait_ge(round_mm, n + 1)
                if pvs is not None:
                    act.wait_ge(pv_mm, pvs)
                b = ps[:, round_bank(par), 0:P * len(tiles)].rearrange("p (j q) -> p j q", q=P)
                qs = slice(P * half, P * half + P)
                full = [j for j in tiles if j]
                last = None
                if full:
                    last = nc.scalar.activation(attn_t[:, 0, full[0]:full[-1] + 1, qs], b[:, 0:len(full)], ACT.Copy)
                if 0 in tiles:
                    last = nc.scalar.activation(attn_t[:, 0, 0:1, qs], b[:, len(full):len(full) + 1], ACT.Copy)
                last.then_inc(round_hi, 1)

            def exp(h, i, c):
                n = 2 * (NT * h + i) + c
                act.wait_ge(s_out, n + 1)
                nb, w = s_shape(i)
                e = E[i % 2][c][:, 0:nb * w]
                nc.scalar.activation(e, e, ACT.Exp, bias=neg_max[:, i % 2, c:c + 1], scale=-1.0,
                                     accum_out=z_sum[:, i % 2, c:c + 1]).then_inc(exp_done, 1)

            def o_group(h, g):
                act.wait_ge(pv_mm, 4 * h + g + 1)
                nc.scalar.activation(o_t[:, 2 * P * g:2 * P * (g + 1)], ps[:, 7, 0:2 * P], ACT.Copy).then_inc(o_copied, 1)
                nc.scalar.activation(o_sq, ps[:, 7, 0:2 * P], ACT.Square).then_inc(o_squared, 1)

            def ln_group(h, g):
                act.wait_ge(ms_mm, 4 * h + g + 1)
                nc.scalar.activation(r_o[:, 2 * P * g:2 * P * (g + 1)], ps[:, 7, 0:2 * P], ACT.Ln, bias=eps[:],
                                     scale=1.0 / P).then_inc(ms_ln, 1)

            for c in range(3):
                v_chunk(0, c)
            for c in range(3):
                k_chunk_hi(0, c)
                if c == 0:
                    unit_hi(U1 + 2, SLOT["Q"], chunk_mm, 3)
            for r, tiles in enumerate(V_ROUNDS):
                round_hi_v(r, r, tiles, None)
            unit_hi(U1 + 3, SLOT["Z"], chunk_mm, 6)
            for c in range(2):
                q_chunk_hi(0, c)

            def wb_unit_hi(j):
                act.wait_ge(wb_in[j % 2], 16 * (j // 2 + 1))
                act.wait_ge(chunk_mm, CHUNKS * NH)
                nc.scalar.activation(X_hi[:, :, j * P:(j + 1) * P], raw[j % 2], ACT.Copy).then_inc(wb_hi, 1)

            def head(h, last):
                R0 = RP + RH * h
                u = U1 + 4 + UH * h
                for i in range(NT):
                    if not last and i == 1:
                        unit_hi(u, SLOT["V"], chunk_mm, CHUNKS * h + 8)
                    if not last and i == 4:
                        unit_hi(u + 1, SLOT["K"], chunk_mm, CHUNKS * h + 10)
                    exp(h, i, 0)
                    if not last and i == 4:
                        v_chunk(h + 1, 0)
                    if i >= 4 and i % 2 == 0:
                        ln_group(h, (i - 4) // 2)
                    exp(h, i, 1)
                    if i == 2:
                        act.wait_ge(y_head, h)
                        z_chunk(h, 0)
                        z_chunk(h, 1)
                        nc.scalar.preload_act_table_set("natural_log_exp_and_others")
                    if not last and i == 5:
                        v_chunk(h + 1, 1)
                    if not last and i == 7:
                        v_chunk(h + 1, 2)
                    if i >= 1:
                        attn_rounds(h, i - 1, R0)
                    if i >= 3 and i % 2 == 1:
                        o_group(h, (i - 3) // 2)
                    if last and i >= 4:
                        wb_unit_hi(2 * i - 8)
                        wb_unit_hi(2 * i - 7)
                if not last:
                    unit_hi(u + 2, SLOT["Q"], chunk_mm, CHUNKS * (h + 1) + 3)
                    k_chunk_hi(h + 1, 0, 2 * NT * (h + 1))
                attn_rounds(h, NT - 1, R0)
                if last:
                    ln_group(h, 2)
                else:
                    k_chunk_hi(h + 1, 1)
                    ln_group(h, 2)
                if last:
                    o_group(h, 3)
                if not last:
                    k_chunk_hi(h + 1, 2)
                    for r, tiles in enumerate(V_ROUNDS):
                        if r == 0:
                            o_group(h, 3)
                        round_hi_v(R0 + 14 + r, 14 + r, tiles, 4 * (h + 1))
                    unit_hi(u + 3, SLOT["Z"], chunk_mm, CHUNKS * (h + 1) + 6)
                    q_chunk_hi(h + 1, 0)
                ln_group(h, 3)
                if not last:
                    q_chunk_hi(h + 1, 1)
                act.wait_ge(ms_ln, 4 * (h + 1))
                nc.scalar.activation(r_o[:, 0:T], r_o[:, 0:T], ACT.Exp, scale=-0.5).then_inc(r_done, 1)

            def attn_rounds(h, i, R0):
                for r, tiles in enumerate(rounds_of(i)):
                    n = ROUND_AT[i] + r
                    pvs = 4 * h + i // 2 if i % 2 == 0 else None
                    round_hi_a(R0 + n, n, tiles, i % 2, pvs)

            with act.Fori(0, NH - 1) as h:
                head(h, False)
            head(NH - 1, True)

            def y4_hi_tile(t, slot):
                act.wait_ge(y4_in[slot], (t // 2 + 1) * 16)
                if t >= 2:
                    act.wait_ge(out4_mm, t - 1)
                nc.scalar.activation(ring[:, slot, 0], y4[slot], ACT.Copy).then_inc(y4_hi, 1)

            N4 = 2 * N2
            y4_hi_tile(0, 0)
            for t in range(NT):
                if t + 1 < NT:
                    y4_hi_tile(t + 1, (t + 1) % 2)
                act.wait_ge(h2_done, t + 1)
                if t >= 2:
                    act.wait_ge(o4_done, t - 1)
                stats(N4 + t, t % 2, h4[t % 2])

        @block.tensor
        def _(pe):
            N2 = NT + 1

            def three(out_ap, wh, wl, xh, xl, start, stop):
                pe.matmul(out_ap, wh, xh, start=start, stop=False)
                pe.matmul(out_ap, wh, xl, start=False, stop=False)
                return pe.matmul(out_ap, wl, xh, start=False, stop=stop)

            def transpose_tile(n, slot, src, reused=True):
                pe.wait_ge(xn_done, n + 1)
                if reused:
                    pe.wait_ge(xh_done, n - 1)
                    pe.wait_ge(xl_done, n - 1)
                for k in range(KT):
                    mm = pe.transpose(ps[:, tr_bank(slot) + k // 4, P * (k % 4):P * (k % 4) + P],
                                      src[:, k * P:(k + 1) * P], ident[:])
                mm.then_inc(tr_done, 1)

            pe.wait_ge(ident_made, 4)
            for t in range(NT + 1):
                transpose_tile(t, t % 2, x0[t % 2], reused=t >= 2)
                if t == 1:
                    pe.wait_ge(const_in, 16 * 12)
                    pe.wait_ge(rows_zero, 1)
                    pe.transpose(ps[:, 0, 0:P], gain_rows, ident[:]).then_inc(gains_mm, 1)

            def unit(u, slot, bank, read, count):
                pe.wait_ge(w_lo, u + 1)
                pe.wait_ge(read, count)
                for c in range(3):
                    for k in range(KT):
                        mm = three(ps[:, bank + c, 0:CW], ring[:, slot, 0, k], ring[:, slot, 1, k],
                                   X_hi[:, k, CW * c:CW * (c + 1)], X_lo[:, k, CW * c:CW * (c + 1)],
                                   k == 0, k == KT - 1)
                mm.then_inc(unit_mm, 1)

            pe.wait_ge(pads_zero, 2)
            pe.wait_ge(xh_done, NT + 1)
            pe.wait_ge(xl_done, NT + 1)
            with pe.Fori(0, KT) as f:
                unit(4 * f, 0, 0, b_done, f)
                unit(4 * f + 1, 1, 3, z_done, f)
                unit(4 * f + 2, 0, 0, c_done, f + 1)
                unit(4 * f + 3, 1, 3, v_done, f + 1)

            def out_tile(t, slot, hi_sem, lo_sem, wh, wl, read, count, done):
                pe.wait_ge(hi_sem, t + 1)
                pe.wait_ge(lo_sem, t + 1)
                if count is not None:
                    pe.wait_ge(read, count)
                for c in range(2):
                    for k in range(KT):
                        mm = three(ps[:, 2 * slot + c, :], ring[:, slot, 0, k], ring[:, slot, 1, k],
                                   wh[:, k, 512 * c:512 * (c + 1)], wl[:, k, 512 * c:512 * (c + 1)],
                                   k == 0, k == KT - 1)
                mm.then_inc(done, 1)

            def out2(t, slot, count):
                out_tile(t, slot, y_hi, y_lo, wo_hi, wo_lo, h1_done, count, out_mm)

            pe.wait_ge(o_hi, KT)
            pe.wait_ge(o_lo, KT)
            pe.wait_ge(b_done, KT)
            out2(0, 0, None)
            pe.wait_ge(z_done, KT)
            out2(1, 1, None)
            transpose_tile(N2, 0, xt[0])
            with pe.Fori(0, (NT - 2) // 2) as i:
                t = 2 * i + 2
                out2(t, 0, t - 1)
                transpose_tile(N2 + t - 1, 1, xt[1])
                out2(t + 1, 1, t)
                transpose_tile(N2 + t, 0, xt[0])
            out2(NT, 0, NT - 1)
            transpose_tile(N2 + NT - 1, 1, xt[1])

            def chunk(kind, h, c, read=None, count=0, k0=0, k1=KT):
                slot = SLOT[kind]
                width, first = (CW, 0) if kind in "VK" else (QW, M)
                if k0 == 0:
                    pe.wait_ge(w_lo, U1 + UH * h + "VKQZ".index(kind) + 1)
                    if read is not None:
                        pe.wait_ge(read, count)
                o = ps[:, chunk_bank(kind, c), 0:width]
                for k in range(k0, k1):
                    cols = slice(first + width * c, first + width * (c + 1))
                    mm = three(o, ring[:, slot, 0, k], ring[:, slot, 1, k], X_hi[:, k, cols], X_lo[:, k, cols],
                               k == 0, k == KT - 1)
                if k1 == KT:
                    mm.then_inc(chunk_mm, 1)

            def v_rounds(h, n0):
                pe.wait_ge(vz_out, 5 * h + 3)
                for r, tiles in enumerate(V_ROUNDS):
                    if n0 is not None:
                        pe.wait_ge(round_hi, n0 + r - 1)
                        pe.wait_ge(round_lo, n0 + r - 1)
                    elif r >= 2:
                        pe.wait_ge(round_hi, r - 1)
                        pe.wait_ge(round_lo, r - 1)
                    for q, j in enumerate(tiles):
                        mm = pe.transpose(ps[:, round_bank(r), P * q:P * (q + 1)],
                                          v_t[:, key_col(j):key_col(j) + P], ident[:])
                    mm.then_inc(round_mm, 1)

            pe.wait_ge(h1_done, NT)
            chunk("V", 0, 0)
            pe.wait_ge(xh_done, N2 + NT)
            pe.wait_ge(xl_done, N2 + NT)
            chunk("V", 0, 1)
            transpose_tile(N2 + NT, 0, xt[0])
            pe.wait_ge(xh_done, N2 + NT + 1)
            pe.wait_ge(xl_done, N2 + NT + 1)
            chunk("V", 0, 2, vz_out, 1)
            chunk("K", 0, 0, vz_out, 2)
            chunk("K", 0, 1, vz_out, 3)
            chunk("K", 0, 2, kq_out, 1)
            v_rounds(0, None)
            chunk("Q", 0, 0, kq_out, 2)
            chunk("Q", 0, 1, kq_out, 3)

            def scores(h, i, c):
                n = 2 * (NT * h + i) + c
                pe.wait_ge(s_out, n)
                nb, w = s_shape(i)
                q = queries[c][:, P * i:P * (i + 1)]
                for b in range(nb):
                    o = ps[:, b, 0:w]
                    pe.matmul(o, q, keys[c][:, 0, b * w:(b + 1) * w], start=True, stop=False)
                    pe.matmul(o, q, keys[c][:, 1, b * w:(b + 1) * w], start=False, stop=b < nb - 1)
                hidden = HD + (nb * w - (M + P * (i + 1)))
                pe.matmul(ps[:, nb - 1, w - hidden:w], mask_q[:], mask_k[:, 0:hidden], start=False,
                          stop=True).then_inc(s_mm, 1)

            def attn_rounds(h, i):
                pe.wait_ge(attn_done, NT * h + i + 1)
                for r, tiles in enumerate(rounds_of(i)):
                    n = ROUND_AT[i] + r
                    pe.wait_ge(round_hi, RP + RH * h + n - 1)
                    pe.wait_ge(round_lo, RP + RH * h + n - 1)
                    for q, j in enumerate(tiles):
                        mm = pe.transpose(ps[:, round_bank(n), P * q:P * (q + 1)],
                                          E[i % 2][0][:, key_col(j):key_col(j) + P], ident[:])
                    mm.then_inc(round_mm, 1)

            def products(h, g):
                n = RP + RH * h + ROUND_AT[2 * g + 1] + len(rounds_of(2 * g + 1))
                pe.wait_ge(round_hi, n)
                pe.wait_ge(round_lo, n)
                pe.wait_ge(ms_ln, 4 * h + g)
                for j in range(2 * g + 3):
                    q = slice(P if j == 2 * g + 2 else 0, 2 * P)
                    mm = three(ps[:, 7, q], V[:, 0, j], V[:, 1, j], attn_t[:, 0, j, q], attn_t[:, 1, j, q],
                               j == 0, j == 2 * g + 2)
                mm.then_inc(pv_mm, 1)

            def mean_squares(h, g):
                pe.wait_ge(o_squared, 4 * h + g + 1)
                pe.matmul(ps[:, 7, 0:2 * P], ones[:], o_sq, start=True, stop=True).then_inc(ms_mm, 1)

            PARTS = ((0, 3), (3, 6), (6, KT))

            def filler(h, p, last):
                k0, k1 = PARTS[p % 3]
                c = p // 3
                if c < 2:
                    chunk("Z", h, c, kq_out, 5 * h + 4 + c, k0, k1)
                elif c < 5 and not last:
                    chunk("V", h + 1, c - 2, vz_out, 5 * h + 4 + c - 2, k0, k1)

            pe.wait_ge(masks_made, 7)
            pe.wait_ge(v_zero, 2)

            def head(h, last):
                pe.wait_ge(keys_dup, 32 * h + 32)
                pe.wait_ge(kq_out, 5 * h + 5)
                for i in range(NT):
                    scores(h, i, 0)
                    filler(h, 2 * i, last)
                    if i >= 4 and i % 2 == 0:
                        mean_squares(h, (i - 4) // 2)
                    scores(h, i, 1)
                    filler(h, 2 * i + 1, last)
                    if i >= 3 and i % 2 == 1:
                        products(h, (i - 3) // 2)
                    if i >= 1:
                        attn_rounds(h, i - 1)
                if not last:
                    chunk("K", h + 1, 0, vz_out, 5 * (h + 1) + 2)
                attn_rounds(h, NT - 1)
                mean_squares(h, 2)
                if not last:
                    chunk("K", h + 1, 1, vz_out, 5 * (h + 1) + 3)
                    chunk("K", h + 1, 2, kq_out, 5 * (h + 1) + 1)
                products(h, 3)
                if not last:
                    v_rounds(h + 1, RP + RH * h + 14)
                    chunk("Q", h + 1, 0, kq_out, 5 * (h + 1) + 2)
                mean_squares(h, 3)
                if not last:
                    chunk("Q", h + 1, 1, kq_out, 5 * (h + 1) + 3)

            with pe.Fori(0, NH - 1) as h:
                head(h, False)
            head(NH - 1, True)

            pe.wait_ge(wb_hi, KT)
            pe.wait_ge(wb_lo, KT)
            pe.wait_ge(s_out, 2 * NT * NH)
            for t in range(2):
                out_tile(t, t, y4_hi, y4_lo, X_hi, X_lo, h2_done, None, out4_mm)
            with pe.Fori(1, NT // 2) as i:
                for s in range(2):
                    out_tile(2 * i + s, s, y4_hi, y4_lo, X_hi, X_lo, h2_done, 2 * i + s - 1, out4_mm)

        @block.vector
        def _(dve):
            N2 = NT + 1
            N4 = 2 * N2

            def unit_lo(u, slot):
                dve.wait_ge(w_hi, u + 1)
                nc.vector.tensor_tensor(ring[:, slot, 1], raw[slot], ring[:, slot, 0], ALU.subtract).then_inc(w_lo, 1)

            def inverse_root(n, slot):
                s = stat[:, slot]
                dve.wait_ge(r0_done, n + 1)
                nc.vector.tensor_scalar(s[:, 1:2], s[:, 0:1], 1.0 / D, EPS, ALU.mult, ALU.add).then_inc(newton, 1)
                dve.wait_ge(newton, 4 * n + 1)
                nc.vector.tensor_scalar(s[:, 4:5], s[:, 3:4], s[:, 3:4], s[:, 1:2], ALU.mult, ALU.mult).then_inc(newton, 1)
                dve.wait_ge(newton, 4 * n + 2)
                nc.vector.tensor_scalar(s[:, 5:6], s[:, 4:5], -0.5, 1.5, ALU.mult, ALU.add).then_inc(newton, 1)
                dve.wait_ge(newton, 4 * n + 3)
                nc.vector.tensor_tensor(s[:, 6:7], s[:, 3:4], s[:, 5:6], ALU.mult).then_inc(newton, 1)
                dve.wait_ge(newton, 4 * n + 4)
                return s[:, 6:7]

            def x_lo(n, slot, col, width):
                dve.wait_ge(xh_done, n + 1)
                nc.vector.tensor_tensor(X_lo[:, :, bass.ds(col, width)],
                                        flat(tr_bank(slot), D).rearrange("p (k n) -> p k n", k=KT)[:, :, 0:width],
                                        X_hi[:, :, bass.ds(col, width)], ALU.subtract).then_inc(xl_done, 1)

            for t in range(NT + 1):
                r = inverse_root(t, t % 2)
                nc.vector.tensor_scalar(x0[t % 2], x0[t % 2], r, None, ALU.mult).then_inc(xn_done, 1)
                if t >= 1:
                    x_lo(t - 1, (t - 1) % 2, key_col(t - 1), M if t == 1 else P)
            dve.wait_ge(const_in, 16 * 12)
            for j in range(2):
                nc.vector.tensor_tensor(lam_in[:, 2 * j], lam_in[:, 2 * j], lam_in[:, 2 * j + 1], ALU.mult).then_inc(lam_step, 1)
            for j in range(2):
                dve.wait_ge(lam_step, j + 1)
                nc.vector.tensor_reduce(lam_s[:, j:j + 1], lam_in[:, 2 * j], AX_X, ALU.add).then_inc(lam_step, 1)
            unit_lo(0, 0)
            x_lo(NT, NT % 2, key_col(NT), P)

            dve.wait_ge(gains_done, 1)
            nc.vector.tensor_scalar(g_sub[:, 1:2], gains[:, 7 * KT:7 * KT + 1], 1.0 - LAMBDA_INIT, None, ALU.mult).then_inc(lam_step, 1)
            dve.wait_ge(lam_exp, 1)
            nc.vector.tensor_scalar(lam_s[:, 7:8], lam_s[:, 2:3], lam_s[:, 3:4], LAMBDA_INIT, ALU.subtract,
                                    ALU.add).then_inc(lam_done, 1)

            cz3 = cz.rearrange("p (b n) -> p b n", b=3)
            conv3 = conv.rearrange("p (b n) -> p b n", b=3)
            nc.vector.memset(vpad[:, 0:2], 0.0).then_inc(vpad_zero, 1)

            def feature(f, last):
                unit_lo(4 * f + 1, 1)
                unit_lo(4 * f + 2, 0)
                dve.wait_ge(unit_mm, 4 * f + 2)
                dve.wait_ge(c_done, f + 1)
                nc.vector.tensor_tensor(vpad[:, 2:2 + LP].rearrange("p (b n) -> p b n", b=3), ps[:, 3:6, 0:CW], cz3,
                                        ALU.mult).then_inc(v_done, 1)
                dve.wait_ge(v_done, f + 1)
                nc.vector.tensor_scalar(conv, vpad[:, 0:LP], conv_w[:, 0, bass.ds(f, 1)], conv_b[:, bass.ds(f, 1)],
                                        ALU.mult, ALU.add).then_inc(conv_step, 1)
                for j in (1, 2):
                    dve.wait_ge(conv_step, 3 * f + j)
                    nc.vector.scalar_tensor_tensor(out=conv, in0=vpad[:, j:j + LP], scalar=conv_w[:, j, bass.ds(f, 1)],
                                                   in1=conv, op0=ALU.mult, op1=ALU.add).then_inc(conv_step, 1)
                unit_lo(4 * f + 3, 1)
                dve.wait_ge(unit_mm, 4 * f + 3)
                dve.wait_ge(conv_step, 3 * f + 3)
                nc.vector.tensor_tensor(conv3, ps[:, 0:3, 0:CW], conv3, ALU.mult).then_inc(b_done, 1)
                dve.wait_ge(o_hi, f + 1)
                nc.vector.tensor_tensor(wo_lo[:, :, bass.ds(f * P, P)], raw_o, wo_hi[:, :, bass.ds(f * P, P)],
                                        ALU.subtract).then_inc(o_lo, 1)
                if not last:
                    unit_lo(4 * f + 4, 0)
                dve.wait_ge(z_done, f + 1)
                dve.wait_ge(b_done, f + 1)
                nc.vector.tensor_tensor(Y[:, bass.ds(f, 1), :], conv.rearrange("p (a n) -> p a n", a=1),
                                        cz.rearrange("p (a n) -> p a n", a=1), ALU.mult).then_inc(y_done, 1)

            dve.wait_ge(vpad_zero, 1)
            with dve.Fori(0, KT - 1) as f:
                feature(f, False)
            feature(KT - 1, True)

            def y_tile_lo(t, slot, col):
                dve.wait_ge(y_hi, t + 1)
                dve.wait_ge(y_done, KT)
                nc.vector.tensor_tensor(ring[:, slot, 1], Y[:, :, bass.ds(col, P)], ring[:, slot, 0],
                                        ALU.subtract).then_inc(y_lo, 1)

            def h1_tile(t, slot, x_count, reused=True):
                dve.wait_ge(out_mm, t + 1)
                dve.wait_ge(x_in[slot], x_count)
                if reused:
                    dve.wait_ge(h1_stored[slot], stored_before(t, slot))
                nc.vector.tensor_tensor(ht[slot], flat(2 * slot, D), xt[slot], ALU.add).then_inc(h1_done, 1)

            def stored_before(t, slot):
                return 8 * (t - 2) if slot == 0 else 8 * (t - 1)

            def x2_count(t, slot):
                return 16 * 6 + 32 + 8 * t if slot == 0 else 16 * 4 + 8 * (t + 1)

            def step2(t, par, nxt=True, prev=True, prev2=True, first=False, meta2=False):
                if prev:
                    h1_tile(t - 1, 1 - par, x2_count(t - 1, 1 - par), reused=not first)
                if nxt:
                    y_tile_lo(t + 1, 1 - par, M + t * P)
                if prev2:
                    x_lo(N2 + t - 2, par, 0 if meta2 else M + (t - 3) * P, M if meta2 else P)
                if prev:
                    r = inverse_root(N2 + t - 1, 1 - par)
                    nc.vector.tensor_scalar(xt[1 - par], ht[1 - par], r, None, ALU.mult).then_inc(xn_done, 1)

            y_tile_lo(0, 0, 0)
            y_tile_lo(1, 1, M)
            step2(1, 1, prev2=False, first=True)
            step2(2, 0, first=True, meta2=True)
            with dve.Fori(0, (NT - 4) // 2) as i:
                step2(2 * i + 3, 1)
                step2(2 * i + 4, 0)
            step2(NT - 1, 1)
            unit_lo(U1, SLOT["V"])
            step2(NT, 0, nxt=False)
            step2(NT + 1, 1, nxt=False)
            unit_lo(U1 + 1, SLOT["K"])
            x_lo(N2 + NT, 0, M + (NT - 1) * P, P)

            def k_chunk_lo(h, c):
                dve.wait_ge(chunk_hi, 5 * h + c + 1)
                b = ps[:, chunk_bank("K", c), 0:CW]
                for q, rows in enumerate((slice(0, HD), slice(HD, P))):
                    ins = nc.vector.tensor_tensor(keys[q][rows, 1, CW * c:CW * (c + 1)], b[rows],
                                                  keys[q][rows, 0, CW * c:CW * (c + 1)], ALU.subtract)
                ins.then_inc(kq_out, 1)

            def q_chunk_lo(h, c):
                dve.wait_ge(chunk_hi, 5 * h + 3 + c + 1)
                b = ps[:, chunk_bank("Q", c), :]
                cols = slice(QW * c, QW * (c + 1))
                nc.vector.tensor_tensor(queries[0][HD:P, cols], b[0:HD], queries[0][0:HD, cols], ALU.subtract)
                nc.vector.tensor_tensor(queries[1][0:HD, cols], b[HD:P], queries[1][HD:P, cols],
                                        ALU.subtract).then_inc(kq_out, 1)

            def round_lo_v(n, par, tiles):
                dve.wait_ge(round_hi, n + 1)
                b = ps[:, round_bank(par), 0:P * len(tiles)]
                if tiles == [0]:
                    nc.vector.tensor_tensor(V[0:M, 1, 0, :], b[0:M], V[0:M, 0, 0, :], ALU.subtract).then_inc(round_lo, 1)
                else:
                    js = slice(tiles[0], tiles[-1] + 1)
                    nc.vector.tensor_tensor(V[:, 1, js, :], b.rearrange("p (j v) -> p j v", v=P), V[:, 0, js, :],
                                            ALU.subtract).then_inc(round_lo, 1)

            def attn_rounds(h, i):
                for r, tiles in enumerate(rounds_of(i)):
                    n = ROUND_AT[i] + r
                    dve.wait_ge(round_hi, RP + RH * h + n + 1)
                    b = ps[:, round_bank(n), 0:P * len(tiles)].rearrange("p (j q) -> p j q", q=P)
                    qs = slice(P * (i % 2), P * (i % 2) + P)
                    full = [j for j in tiles if j]
                    if full:
                        js = slice(full[0], full[-1] + 1)
                        ins = nc.vector.tensor_tensor(attn_t[:, 1, js, qs], b[:, 0:len(full)], attn_t[:, 0, js, qs],
                                                      ALU.subtract)
                    if 0 in tiles:
                        ins = nc.vector.tensor_tensor(attn_t[:, 1, 0:1, qs], b[:, len(full):len(full) + 1],
                                                      attn_t[:, 0, 0:1, qs], ALU.subtract)
                    ins.then_inc(round_lo, 1)

            def scores_out(h, i, c):
                n = 2 * (NT * h + i) + c
                dve.wait_ge(s_mm, n + 1)
                nb, w = s_shape(i)
                e = E[i % 2][c][:, 0:nb * w].rearrange("p (b n) -> p b n", b=nb)
                nc.vector.tensor_scalar(e, ps[:, 0:nb, 0:w], -SCALE, None, ALU.mult, ALU.min,
                                        accum_out=neg_max[:, i % 2, c:c + 1]).then_inc(s_out, 1)

            def inverse_sums(h, i):
                dve.wait_ge(exp_done, 2 * (NT * h + i) + 2)
                nc.vector.reciprocal(z_inv[:, i % 2, 0:2], z_sum[:, i % 2, :]).then_inc(recip_done, 1)
                dve.wait_ge(recip_done, NT * h + i + 1)
                nc.vector.tensor_tensor(z_inv[:, i % 2, 2:3], z_inv[:, i % 2, 1:2], lam_s[:, 7:8],
                                        ALU.mult).then_inc(inv_done, 1)

            def combine(h, i):
                dve.wait_ge(e1_scaled, NT * h + i + 1)
                nb, w = s_shape(i)
                nc.vector.scalar_tensor_tensor(out=E[i % 2][0][:, 0:nb * w], in0=E[i % 2][0][:, 0:nb * w],
                                               scalar=z_inv[:, i % 2, 0:1], in1=E[i % 2][1][:, 0:nb * w],
                                               op0=ALU.mult, op1=ALU.subtract).then_inc(attn_done, 1)

            def y_out(h):
                dve.wait_ge(or_done, h + 1)
                dve.wait_ge(vz_out, 5 * h + 5)
                dve.wait_ge(y_stored, 16 * h)
                nc.vector.scalar_tensor_tensor(out=y_o, in0=o_t, scalar=g_sub[:, 1:2], in1=z_act, op0=ALU.mult,
                                               op1=ALU.mult).then_inc(y_head, 1)

            def wb_unit_lo(j):
                dve.wait_ge(wb_hi, j + 1)
                nc.vector.tensor_tensor(X_lo[:, :, j * P:(j + 1) * P], raw[j % 2], X_hi[:, :, j * P:(j + 1) * P],
                                        ALU.subtract).then_inc(wb_lo, 1)

            dve.wait_ge(lam_done, 1)
            dve.wait_ge(out_mm, NT + 1)
            for part in range(2):
                nc.vector.memset(V[:, part, 0, :].bitcast(F32), 0.0).then_inc(v_zero, 1)
            for c in range(3):
                k_chunk_lo(0, c)
                if c == 0:
                    unit_lo(U1 + 2, SLOT["Q"])
            for r, tiles in enumerate(V_ROUNDS):
                round_lo_v(r, r, tiles)
            unit_lo(U1 + 3, SLOT["Z"])
            for c in range(2):
                q_chunk_lo(0, c)

            def head(h, last):
                u = U1 + 4 + UH * h
                for i in range(NT):
                    if not last and i == 1:
                        unit_lo(u, SLOT["V"])
                    if not last and i == 4:
                        unit_lo(u + 1, SLOT["K"])
                    scores_out(h, i, 0)
                    if i >= 1:
                        inverse_sums(h, i - 1)
                    scores_out(h, i, 1)
                    if i >= 1:
                        combine(h, i - 1)
                        attn_rounds(h, i - 1)
                    if last and i >= 4:
                        wb_unit_lo(2 * i - 8)
                        wb_unit_lo(2 * i - 7)
                inverse_sums(h, NT - 1)
                combine(h, NT - 1)
                if not last:
                    unit_lo(u + 2, SLOT["Q"])
                    k_chunk_lo(h + 1, 0)
                attn_rounds(h, NT - 1)
                if not last:
                    k_chunk_lo(h + 1, 1)
                    k_chunk_lo(h + 1, 2)
                    for r, tiles in enumerate(V_ROUNDS):
                        round_lo_v(RP + RH * h + 14 + r, 14 + r, tiles)
                    unit_lo(u + 3, SLOT["Z"])
                    q_chunk_lo(h + 1, 0)
                    q_chunk_lo(h + 1, 1)
                y_out(h)

            with dve.Fori(0, NH - 1) as h:
                head(h, False)
            head(NH - 1, True)

            def y4_lo_tile(t, slot):
                dve.wait_ge(y4_hi, t + 1)
                nc.vector.tensor_tensor(ring[:, slot, 1], y4[slot], ring[:, slot, 0], ALU.subtract).then_inc(y4_lo, 1)

            y4_lo_tile(0, 0)
            dve.wait_ge(gf_in, 16)
            for t in range(NT):
                s = t % 2
                if t + 1 < NT:
                    y4_lo_tile(t + 1, 1 - s)
                dve.wait_ge(out4_mm, t + 1)
                dve.wait_ge(h4_in[s], 16 * (t // 2 + 1))
                nc.vector.tensor_tensor(h4[s], flat(2 * s, D), h4[s], ALU.add).then_inc(h2_done, 1)
                r = inverse_root(N4 + t, s)
                if t >= 2:
                    dve.wait_ge(o4_stored[s], 16 * (t // 2))
                nc.vector.scalar_tensor_tensor(out=o4[s], in0=h4[s], scalar=r, in1=g_final, op0=ALU.mult,
                                               op1=ALU.mult).then_inc(o4_done, 1)


_INS = ['x', 'meta_tokens', 'a_norm_g', 'a_w_in', 'a_conv_w', 'a_conv_b', 'a_w_out', 'kv_norm_g', 'w_kv', 'b_norm_g',
        'b_w_in', 'b_lambda_q1', 'b_lambda_k1', 'b_lambda_q2', 'b_lambda_k2', 'b_subln_g', 'b_w_out', 'final_norm_g']


def kernel(**inputs):
    import numpy as _np
    import concourse.bacc as _bacc
    from concourse import mybir as _mybir
    from concourse.bass_utils import run_bass_kernel_spmd as _run

    nc = _bacc.Bacc("TRN2", target_bir_lowering=False, num_devices=1)
    arrays, args = {}, []
    for name in _INS:
        a = _np.ascontiguousarray(inputs[name])
        arrays[f"in_{name}_dram"] = a
        args.append(nc.dram_tensor(f"in_{name}_dram", a.shape, _mybir.dt.from_np(a.dtype), kind="ExternalInput").ap())
    args.append(nc.dram_tensor("out_0_dram", inputs["x"].shape, _mybir.dt.float32, kind="ExternalOutput").ap())
    yoco_kernel(nc, *args)
    r = _run(nc, [arrays], core_ids=[0])
    return r.results[0]["out_0_dram"]
```

```python
import math
from contextlib import ExitStack

import concourse.bass as bass
from concourse import mybir

P = 128
EPS = 1e-6
LAMBDA_INIT = 0.8 - 0.6 * math.exp(-0.3 * 1)

ALU = mybir.AluOpType
ACT = mybir.ActivationFunctionType
F32 = mybir.dt.float32
F32R = mybir.dt.float32r
BF16 = mybir.dt.bfloat16
AX_X = mybir.AxisListType.X
MASKED = -1.0e30


def yoco_kernel(nc, x, meta_tokens, a_norm_g, a_w_in, a_conv_w, a_conv_b, a_w_out, kv_norm_g, w_kv,
                b_norm_g, b_w_in, b_lambda_q1, b_lambda_k1, b_lambda_q2, b_lambda_k2, b_subln_g,
                b_w_out, final_norm_g, out):
    _, T, D = x.shape
    M = meta_tokens.shape[0]
    L = T + M
    KT = D // P
    NT = T // P
    CW = 348
    LP = 3 * CW
    NH = KT
    HD = P // 2
    QW = 512
    SCALE = HD ** -0.5
    assert L <= LP and T == 2 * QW and NH * P == D and a_conv_w.shape[1] == 3

    x_rows = x[0]
    out_rows = out[0]
    w_in_a = a_w_in[0].rearrange("(k p) n -> p k n", p=P)
    w_out_a = a_w_out[0].rearrange("(k p) n -> p k n", p=P)
    w_kv_v = w_kv.rearrange("(k p) n -> p k n", p=P)
    w_in_b = b_w_in[0].rearrange("(k p) n -> p k n", p=P)
    w_out_b = b_w_out[0].rearrange("(k p) n -> p k n", p=P)
    h1_dram = nc.dram_tensor("h1_scratch", [T, D], F32, kind="Internal").ap()
    y_dram = nc.dram_tensor("y_scratch", [P, NH, T], F32, kind="Internal").ap()

    with ExitStack() as ctx:
        def sb(name, shape, dt):
            return ctx.enter_context(nc.sbuf_tensor(name, shape, dt))

        def sem(name):
            return ctx.enter_context(nc.semaphore(name))

        X_hi = sb("X_hi", [P, KT, LP], F32R)
        X_lo = sb("X_lo", [P, KT, LP], F32R)
        ring = sb("ring", [P, 2, 2, KT, P], F32R)
        BIGW = 2 * KT * D
        big = sb("big", [P, BIGW], F32R)
        wo_hi = big[:, 0:KT * D].rearrange("p (k n) -> p k n", k=KT)
        wo_lo = big[:, KT * D:2 * KT * D].rearrange("p (k n) -> p k n", k=KT)
        keys = [big[:, 2 * LP * c:2 * LP * (c + 1)].rearrange("p (s n) -> p s n", s=2) for c in range(2)]
        at = 4 * LP
        queries = [big[:, at + T * c:at + T * (c + 1)] for c in range(2)]
        at += 2 * T
        NK = NT + 1
        V = big[:, at:at + 2 * NK * P].rearrange("p (s j v) -> p s j v", s=2, j=NK)
        at += 2 * NK * P
        attn_t = big[:, at:at + 2 * NK * 2 * P].rearrange("p (s j q) -> p s j q", s=2, j=NK)
        assert at + 4 * NK * P <= BIGW

        WORK = KT * LP + 2 * D + D + 3 * LP + 16
        work = sb("work", [P, WORK], F32)
        raw_at = KT * LP
        misc_at = raw_at + 2 * D
        raw = [work[:, raw_at + D * s:raw_at + D * (s + 1)].rearrange("p (k n) -> p k n", k=KT) for s in range(2)]
        X0S = 6
        x0 = [work[:, D * s:D * (s + 1)] for s in range(X0S)]
        squares0 = work[:, D * X0S:D * (X0S + 1)]
        Y = work[:, 0:KT * LP].rearrange("p (k n) -> p k n", k=KT)
        raw_o = work[:, misc_at:misc_at + D].rearrange("p (k n) -> p k n", k=KT)
        cz = work[:, misc_at + D:misc_at + D + LP]
        vpad = work[:, misc_at + D + LP:misc_at + D + 2 * LP + 2]
        conv = work[:, misc_at + D + 2 * LP + 2:misc_at + D + 3 * LP + 2]
        xt = [work[:, misc_at + D * s:misc_at + D * (s + 1)] for s in range(2)]
        ht = [work[:, misc_at + D * (2 + s):misc_at + D * (3 + s)] for s in range(2)]
        E = [[work[:, LP * (2 * s + c):LP * (2 * s + c + 1)] for c in range(2)] for s in range(2)]
        v_t = work[:, 4 * LP:5 * LP]
        z_act = work[:, 5 * LP:5 * LP + T]
        o_t = work[:, 6 * LP:6 * LP + T]
        r_o = work[:, 7 * LP:7 * LP + T]
        y_o = work[:, misc_at:misc_at + T]
        o_sq = work[:, misc_at + T:misc_at + T + 2 * P]
        y4 = [work[:, D * s:D * (s + 1)].rearrange("p (k n) -> p k n", k=NH) for s in range(2)]
        h4 = [work[:, D * (2 + s):D * (3 + s)] for s in range(2)]
        o4 = [work[:, D * (4 + s):D * (5 + s)] for s in range(2)]
        g_final = work[:, 7 * D:8 * D]

        ident = sb("ident", [P, P], F32)
        ones = sb("ones", [P, P], F32)
        mask_q = sb("mask_q", [P, P], BF16)
        mask_k = sb("mask_k", [P, HD + LP - L], BF16)
        gain_rows = work[:, misc_at + D:misc_at + D + P]
        gains = sb("gains", [P, 8 * KT], F32)
        g_a = gains[:, 0:KT]
        g_kv = gains[:, KT:2 * KT]
        g_b = gains[:, 2 * KT:3 * KT]
        conv_b = gains[:, 3 * KT:4 * KT]
        conv_w = gains[:, 4 * KT:7 * KT].rearrange("p (j k) -> p j k", j=3)
        g_sub = sb("g_sub", [P, 2], F32)
        lam_in = sb("lam_in", [P, 4, HD], F32)
        lam_s = sb("lam_s", [P, 8], F32)
        eps = sb("eps", [P, 1], F32)
        stat = sb("stat", [P, 2, 8], F32)
        neg_max = sb("neg_max", [P, 2, 2], F32)
        z_sum = sb("z_sum", [P, 2, 2], F32)
        z_inv = sb("z_inv", [P, 2, 3], F32)
        ps = ctx.enter_context(nc.psum_tensor("ps", [P, 8, 512], F32))

        def flat(bank, width):
            return ps[:].rearrange("p b n -> p (b n)")[:, bank * 512:bank * 512 + width]

        const_in = sem("const_in")
        rows_zero = sem("rows_zero")
        gains_mm = sem("gains_mm")
        gains_done = sem("gains_done")
        ident_made = sem("ident_made")
        masks_made = sem("masks_made")
        pads_zero = sem("pads_zero")
        lam_step = sem("lam_step")
        lam_exp = sem("lam_exp")
        lam_done = sem("lam_done")
        x0_in = [sem(f"x0_in{s}") for s in range(X0S)]
        x_in = [sem(f"x_in{s}") for s in range(2)]
        sq_done = sem("sq_done")
        ln_done = sem("ln_done")
        r0_done = sem("r0_done")
        newton = sem("newton")
        xn_done = sem("xn_done")
        tr_done = sem("tr_done")
        xh_done = sem("xh_done")
        xl_done = sem("xl_done")
        raw_in = [sem(f"raw_in{s}") for s in range(2)]
        w_scaled = sem("w_scaled")
        w_hi = sem("w_hi")
        w_lo = sem("w_lo")
        c_done = sem("c_done")
        v_done = sem("v_done")
        conv_step = sem("conv_step")
        b_done = sem("b_done")
        z_done = sem("z_done")
        y_done = sem("y_done")
        o_in = sem("o_in")
        o_hi = sem("o_hi")
        o_lo = sem("o_lo")
        y0_hi = sem("y0_hi")
        y0_lo = sem("y0_lo")
        y_hi = sem("y_hi")
        y_lo = sem("y_lo")
        out_mm = sem("out_mm")
        h1_done = sem("h1_done")
        vpad_zero = sem("vpad_zero")
        v_zero = sem("v_zero")
        h1_stored = [sem(f"h1_stored{s}") for s in range(2)]
        unit_mm = sem("unit_mm")
        chunk_mm = sem("chunk_mm")
        chunk_hi = sem("chunk_hi")
        kq_out = sem("kq_out")
        vz_out = sem("vz_out")
        z_silu = sem("z_silu")
        keys_dup = sem("keys_dup")
        s_mm = sem("s_mm")
        s_out = sem("s_out")
        exp_done = sem("exp_done")
        recip_done = sem("recip_done")
        inv_done = sem("inv_done")
        e1_scaled = sem("e1_scaled")
        attn_done = sem("attn_done")
        round_mm = sem("round_mm")
        round_hi = sem("round_hi")
        round_lo = sem("round_lo")
        pv_mm = sem("pv_mm")
        o_copied = sem("o_copied")
        o_squared = sem("o_squared")
        ms_mm = sem("ms_mm")
        ms_ln = sem("ms_ln")
        r_done = sem("r_done")
        or_done = sem("or_done")
        y_head = sem("y_head")
        y_stored = sem("y_stored")
        wb_in = [sem(f"wb_in{s}") for s in range(2)]
        wb_hi = sem("wb_hi")
        wb_lo = sem("wb_lo")
        y4_in = [sem(f"y4_in{s}") for s in range(2)]
        h4_in = [sem(f"h4_in{s}") for s in range(2)]
        gf_in = sem("gf_in")
        y4_hi = sem("y4_hi")
        y4_lo = sem("y4_lo")
        out4_mm = sem("out4_mm")
        h2_done = sem("h2_done")
        o4_done = sem("o4_done")
        o4_stored = [sem(f"o4_stored{s}") for s in range(2)]

        NCONST = 14
        U1 = 4 * KT
        UH = 4
        CHUNKS = 10
        CHUNK_OF = {"V": 0, "K": 3, "Q": 6, "Z": 8}
        RH = 18
        RP = 4
        SLOT = {"V": 1, "K": 0, "Q": 1, "Z": 0}

        def rounds_of(i):
            tiles = list(range(1, i + 2)) + [0]
            return [tiles[a:a + 4] for a in range(0, len(tiles), 4)]

        ROUND_AT = [sum(len(rounds_of(a)) for a in range(i)) for i in range(NT)]
        V_ROUNDS = [[1, 2, 3], [4, 5, 6], [7, 8], [0]]
        assert ROUND_AT[-1] + len(rounds_of(NT - 1)) + len(V_ROUNDS) == RH

        def round_bank(n):
            return 5 + n % 2

        def chunk_bank(kind, c):
            return 4 if kind == "V" else 3 + c % 2

        def s_bank(i, c):
            return 2 * c if s_shape(i)[0] <= 2 else 0

        def s_read(h, i, c):
            n = 2 * (NT * h + i) + c
            shares = s_shape(i)[0] == 3 or (c == 0 and s_shape((i - 1) % NT)[0] == 3)
            return n + 1 if shares or (i, c) == (0, 0) else n

        def tr_bank(slot):
            return 6 - 2 * slot

        def s_shape(i):
            n = M + P * (i + 1)
            if n <= 512:
                return 1, n
            if n <= 1024:
                return 2, n // 2
            return 3, CW

        FILL_AT = [1, 2, 3, 4, 5, None, 6, 7, 8, 9, 10, 11, 12, 13, 14, None]
        WB_AT = [(), (), (), (0, 1), (2, 3), (4,), (5, 6), (7,)]

        def key_col(j):
            return 0 if j == 0 else M + P * (j - 1)

        block = ctx.enter_context(nc.Block())

        @block.sync
        def _(sp):
            def load_x(t, slot, dst, sems):
                if t is None:
                    sp.dma_start(dst[slot][0:M, :], meta_tokens).then_inc(sems[slot], 16)
                    sp.dma_start(dst[slot][M:P, :], x_rows[0:P - M, :]).then_inc(sems[slot], 16)
                else:
                    sp.dma_start(dst[slot], x_rows[bass.ds(t * P, P), :]).then_inc(sems[slot], 16)

            load_x(None, 0, x0, x0_in)
            load_x(0, 1, x0, x0_in)
            for r, v in enumerate((a_norm_g[0], kv_norm_g, b_norm_g[0], a_conv_b[0], a_conv_w[0, 0], a_conv_w[0, 1],
                                   a_conv_w[0, 2])):
                sp.dma_start(gain_rows[KT * r:KT * (r + 1), :], v.rearrange("(k p) -> k p", p=P)).then_inc(const_in, 16)
            sp.dma_start(gain_rows[7 * KT:8 * KT, :], b_subln_g[0:1, :].to_broadcast([KT, P])).then_inc(const_in, 16)
            for j, v in enumerate((b_lambda_q1, b_lambda_k1, b_lambda_q2, b_lambda_k2)):
                sp.dma_start(lam_in[:, j, :], v[0:1, :].to_broadcast([P, HD])).then_inc(const_in, 16)

            def load_unit(u, slot, w, col):
                sp.wait_ge(w_hi, u - 1)
                sp.wait_ge(w_lo, u - 1)
                sp.dma_start(raw[slot], w[:, :, bass.ds(col, P)]).then_inc(raw_in[slot], 16)

            ORDER = (1, 2, 0, 3)
            for t in range(2, NT + 1):
                if t == 3:
                    for n in range(2):
                        sp.dma_start(raw[n], w_in_a[:, :, ORDER[n] * D:ORDER[n] * D + P]).then_inc(raw_in[n], 16)
                if t >= X0S:
                    sp.wait_ge(tr_done, t - X0S + 1)
                load_x(t - 1, t % X0S, x0, x0_in)
            sp.dma_start(raw_o, w_out_a[:, :, 0:P]).then_inc(o_in, 16)
            for n in (2, 3):
                load_unit(n, n % 2, w_in_a, ORDER[n] * D)
            with sp.Fori(1, KT) as f:
                sp.wait_ge(o_hi, f)
                sp.wait_ge(o_lo, f)
                sp.dma_start(raw_o, w_out_a[:, :, bass.ds(f * P, P)]).then_inc(o_in, 16)
                for n in range(4):
                    load_unit(4 * f + n, n % 2, w_in_a, f * P + ORDER[n] * D)

            sp.wait_ge(o_hi, KT)
            sp.wait_ge(o_lo, KT)
            sp.wait_ge(y_done, KT)
            load_x(None, 0, xt, x_in)
            load_x(0, 1, xt, x_in)
            def load_head_unit(u, kind, h, ahead=0):
                slot = SLOT[kind]
                w, col = {"V": (w_kv_v, D), "K": (w_kv_v, 0), "Q": (w_in_b, 0), "Z": (w_in_b, D)}[kind]
                load_unit(u, slot, w, h * P + (col + ahead * P))

            sp.wait_ge(w_hi, U1)
            sp.wait_ge(w_lo, U1)
            load_head_unit(U1, "V", 0)
            sp.dma_start(raw[SLOT["K"]], w_kv_v[:, :, 0:P]).then_inc(raw_in[SLOT["K"]], 16)

            def store_h1(t, slot, stored=None):
                sp.wait_ge(h1_done, t + 1)
                sp.dma_start(h1_dram[bass.ds((t - 1) * P, P), :],
                             ht[slot]).then_inc(h1_stored[slot] if stored is None else stored, 16)

            def step2(t, slot):
                sp.wait_ge(tr_done, NT + 1 + t)
                load_x(t, 1 - slot, xt, x_in)
                store_h1(t, slot)

            with sp.Fori(0, (NT - 2) // 2) as i:
                step2(2 * i + 1, 1)
                step2(2 * i + 2, 0)
            step2(NT - 1, 1)
            store_h1(NT, 0, y_stored)

            def dup_keys(h):
                sp.wait_ge(kq_out, 5 * h + 3)
                sp.dma_start(keys[0][HD:P].bitcast(F32), keys[0][0:HD].bitcast(F32)).then_inc(keys_dup, 16)
                sp.dma_start(keys[1][0:HD].bitcast(F32), keys[1][HD:P].bitcast(F32)).then_inc(keys_dup, 16)

            load_head_unit(U1 + 2, "Q", 0)
            load_head_unit(U1 + 3, "Z", 0)

            def store_y(h):
                sp.wait_ge(y_head, h + 2)
                sp.dma_start(y_dram[:, bass.ds(h, 1), :], y_o.rearrange("p (a n) -> p a n", a=1)).then_inc(y_stored, 16)

            def head(h, ahead):
                u = U1 + 4 + UH * h
                load_head_unit(u + 2, "Q", h + 1)
                load_head_unit(u + 3, "Z", h + 1)
                if ahead:
                    load_head_unit(u + 4, "V", h + 1, 1)
                dup_keys(h + 1)
                store_y(h)
                if ahead:
                    load_head_unit(u + 5, "K", h + 1, 1)

            load_head_unit(U1 + 4, "V", 1)
            dup_keys(0)
            load_head_unit(U1 + 5, "K", 1)
            with sp.Fori(0, NH - 2) as h:
                head(h, True)
            head(NH - 2, False)
            UL = U1 + 4 + UH * (NH - 1)
            sp.wait_ge(w_hi, UL)
            sp.wait_ge(w_lo, UL)
            for j in range(KT):
                if j >= 2:
                    sp.wait_ge(wb_hi, j - 1)
                    sp.wait_ge(wb_lo, j - 1)
                sp.dma_start(raw[j % 2], w_out_b[:, :, j * P:(j + 1) * P]).then_inc(wb_in[j % 2], 16)
            store_y(NH - 1)

            sp.dma_start(g_final, final_norm_g.rearrange("(a n) -> a n", a=1).to_broadcast([P, D])).then_inc(gf_in, 16)
            for s in range(2):
                sp.wait_ge(h1_stored[s], 16 * (NT // 2 - 1 + s))
            sp.wait_ge(y_stored, 16 * (NH + 1))

            def load4(t, slot):
                sp.dma_start(y4[slot], y_dram[:, :, bass.ds(t * P, P)]).then_inc(y4_in[slot], 16)
                sp.dma_start(h4[slot], h1_dram[bass.ds(t * P, P), :]).then_inc(h4_in[slot], 16)

            def store4(t, slot):
                sp.wait_ge(o4_done, t + 1)
                sp.dma_start(out_rows[bass.ds(t * P, P), :], o4[slot]).then_inc(o4_stored[slot], 16)

            load4(0, 0)
            load4(1, 1)
            with sp.Fori(0, NT // 2 - 1) as i:
                for s in range(2):
                    t = 2 * i + s
                    store4(t, s)
                    sp.wait_ge(y4_lo, t + 1)
                    load4(t + 2, s)
            for s in range(2):
                store4(NT - 2 + s, s)
            for s in range(2):
                sp.wait_ge(o4_stored[s], 16 * (NT // 2))

        @block.gpsimd
        def _(pool):
            nc.gpsimd.memset(ident[:], 0.0).then_inc(ident_made, 1)
            nc.gpsimd.memset(ones[:], 1.0).then_inc(ident_made, 1)
            nc.gpsimd.memset(eps[:], EPS).then_inc(ident_made, 1)
            pool.wait_ge(ident_made, 3)
            nc.gpsimd.affine_select(out=ident[:], in_=ident[:], compare_op=ALU.not_equal, fill=1.0, base=0,
                                    pattern=[[-1, P]], channel_multiplier=1).then_inc(ident_made, 1)
            pool.wait_ge(ident_made, 4)
            nc.gpsimd.memset(gain_rows[8 * KT:P, :], 0.0).then_inc(rows_zero, 1)
            pool.wait_ge(rows_zero, 1)
            nc.gpsimd.memset(X_hi[:, :, L:LP].bitcast(F32), 0.0).then_inc(pads_zero, 1)
            nc.gpsimd.memset(X_lo[:, :, L:LP].bitcast(F32), 0.0).then_inc(pads_zero, 1)
            nc.gpsimd.memset(mask_q[:], 0.0).then_inc(masks_made, 1)
            nc.gpsimd.memset(mask_k[:], 0.0).then_inc(masks_made, 1)
            pool.wait_ge(masks_made, 2)
            for n, (rows, value) in enumerate((
                    (mask_q[0:2, :], 1.0), (mask_k[0:2, HD:], MASKED), (mask_q[0:1, HD:P], 0.0),
                    (mask_k[0:1, 0:HD], MASKED), (mask_k[0:1, HD:], 0.0))):
                nc.gpsimd.memset(rows, value).then_inc(masks_made, 1)
                pool.wait_ge(masks_made, n + 3)

            def scale_unit(u, slot, count, g):
                pool.wait_ge(raw_in[slot], count)
                nc.gpsimd.tensor_tensor(raw[slot], raw[slot], g.unsqueeze(2).to_broadcast([P, KT, P]),
                                        ALU.mult).then_inc(w_scaled, 1)

            pool.wait_ge(gains_done, 1)
            with pool.Fori(0, KT) as f:
                for n in range(4):
                    scale_unit(4 * f + n, n % 2, 32 * f + 16 * (n // 2 + 1), g_a)
            R1 = 16 * (U1 // 2)
            scale_unit(U1, 1, R1 + 16, g_kv)
            scale_unit(U1 + 1, 0, R1 + 16, g_kv)
            scale_unit(U1 + 2, 1, R1 + 32, g_b)
            scale_unit(U1 + 3, 0, R1 + 32, g_b)

            def scale_e1(h, i):
                pool.wait_ge(inv_done, NT * h + i + 1)
                nb, w = s_shape(i)
                e1 = E[i % 2][1][:, 0:nb * w]
                nc.gpsimd.tensor_tensor(e1, e1, z_inv[:, i % 2, 2:3].to_broadcast([P, nb * w]),
                                        ALU.mult).then_inc(e1_scaled, 1)

            def head(h, last):
                for i in range(NT):
                    if not last:
                        u = U1 + 4 + UH * h
                        at = R1 + 32 + 32 * h
                        if i == 0:
                            scale_unit(u, 1, at + 16, g_kv)
                        if i == 2:
                            scale_unit(u + 1, 0, at + 16, g_kv)
                        if i == 5:
                            scale_unit(u + 2, 1, at + 32, g_b)
                        if i == 7:
                            scale_unit(u + 3, 0, at + 32, g_b)
                    scale_e1(h, i)
                pool.wait_ge(r_done, h + 1)
                nc.gpsimd.tensor_tensor(o_t, o_t, r_o, ALU.mult).then_inc(or_done, 1)

            with pool.Fori(0, NH - 1) as h:
                head(h, False)
            head(NH - 1, True)

        @block.scalar
        def _(act):
            def unit_hi(u, slot, sem_used, used):
                act.wait_ge(w_scaled, u + 1)
                if used is not None:
                    act.wait_ge(sem_used, used)
                nc.scalar.activation(ring[:, slot, 0], raw[slot], ACT.Copy).then_inc(w_hi, 1)

            def stats(n, slot, src, squares=None):
                s = stat[:, slot]
                nc.scalar.activation(flat(tr_bank(slot), D) if squares is None else squares, src, ACT.Square,
                                     accum_out=s[:, 0:1]).then_inc(sq_done, 1)
                act.wait_ge(sq_done, n + 1)
                nc.scalar.activation(s[:, 2:3], s[:, 0:1], ACT.Ln, bias=eps[:], scale=1.0 / D).then_inc(ln_done, 1)
                act.wait_ge(ln_done, n + 1)
                nc.scalar.activation(s[:, 3:4], s[:, 2:3], ACT.Exp, scale=-0.5).then_inc(r0_done, 1)

            def x_hi(n, slot, col, width):
                act.wait_ge(tr_done, n + 1)
                nc.scalar.activation(X_hi[:, :, bass.ds(col, width)],
                                     flat(tr_bank(slot), D).rearrange("p (k n) -> p k n", k=KT)[:, :, 0:width],
                                     ACT.Copy).then_inc(xh_done, 1)

            nc.scalar.preload_act_table_set("natural_log_exp_and_others")
            act.wait_ge(ident_made, 3)
            for t in range(NT + 1):
                act.wait_ge(x0_in[t % X0S], 32 + 16 * (t // X0S) if t % X0S == 0 else 16 * (t // X0S + 1))
                if t >= 2:
                    act.wait_ge(xn_done, t - 1)
                stats(t, t % 2, x0[t % X0S], squares0)
                if t >= 2:
                    x_hi(t - 2, t % 2, key_col(t - 2), M if t == 2 else P)
                if t == 3:
                    act.wait_ge(gains_mm, 1)
                    nc.scalar.activation(gains[:], ps[:, 3, 0:8 * KT], ACT.Copy).then_inc(gains_done, 1)
                if t == 5:
                    unit_hi(0, 0, None, None)
                if t == 7:
                    unit_hi(1, 1, None, None)
            act.wait_ge(lam_step, 4)
            nc.scalar.activation(lam_s[:, 2:4], lam_s[:, 0:2], ACT.Exp).then_inc(lam_exp, 1)
            for t in (NT - 1, NT):
                x_hi(t, t % 2, key_col(t), P)

            nc.scalar.preload_act_table_set("silu_and_others")

            def feature(f, first=False, last=False):
                if not first:
                    unit_hi(4 * f + 1, 1, unit_mm, 4 * f)
                act.wait_ge(unit_mm, 4 * f + 1)
                if not first:
                    act.wait_ge(y_done, f)
                nc.scalar.activation(cz.rearrange("p (b n) -> p b n", b=3), ps[:, 0:3, 0:CW], ACT.Copy).then_inc(c_done, 1)
                unit_hi(4 * f + 2, 0, unit_mm, 4 * f + 1)
                act.wait_ge(o_in, 16 * f + 16)
                nc.scalar.activation(wo_hi[:, :, bass.ds(f * P, P)], raw_o, ACT.Copy).then_inc(o_hi, 1)
                unit_hi(4 * f + 3, 1, unit_mm, 4 * f + 2)
                if not last:
                    unit_hi(4 * f + 4, 0, unit_mm, 4 * f + 3)
                else:
                    act.wait_ge(y_done, KT - 1)
                    act.wait_ge(unit_mm, U1 - 1)
                    nc.scalar.activation(ring[:, 0, 0, 0:KT - 1], Y[:, 0:KT - 1, 0:P], ACT.Copy).then_inc(y0_hi, 1)
                act.wait_ge(unit_mm, 4 * f + 4)
                act.wait_ge(v_done, f + 1)
                nc.scalar.activation(cz.rearrange("p (b n) -> p b n", b=3), ps[:, 3:6, 0:CW], ACT.Silu).then_inc(z_done, 1)

            feature(0, first=True)
            with act.Fori(1, KT - 1) as f:
                feature(f)
            feature(KT - 1, last=True)


            def y_tile_hi(t, slot, col):
                act.wait_ge(y_done, KT)
                nc.scalar.activation(ring[:, slot, 0], Y[:, :, bass.ds(col, P)], ACT.Copy).then_inc(y_hi, 1)

            N2 = NT + 1

            def step2(t, par, nxt=True, prev=True, prev2=True, meta2=False):
                if nxt:
                    act.wait_ge(out_mm, t)
                    y_tile_hi(t + 1, 1 - par, M + t * P)
                if prev2:
                    x_hi(N2 + t - 2, par, 0 if meta2 else M + (t - 3) * P, M if meta2 else P)
                if prev:
                    act.wait_ge(h1_done, t)
                    act.wait_ge(xn_done, N2 + t - 2)
                    act.wait_ge(xl_done, N2 + t - 2)
                    stats(N2 + t - 1, 1 - par, ht[1 - par])

            act.wait_ge(y_done, KT)
            nc.scalar.activation(ring[:, 0, 0, KT - 1], Y[:, KT - 1, 0:P], ACT.Copy).then_inc(y_hi, 1)
            y_tile_hi(1, 1, M)
            nc.scalar.preload_act_table_set("natural_log_exp_and_others")
            step2(1, 1, prev2=False)
            step2(2, 0, meta2=True)
            with act.Fori(0, (NT - 4) // 2) as i:
                step2(2 * i + 3, 1)
                step2(2 * i + 4, 0)
            step2(NT - 1, 1)
            unit_hi(U1, SLOT["V"], out_mm, NT)
            step2(NT, 0, nxt=False)
            step2(NT + 1, 1, nxt=False)
            unit_hi(U1 + 1, SLOT["K"], out_mm, NT + 1)
            x_hi(N2 + NT, 0, M + (NT - 1) * P, P)

            def chunk(kind, h, c):
                act.wait_ge(chunk_mm, CHUNKS * h + CHUNK_OF[kind] + c + 1)
                return ps[:, chunk_bank(kind, c), 0:CW if kind in "VK" else QW]

            def v_chunk(h, c):
                b = chunk("V", h, c)
                nc.scalar.activation(v_t[:, CW * c:CW * (c + 1)], b, ACT.Copy).then_inc(vz_out, 1)

            def k_chunk_hi(h, c, scores=None):
                b = chunk("K", h, c)
                if scores is not None:
                    act.wait_ge(s_mm, scores)
                nc.scalar.activation(keys[0][0:HD, 0, CW * c:CW * (c + 1)], b[0:HD], ACT.Copy)
                nc.scalar.activation(keys[1][HD:P, 0, CW * c:CW * (c + 1)], b[HD:P], ACT.Copy).then_inc(chunk_hi, 1)

            def q_chunk_hi(h, c):
                b = chunk("Q", h, c)
                nc.scalar.activation(queries[0][0:HD, QW * c:QW * (c + 1)], b[0:HD], ACT.Copy)
                nc.scalar.activation(queries[1][HD:P, QW * c:QW * (c + 1)], b[HD:P], ACT.Copy).then_inc(chunk_hi, 1)

            def z_copy(h):
                act.wait_ge(y_head, h + 1)
                act.wait_ge(chunk_mm, CHUNKS * h + CHUNK_OF["Z"] + 2)
                nc.scalar.activation(z_act.rearrange("p (c n) -> p c n", c=2), ps[:, 3:5, :], ACT.Copy).then_inc(vz_out, 1)

            def round_hi_v(n, par, tiles, pvs):
                act.wait_ge(round_mm, n + 1)
                if pvs is not None:
                    act.wait_ge(pv_mm, pvs)
                b = ps[:, round_bank(par), 0:P * len(tiles)]
                if tiles == [0]:
                    nc.scalar.activation(V[0:M, 0, 0, :], b[0:M], ACT.Copy).then_inc(round_hi, 1)
                else:
                    nc.scalar.activation(V[:, 0, tiles[0]:tiles[-1] + 1, :], b.rearrange("p (j v) -> p j v", v=P),
                                         ACT.Copy).then_inc(round_hi, 1)

            def round_hi_a(n, par, tiles, half, pvs):
                act.wait_ge(round_mm, n + 1)
                if pvs is not None:
                    act.wait_ge(pv_mm, pvs)
                b = ps[:, round_bank(par), 0:P * len(tiles)].rearrange("p (j q) -> p j q", q=P)
                qs = slice(P * half, P * half + P)
                full = [j for j in tiles if j]
                last = None
                if full:
                    last = nc.scalar.activation(attn_t[:, 0, full[0]:full[-1] + 1, qs], b[:, 0:len(full)], ACT.Copy)
                if 0 in tiles:
                    last = nc.scalar.activation(attn_t[:, 0, 0:1, qs], b[:, len(full):len(full) + 1], ACT.Copy)
                last.then_inc(round_hi, 1)

            def exp(h, i, c):
                n = 2 * (NT * h + i) + c
                act.wait_ge(s_out, n + 2)
                nb, w = s_shape(i)
                e = E[i % 2][c][:, 0:nb * w]
                nc.scalar.activation(e, e, ACT.Exp, bias=neg_max[:, i % 2, c:c + 1], scale=-1.0,
                                     accum_out=z_sum[:, i % 2, c:c + 1]).then_inc(exp_done, 1)

            def o_group(h, g):
                act.wait_ge(pv_mm, 4 * h + g + 1)
                nc.scalar.activation(o_t[:, 2 * P * g:2 * P * (g + 1)], ps[:, 7, 0:2 * P], ACT.Copy).then_inc(o_copied, 1)
                nc.scalar.activation(o_sq, ps[:, 7, 0:2 * P], ACT.Square).then_inc(o_squared, 1)

            def ln_group(h, g):
                act.wait_ge(ms_mm, 4 * h + g + 1)
                nc.scalar.activation(r_o[:, 2 * P * g:2 * P * (g + 1)], ps[:, 7, 0:2 * P], ACT.Ln, bias=eps[:],
                                     scale=1.0 / P).then_inc(ms_ln, 1)

            for c in range(3):
                v_chunk(0, c)
            for c in range(3):
                k_chunk_hi(0, c)
                if c == 0:
                    unit_hi(U1 + 2, SLOT["Q"], chunk_mm, 3)
            for r, tiles in enumerate(V_ROUNDS):
                round_hi_v(r, r, tiles, None)
            unit_hi(U1 + 3, SLOT["Z"], chunk_mm, 6)
            for c in range(2):
                q_chunk_hi(0, c)

            def wb_unit_hi(j):
                act.wait_ge(wb_in[j % 2], 16 * (j // 2 + 1))
                act.wait_ge(chunk_mm, CHUNKS * NH)
                nc.scalar.activation(X_hi[:, :, j * P:(j + 1) * P], raw[j % 2], ACT.Copy).then_inc(wb_hi, 1)

            def head(h, last):
                R0 = RP + RH * h
                u = U1 + 4 + UH * h
                for i in range(NT):
                    if not last and i == 4:
                        v_chunk(h + 1, 0)
                    exp(h, i, 0)
                    if i >= 4 and i % 2 == 0:
                        ln_group(h, (i - 4) // 2)
                    exp(h, i, 1)
                    if i == 2:
                        z_copy(h)
                    if not last and i == 5:
                        v_chunk(h + 1, 1)
                    if i >= 1:
                        attn_rounds(h, i - 1, R0)
                    if i >= 3 and i % 2 == 1:
                        o_group(h, (i - 3) // 2)
                    if not last:
                        if i == 7:
                            v_chunk(h + 1, 2)
                        if i == 0:
                            unit_hi(u, SLOT["V"], chunk_mm, CHUNKS * h + 8)
                        if i == 3:
                            unit_hi(u + 1, SLOT["K"], chunk_mm, CHUNKS * h + 10)
                    for j in WB_AT[i] if last else ():
                        wb_unit_hi(j)
                if not last:
                    unit_hi(u + 2, SLOT["Q"], chunk_mm, CHUNKS * (h + 1) + 3)
                    k_chunk_hi(h + 1, 0, 2 * NT * (h + 1))
                for r in range(3):
                    attn_round(h, NT - 1, R0, r)
                    if r == 1:
                        ln_group(h, 2)
                        if not last:
                            k_chunk_hi(h + 1, 1)
                act.wait_ge(vz_out, 4 * h + 4)
                nc.scalar.activation(z_act, z_act, ACT.Silu).then_inc(z_silu, 1)
                nc.scalar.preload_act_table_set("natural_log_exp_and_others")
                if not last:
                    k_chunk_hi(h + 1, 2)
                    unit_hi(u + 3, SLOT["Z"], chunk_mm, CHUNKS * (h + 1) + 6)
                o_group(h, 3)
                if not last:
                    for r, tiles in enumerate(V_ROUNDS):
                        round_hi_v(R0 + 14 + r, 14 + r, tiles, 4 * (h + 1))
                ln_group(h, 3)
                act.wait_ge(ms_ln, 4 * (h + 1))
                nc.scalar.activation(r_o[:, 0:T], r_o[:, 0:T], ACT.Exp, scale=-0.5).then_inc(r_done, 1)
                if not last:
                    q_chunk_hi(h + 1, 0)
                    q_chunk_hi(h + 1, 1)

            def attn_rounds(h, i, R0):
                for r in range(len(rounds_of(i))):
                    attn_round(h, i, R0, r)

            def attn_round(h, i, R0, r):
                n = ROUND_AT[i] + r
                pvs = 4 * h + i // 2 if i % 2 == 0 and i > 0 else None
                round_hi_a(R0 + n, n, rounds_of(i)[r], i % 2, pvs)

            with act.Fori(0, NH - 1) as h:
                head(h, False)
            head(NH - 1, True)

            def y4_hi_tile(t, slot):
                act.wait_ge(y4_in[slot], (t // 2 + 1) * 16)
                if t >= 2:
                    act.wait_ge(out4_mm, t - 1)
                nc.scalar.activation(ring[:, slot, 0], y4[slot], ACT.Copy).then_inc(y4_hi, 1)

            N4 = 2 * N2
            y4_hi_tile(0, 0)
            for t in range(NT):
                if t + 1 < NT:
                    y4_hi_tile(t + 1, (t + 1) % 2)
                act.wait_ge(h2_done, t + 1)
                if t >= 2:
                    act.wait_ge(o4_done, t - 1)
                stats(N4 + t, t % 2, h4[t % 2])

        @block.tensor
        def _(pe):
            N2 = NT + 1

            def three(out_ap, wh, wl, xh, xl, start, stop):
                pe.matmul(out_ap, wh, xh, start=start, stop=False)
                pe.matmul(out_ap, wh, xl, start=False, stop=False)
                return pe.matmul(out_ap, wl, xh, start=False, stop=stop)

            def transpose_tile(n, slot, src, reused=True):
                pe.wait_ge(xn_done, n + 1)
                if reused:
                    pe.wait_ge(xh_done, n - 1)
                    pe.wait_ge(xl_done, n - 1)
                for k in range(KT):
                    mm = pe.transpose(ps[:, tr_bank(slot) + k // 4, P * (k % 4):P * (k % 4) + P],
                                      src[:, k * P:(k + 1) * P], ident[:])
                mm.then_inc(tr_done, 1)

            pe.wait_ge(ident_made, 4)
            def unit_part(slot, bank, c, k0=0, k1=KT):
                for k in range(k0, k1):
                    mm = three(ps[:, bank + c, 0:CW], ring[:, slot, 0, k], ring[:, slot, 1, k],
                               X_hi[:, k, CW * c:CW * (c + 1)], X_lo[:, k, CW * c:CW * (c + 1)],
                               k == 0, k == KT - 1)
                return mm

            for t in range(NT + 1):
                transpose_tile(t, t % 2, x0[t % X0S], reused=t >= 2)
                if t == 1:
                    pe.wait_ge(const_in, 16 * 12)
                    pe.wait_ge(rows_zero, 1)
                    pe.transpose(ps[:, 3, 0:P], gain_rows, ident[:]).then_inc(gains_mm, 1)
                if t == 6:
                    pe.wait_ge(xl_done, 4)
                    pe.wait_ge(w_lo, 1)
                    unit_part(0, 0, 0, 0, 4)
                if t == 7:
                    unit_part(0, 0, 0, 4, KT)
            pe.wait_ge(xl_done, 7)
            unit_part(0, 0, 1)
            pe.wait_ge(pads_zero, 2)
            pe.wait_ge(xl_done, NT + 1)
            unit_part(0, 0, 2).then_inc(unit_mm, 1)

            def unit(u, slot, bank, read=None, count=0):
                pe.wait_ge(w_lo, u + 1)
                if read is not None:
                    pe.wait_ge(read, count)
                for c in range(3):
                    mm = unit_part(slot, bank, c)
                mm.then_inc(unit_mm, 1)

            def second_half(f):
                unit(4 * f + 2, 0, 0, c_done, f + 1)
                unit(4 * f + 3, 1, 3, v_done, f + 1)

            pe.wait_ge(gains_done, 1)
            unit(1, 1, 3)
            with pe.Fori(0, KT - 1) as f:
                second_half(f)
                unit(4 * f + 4, 0, 0, b_done, f + 1)
                unit(4 * f + 5, 1, 3, z_done, f + 1)
            second_half(KT - 1)

            def out_tile(t, slot, hi_sem, lo_sem, wh, wl, read, count, done, early=None):
                if early is not None:
                    pe.wait_ge(early[0], 1)
                    pe.wait_ge(early[1], 1)
                if count is not None:
                    pe.wait_ge(read, count)
                for c in range(2):
                    for k in range(KT):
                        if c == 0 and k == (0 if early is None else KT - 1):
                            pe.wait_ge(hi_sem, t + 1)
                            pe.wait_ge(lo_sem, t + 1)
                        mm = three(ps[:, 2 * slot + c, :], ring[:, slot, 0, k], ring[:, slot, 1, k],
                                   wh[:, k, 512 * c:512 * (c + 1)], wl[:, k, 512 * c:512 * (c + 1)],
                                   k == 0, k == KT - 1)
                mm.then_inc(done, 1)

            def out2(t, slot, count, early=None):
                out_tile(t, slot, y_hi, y_lo, wo_hi, wo_lo, h1_done, count, out_mm, early)

            pe.wait_ge(o_hi, KT)
            pe.wait_ge(o_lo, KT)
            pe.wait_ge(b_done, KT)
            out2(0, 0, None, (y0_hi, y0_lo))
            pe.wait_ge(z_done, KT)
            out2(1, 1, None)
            transpose_tile(N2, 0, xt[0])
            with pe.Fori(0, (NT - 2) // 2) as i:
                t = 2 * i + 2
                out2(t, 0, t - 1)
                transpose_tile(N2 + t - 1, 1, xt[1])
                out2(t + 1, 1, t)
                transpose_tile(N2 + t, 0, xt[0])
            out2(NT, 0, NT - 1)
            transpose_tile(N2 + NT - 1, 1, xt[1])

            def chunk(kind, h, c, read=None, count=0, k0=0, k1=KT):
                slot = SLOT[kind]
                width, first = (CW, 0) if kind in "VK" else (QW, M)
                if k0 == 0:
                    pe.wait_ge(w_lo, U1 + UH * h + "VKQZ".index(kind) + 1)
                    if read is not None:
                        pe.wait_ge(read, count)
                o = ps[:, chunk_bank(kind, c), 0:width]
                for k in range(k0, k1):
                    cols = slice(first + width * c, first + width * (c + 1))
                    mm = three(o, ring[:, slot, 0, k], ring[:, slot, 1, k], X_hi[:, k, cols], X_lo[:, k, cols],
                               k == 0, k == KT - 1)
                if k1 == KT:
                    mm.then_inc(chunk_mm, 1)

            def v_rounds(h, n0, rounds=range(len(V_ROUNDS))):
                pe.wait_ge(vz_out, 4 * h + 3)
                for r, tiles in [(r, V_ROUNDS[r]) for r in rounds]:
                    if n0 is not None:
                        pe.wait_ge(round_hi, n0 + r - 1)
                        pe.wait_ge(round_lo, n0 + r - 1)
                    elif r >= 2:
                        pe.wait_ge(round_hi, r - 1)
                        pe.wait_ge(round_lo, r - 1)
                    for q, j in enumerate(tiles):
                        mm = pe.transpose(ps[:, round_bank(r), P * q:P * (q + 1)],
                                          v_t[:, key_col(j):key_col(j) + P], ident[:])
                    mm.then_inc(round_mm, 1)

            pe.wait_ge(xh_done, N2 + NT)
            pe.wait_ge(xl_done, N2 + NT)
            chunk("V", 0, 0)
            transpose_tile(N2 + NT, 0, xt[0])
            chunk("V", 0, 1, vz_out, 1)
            pe.wait_ge(h1_done, NT)
            pe.wait_ge(xh_done, N2 + NT + 1)
            pe.wait_ge(xl_done, N2 + NT + 1)
            chunk("V", 0, 2, vz_out, 2)
            chunk("K", 0, 0)
            chunk("K", 0, 1, vz_out, 3)
            chunk("K", 0, 2, kq_out, 1)
            v_rounds(0, None)
            chunk("Q", 0, 0, kq_out, 3)
            chunk("Q", 0, 1, kq_out, 2)

            def scores(h, i, c):
                pe.wait_ge(s_out, s_read(h, i, c))
                nb, w = s_shape(i)
                q = queries[c][:, P * i:P * (i + 1)]
                bank = s_bank(i, c)
                for b in range(nb):
                    o = ps[:, bank + b, 0:w]
                    pe.matmul(o, q, keys[c][:, 0, b * w:(b + 1) * w], start=True, stop=False)
                    pe.matmul(o, q, keys[c][:, 1, b * w:(b + 1) * w], start=False, stop=b < nb - 1)
                hidden = HD + (nb * w - (M + P * (i + 1)))
                pe.matmul(ps[:, bank + nb - 1, w - hidden:w], mask_q[:], mask_k[:, 0:hidden], start=False,
                          stop=True).then_inc(s_mm, 1)

            def attn_rounds(h, i, rounds=None):
                pe.wait_ge(attn_done, NT * h + i + 1)
                for r in range(len(rounds_of(i))) if rounds is None else rounds:
                    tiles = rounds_of(i)[r]
                    n = ROUND_AT[i] + r
                    pe.wait_ge(round_hi, RP + RH * h + n - 1)
                    pe.wait_ge(round_lo, RP + RH * h + n - 1)
                    for q, j in enumerate(tiles):
                        mm = pe.transpose(ps[:, round_bank(n), P * q:P * (q + 1)],
                                          E[i % 2][0][:, key_col(j):key_col(j) + P], ident[:])
                    mm.then_inc(round_mm, 1)

            def products(h, g):
                n = RP + RH * h + ROUND_AT[2 * g + 1] + len(rounds_of(2 * g + 1))
                pe.wait_ge(round_hi, n)
                pe.wait_ge(round_lo, n)
                if g:
                    pe.wait_ge(ms_ln, 4 * h + g)
                for j in range(2 * g + 3):
                    q = slice(P if j == 2 * g + 2 else 0, 2 * P)
                    mm = three(ps[:, 7, q], V[:, 0, j], V[:, 1, j], attn_t[:, 0, j, q], attn_t[:, 1, j, q],
                               j == 0, j == 2 * g + 2)
                mm.then_inc(pv_mm, 1)

            def mean_squares(h, g):
                pe.wait_ge(o_squared, 4 * h + g + 1)
                pe.matmul(ps[:, 7, 0:2 * P], ones[:], o_sq, start=True, stop=True).then_inc(ms_mm, 1)

            PARTS = ((0, 3), (3, 6), (6, KT))

            def filler(h, p, last):
                k0, k1 = PARTS[p % 3]
                c = p // 3
                if c < 2:
                    chunk("Z", h, c, kq_out, 5 * h + 4 + c, k0, k1)
                elif not last:
                    chunk("V", h + 1, c - 2, vz_out, 4 * h + 4 + c - 2, k0, k1)

            pe.wait_ge(masks_made, 7)
            pe.wait_ge(v_zero, 2)

            def head(h, last):
                filler(h, 0, last)
                pe.wait_ge(keys_dup, 32 * h + 32)
                pe.wait_ge(kq_out, 5 * h + 5)
                for i in range(NT):
                    if i == 3:
                        pe.wait_ge(vz_out, 4 * h + 4)
                    for c in range(2):
                        scores(h, i, c)
                        if FILL_AT[2 * i + c] is not None:
                            filler(h, FILL_AT[2 * i + c], last)
                        if c == 0 and i >= 4 and i % 2 == 0:
                            mean_squares(h, (i - 4) // 2)
                    if i >= 3 and i % 2 == 1:
                        products(h, (i - 3) // 2)
                    if i >= 1:
                        attn_rounds(h, i - 1)
                if not last:
                    chunk("K", h + 1, 0, s_out, 2 * NT * (h + 1))
                attn_rounds(h, NT - 1, (0, 1))
                mean_squares(h, 2)
                if not last:
                    chunk("K", h + 1, 1, vz_out, 4 * (h + 1) + 3)
                attn_rounds(h, NT - 1, (2,))
                if not last:
                    chunk("K", h + 1, 2, kq_out, 5 * (h + 1) + 1)
                products(h, 3)
                if not last:
                    v_rounds(h + 1, RP + RH * h + 14, (0, 1))
                    chunk("Q", h + 1, 0, kq_out, 5 * (h + 1) + 3, 0, 3)
                    v_rounds(h + 1, RP + RH * h + 14, (2, 3))
                mean_squares(h, 3)
                if not last:
                    chunk("Q", h + 1, 0, k0=3)
                    chunk("Q", h + 1, 1, kq_out, 5 * (h + 1) + 2)

            with pe.Fori(0, NH - 1) as h:
                head(h, False)
            head(NH - 1, True)

            pe.wait_ge(wb_hi, KT)
            pe.wait_ge(wb_lo, KT)
            pe.wait_ge(s_out, 2 * NT * NH + 1)
            for t in range(2):
                out_tile(t, t, y4_hi, y4_lo, X_hi, X_lo, h2_done, None, out4_mm)
            with pe.Fori(1, NT // 2) as i:
                for s in range(2):
                    out_tile(2 * i + s, s, y4_hi, y4_lo, X_hi, X_lo, h2_done, 2 * i + s - 1, out4_mm)

        @block.vector
        def _(dve):
            N2 = NT + 1
            N4 = 2 * N2

            def unit_lo(u, slot):
                dve.wait_ge(w_hi, u + 1)
                nc.vector.tensor_tensor(ring[:, slot, 1], raw[slot], ring[:, slot, 0], ALU.subtract).then_inc(w_lo, 1)

            def inverse_root(n, slot):
                s = stat[:, slot]
                dve.wait_ge(r0_done, n + 1)
                nc.vector.tensor_scalar(s[:, 1:2], s[:, 0:1], 1.0 / D, EPS, ALU.mult, ALU.add).then_inc(newton, 1)
                dve.wait_ge(newton, 4 * n + 1)
                nc.vector.tensor_scalar(s[:, 4:5], s[:, 3:4], s[:, 3:4], s[:, 1:2], ALU.mult, ALU.mult).then_inc(newton, 1)
                dve.wait_ge(newton, 4 * n + 2)
                nc.vector.tensor_scalar(s[:, 5:6], s[:, 4:5], -0.5, 1.5, ALU.mult, ALU.add).then_inc(newton, 1)
                dve.wait_ge(newton, 4 * n + 3)
                nc.vector.tensor_tensor(s[:, 6:7], s[:, 3:4], s[:, 5:6], ALU.mult).then_inc(newton, 1)
                dve.wait_ge(newton, 4 * n + 4)
                return s[:, 6:7]

            def x_lo(n, slot, col, width):
                dve.wait_ge(xh_done, n + 1)
                nc.vector.tensor_tensor(X_lo[:, :, bass.ds(col, width)],
                                        flat(tr_bank(slot), D).rearrange("p (k n) -> p k n", k=KT)[:, :, 0:width],
                                        X_hi[:, :, bass.ds(col, width)], ALU.subtract).then_inc(xl_done, 1)

            for t in range(NT + 1):
                r = inverse_root(t, t % 2)
                nc.vector.tensor_scalar(x0[t % X0S], x0[t % X0S], r, None, ALU.mult).then_inc(xn_done, 1)
                if t >= 2:
                    x_lo(t - 2, t % 2, key_col(t - 2), M if t == 2 else P)
                if t == 5:
                    unit_lo(0, 0)
                if t == 7:
                    unit_lo(1, 1)
            dve.wait_ge(const_in, 16 * 12)
            for j in range(2):
                nc.vector.tensor_tensor(lam_in[:, 2 * j], lam_in[:, 2 * j], lam_in[:, 2 * j + 1], ALU.mult).then_inc(lam_step, 1)
            for j in range(2):
                dve.wait_ge(lam_step, j + 1)
                nc.vector.tensor_reduce(lam_s[:, j:j + 1], lam_in[:, 2 * j], AX_X, ALU.add).then_inc(lam_step, 1)
            for t in (NT - 1, NT):
                x_lo(t, t % 2, key_col(t), P)

            dve.wait_ge(gains_done, 1)
            nc.vector.tensor_scalar(g_sub[:, 1:2], gains[:, 7 * KT:7 * KT + 1], 1.0 - LAMBDA_INIT, None, ALU.mult).then_inc(lam_step, 1)
            dve.wait_ge(lam_exp, 1)
            nc.vector.tensor_scalar(lam_s[:, 7:8], lam_s[:, 2:3], lam_s[:, 3:4], LAMBDA_INIT, ALU.subtract,
                                    ALU.add).then_inc(lam_done, 1)

            cz3 = cz.rearrange("p (b n) -> p b n", b=3)
            conv3 = conv.rearrange("p (b n) -> p b n", b=3)
            nc.vector.memset(vpad[:, 0:2], 0.0).then_inc(vpad_zero, 1)

            def feature(f, first=False, last=False):
                if not first:
                    unit_lo(4 * f + 1, 1)
                unit_lo(4 * f + 2, 0)
                dve.wait_ge(o_hi, f + 1)
                nc.vector.tensor_tensor(wo_lo[:, :, bass.ds(f * P, P)], raw_o, wo_hi[:, :, bass.ds(f * P, P)],
                                        ALU.subtract).then_inc(o_lo, 1)
                dve.wait_ge(unit_mm, 4 * f + 2)
                dve.wait_ge(c_done, f + 1)
                nc.vector.tensor_tensor(vpad[:, 2:2 + LP].rearrange("p (b n) -> p b n", b=3), ps[:, 3:6, 0:CW], cz3,
                                        ALU.mult).then_inc(v_done, 1)
                dve.wait_ge(v_done, f + 1)
                nc.vector.tensor_scalar(conv, vpad[:, 0:LP], conv_w[:, 0, bass.ds(f, 1)], conv_b[:, bass.ds(f, 1)],
                                        ALU.mult, ALU.add).then_inc(conv_step, 1)
                for j in (1, 2):
                    dve.wait_ge(conv_step, 3 * f + j)
                    nc.vector.scalar_tensor_tensor(out=conv, in0=vpad[:, j:j + LP], scalar=conv_w[:, j, bass.ds(f, 1)],
                                                   in1=conv, op0=ALU.mult, op1=ALU.add).then_inc(conv_step, 1)
                unit_lo(4 * f + 3, 1)
                dve.wait_ge(unit_mm, 4 * f + 3)
                dve.wait_ge(conv_step, 3 * f + 3)
                nc.vector.tensor_tensor(conv3, ps[:, 0:3, 0:CW], conv3, ALU.mult).then_inc(b_done, 1)
                if not last:
                    unit_lo(4 * f + 4, 0)
                else:
                    dve.wait_ge(y0_hi, 1)
                    nc.vector.tensor_tensor(ring[:, 0, 1, 0:KT - 1], Y[:, 0:KT - 1, 0:P], ring[:, 0, 0, 0:KT - 1],
                                            ALU.subtract).then_inc(y0_lo, 1)
                dve.wait_ge(z_done, f + 1)
                dve.wait_ge(b_done, f + 1)
                nc.vector.tensor_tensor(Y[:, bass.ds(f, 1), :], conv.rearrange("p (a n) -> p a n", a=1),
                                        cz.rearrange("p (a n) -> p a n", a=1), ALU.mult).then_inc(y_done, 1)

            dve.wait_ge(vpad_zero, 1)
            feature(0, first=True)
            with dve.Fori(1, KT - 1) as f:
                feature(f)
            feature(KT - 1, last=True)

            def y_tile_lo(t, slot, col):
                dve.wait_ge(y_hi, t + 1)
                dve.wait_ge(y_done, KT)
                nc.vector.tensor_tensor(ring[:, slot, 1], Y[:, :, bass.ds(col, P)], ring[:, slot, 0],
                                        ALU.subtract).then_inc(y_lo, 1)

            def h1_tile(t, slot, x_count, reused=True):
                dve.wait_ge(out_mm, t + 1)
                dve.wait_ge(x_in[slot], x_count)
                if reused:
                    dve.wait_ge(h1_stored[slot], stored_before(t, slot))
                nc.vector.tensor_tensor(ht[slot], flat(2 * slot, D), xt[slot], ALU.add).then_inc(h1_done, 1)

            def stored_before(t, slot):
                return 8 * (t - 2) if slot == 0 else 8 * (t - 1)

            def x2_count(t, slot):
                return 32 + 8 * t if slot == 0 else 8 * (t + 1)

            def step2(t, par, nxt=True, prev=True, prev2=True, first=False, meta2=False):
                if prev:
                    h1_tile(t - 1, 1 - par, x2_count(t - 1, 1 - par), reused=not first)
                if nxt:
                    y_tile_lo(t + 1, 1 - par, M + t * P)
                if prev2:
                    x_lo(N2 + t - 2, par, 0 if meta2 else M + (t - 3) * P, M if meta2 else P)
                if prev:
                    r = inverse_root(N2 + t - 1, 1 - par)
                    nc.vector.tensor_scalar(xt[1 - par], ht[1 - par], r, None, ALU.mult).then_inc(xn_done, 1)

            dve.wait_ge(y_hi, 1)
            dve.wait_ge(y_done, KT)
            nc.vector.tensor_tensor(ring[:, 0, 1, KT - 1], Y[:, KT - 1, 0:P], ring[:, 0, 0, KT - 1],
                                    ALU.subtract).then_inc(y_lo, 1)
            y_tile_lo(1, 1, M)
            step2(1, 1, prev2=False, first=True)
            step2(2, 0, first=True, meta2=True)
            with dve.Fori(0, (NT - 4) // 2) as i:
                step2(2 * i + 3, 1)
                step2(2 * i + 4, 0)
            step2(NT - 1, 1)
            unit_lo(U1, SLOT["V"])
            step2(NT, 0, nxt=False)
            step2(NT + 1, 1, nxt=False)
            unit_lo(U1 + 1, SLOT["K"])
            x_lo(N2 + NT, 0, M + (NT - 1) * P, P)

            def k_chunk_lo(h, c):
                dve.wait_ge(chunk_hi, 5 * h + c + 1)
                b = ps[:, chunk_bank("K", c), 0:CW]
                for q, rows in enumerate((slice(0, HD), slice(HD, P))):
                    ins = nc.vector.tensor_tensor(keys[q][rows, 1, CW * c:CW * (c + 1)], b[rows],
                                                  keys[q][rows, 0, CW * c:CW * (c + 1)], ALU.subtract)
                ins.then_inc(kq_out, 1)

            def q_chunk_lo(h, c):
                dve.wait_ge(chunk_hi, 5 * h + 3 + c + 1)
                b = ps[:, chunk_bank("Q", c), :]
                cols = slice(QW * c, QW * (c + 1))
                nc.vector.tensor_tensor(queries[0][HD:P, cols], b[0:HD], queries[0][0:HD, cols], ALU.subtract)
                nc.vector.tensor_tensor(queries[1][0:HD, cols], b[HD:P], queries[1][HD:P, cols],
                                        ALU.subtract).then_inc(kq_out, 1)

            def round_lo_v(n, par, tiles):
                dve.wait_ge(round_hi, n + 1)
                b = ps[:, round_bank(par), 0:P * len(tiles)]
                if tiles == [0]:
                    nc.vector.tensor_tensor(V[0:M, 1, 0, :], b[0:M], V[0:M, 0, 0, :], ALU.subtract).then_inc(round_lo, 1)
                else:
                    js = slice(tiles[0], tiles[-1] + 1)
                    nc.vector.tensor_tensor(V[:, 1, js, :], b.rearrange("p (j v) -> p j v", v=P), V[:, 0, js, :],
                                            ALU.subtract).then_inc(round_lo, 1)

            def attn_rounds(h, i):
                for r in range(len(rounds_of(i))):
                    attn_round(h, i, r)

            def attn_round(h, i, r):
                tiles = rounds_of(i)[r]
                n = ROUND_AT[i] + r
                dve.wait_ge(round_hi, RP + RH * h + n + 1)
                b = ps[:, round_bank(n), 0:P * len(tiles)].rearrange("p (j q) -> p j q", q=P)
                qs = slice(P * (i % 2), P * (i % 2) + P)
                full = [j for j in tiles if j]
                if full:
                    js = slice(full[0], full[-1] + 1)
                    ins = nc.vector.tensor_tensor(attn_t[:, 1, js, qs], b[:, 0:len(full)], attn_t[:, 0, js, qs],
                                                  ALU.subtract)
                if 0 in tiles:
                    ins = nc.vector.tensor_tensor(attn_t[:, 1, 0:1, qs], b[:, len(full):len(full) + 1],
                                                  attn_t[:, 0, 0:1, qs], ALU.subtract)
                ins.then_inc(round_lo, 1)

            def scores_out(h, i, c):
                n = 2 * (NT * h + i) + c
                dve.wait_ge(s_mm, n + 1)
                nb, w = s_shape(i)
                e = E[i % 2][c][:, 0:nb * w].rearrange("p (b n) -> p b n", b=nb)
                bank = s_bank(i, c)
                nc.vector.tensor_scalar(e, ps[:, bank:bank + nb, 0:w], -SCALE, None, ALU.mult, ALU.min,
                                        accum_out=neg_max[:, i % 2, c:c + 1]).then_inc(s_out, 1)

            def inverse_sums(h, i):
                dve.wait_ge(exp_done, 2 * (NT * h + i) + 2)
                nc.vector.reciprocal(z_inv[:, i % 2, 0:2], z_sum[:, i % 2, :]).then_inc(recip_done, 1)
                dve.wait_ge(recip_done, NT * h + i + 1)
                nc.vector.tensor_tensor(z_inv[:, i % 2, 2:3], z_inv[:, i % 2, 1:2], lam_s[:, 7:8],
                                        ALU.mult).then_inc(inv_done, 1)

            def combine(h, i):
                dve.wait_ge(e1_scaled, NT * h + i + 1)
                nb, w = s_shape(i)
                nc.vector.scalar_tensor_tensor(out=E[i % 2][0][:, 0:nb * w], in0=E[i % 2][0][:, 0:nb * w],
                                               scalar=z_inv[:, i % 2, 0:1], in1=E[i % 2][1][:, 0:nb * w],
                                               op0=ALU.mult, op1=ALU.subtract).then_inc(attn_done, 1)

            def y_out(h):
                dve.wait_ge(or_done, h + 1)
                dve.wait_ge(z_silu, h + 1)
                dve.wait_ge(y_stored, 16 * (h + 1))
                nc.vector.scalar_tensor_tensor(out=y_o, in0=o_t, scalar=g_sub[:, 1:2], in1=z_act, op0=ALU.mult,
                                               op1=ALU.mult).then_inc(y_head, 1)

            def wb_unit_lo(j):
                dve.wait_ge(wb_hi, j + 1)
                nc.vector.tensor_tensor(X_lo[:, :, j * P:(j + 1) * P], raw[j % 2], X_hi[:, :, j * P:(j + 1) * P],
                                        ALU.subtract).then_inc(wb_lo, 1)

            dve.wait_ge(lam_done, 1)
            dve.wait_ge(out_mm, NT + 1)
            for part in range(2):
                nc.vector.memset(V[:, part, 0, :].bitcast(F32), 0.0).then_inc(v_zero, 1)
            nc.vector.memset(neg_max[:], 0.0).then_inc(s_out, 1)
            nc.vector.memset(z_inv[:], 0.0).then_inc(y_head, 1)
            for c in range(3):
                k_chunk_lo(0, c)
                if c == 0:
                    unit_lo(U1 + 2, SLOT["Q"])
            for r, tiles in enumerate(V_ROUNDS):
                round_lo_v(r, r, tiles)
            unit_lo(U1 + 3, SLOT["Z"])
            for c in range(2):
                q_chunk_lo(0, c)

            def head(h, last):
                u = U1 + 4 + UH * h
                for i in range(NT):
                    scores_out(h, i, 0)
                    if i >= 1:
                        combine(h, i - 1)
                    scores_out(h, i, 1)
                    if i == NT - 1:
                        inverse_sums(h, i)
                    if i >= 1:
                        attn_rounds(h, i - 1)
                    if not last and i == 0:
                        unit_lo(u, SLOT["V"])
                    if i < NT - 1:
                        inverse_sums(h, i)
                    if not last and i == 3:
                        unit_lo(u + 1, SLOT["K"])
                    for j in WB_AT[i] if last else ():
                        wb_unit_lo(j)
                combine(h, NT - 1)
                if not last:
                    unit_lo(u + 2, SLOT["Q"])
                    k_chunk_lo(h + 1, 0)
                for r in range(3):
                    attn_round(h, NT - 1, r)
                    if not last and r == 1:
                        k_chunk_lo(h + 1, 1)
                if not last:
                    k_chunk_lo(h + 1, 2)
                    unit_lo(u + 3, SLOT["Z"])
                    for r, tiles in enumerate(V_ROUNDS):
                        round_lo_v(RP + RH * h + 14 + r, 14 + r, tiles)
                    q_chunk_lo(h + 1, 0)
                y_out(h)
                if not last:
                    q_chunk_lo(h + 1, 1)

            with dve.Fori(0, NH - 1) as h:
                head(h, False)
            head(NH - 1, True)

            def y4_lo_tile(t, slot):
                dve.wait_ge(y4_hi, t + 1)
                nc.vector.tensor_tensor(ring[:, slot, 1], y4[slot], ring[:, slot, 0], ALU.subtract).then_inc(y4_lo, 1)

            y4_lo_tile(0, 0)
            dve.wait_ge(gf_in, 16)
            for t in range(NT):
                s = t % 2
                if t + 1 < NT:
                    y4_lo_tile(t + 1, 1 - s)
                dve.wait_ge(out4_mm, t + 1)
                dve.wait_ge(h4_in[s], 16 * (t // 2 + 1))
                nc.vector.tensor_tensor(h4[s], flat(2 * s, D), h4[s], ALU.add).then_inc(h2_done, 1)
                r = inverse_root(N4 + t, s)
                if t >= 2:
                    dve.wait_ge(o4_stored[s], 16 * (t // 2))
                nc.vector.scalar_tensor_tensor(out=o4[s], in0=h4[s], scalar=r, in1=g_final, op0=ALU.mult,
                                               op1=ALU.mult).then_inc(o4_done, 1)


_INS = ['x', 'meta_tokens', 'a_norm_g', 'a_w_in', 'a_conv_w', 'a_conv_b', 'a_w_out', 'kv_norm_g', 'w_kv', 'b_norm_g',
        'b_w_in', 'b_lambda_q1', 'b_lambda_k1', 'b_lambda_q2', 'b_lambda_k2', 'b_subln_g', 'b_w_out', 'final_norm_g']


def kernel(**inputs):
    import numpy as _np
    import concourse.bacc as _bacc
    from concourse import mybir as _mybir
    from concourse.bass_utils import run_bass_kernel_spmd as _run

    nc = _bacc.Bacc("TRN2", target_bir_lowering=False, num_devices=1)
    arrays, args = {}, []
    for name in _INS:
        a = _np.ascontiguousarray(inputs[name])
        arrays[f"in_{name}_dram"] = a
        args.append(nc.dram_tensor(f"in_{name}_dram", a.shape, _mybir.dt.from_np(a.dtype), kind="ExternalInput").ap())
    args.append(nc.dram_tensor("out_0_dram", inputs["x"].shape, _mybir.dt.float32, kind="ExternalOutput").ap())
    yoco_kernel(nc, *args)
    r = _run(nc, [arrays], core_ids=[0])
    return r.results[0]["out_0_dram"]
```

```python
import math
from contextlib import ExitStack

import concourse.bass as bass
from concourse import mybir

P = 128
EPS = 1e-6
LAMBDA_INIT = 0.8 - 0.6 * math.exp(-0.3 * 1)

ALU = mybir.AluOpType
ACT = mybir.ActivationFunctionType
F32 = mybir.dt.float32
F32R = mybir.dt.float32r
BF16 = mybir.dt.bfloat16
AX_X = mybir.AxisListType.X
MASKED = -1.0e30


def yoco_kernel(nc, x, meta_tokens, a_norm_g, a_w_in, a_conv_w, a_conv_b, a_w_out, kv_norm_g, w_kv,
                b_norm_g, b_w_in, b_lambda_q1, b_lambda_k1, b_lambda_q2, b_lambda_k2, b_subln_g,
                b_w_out, final_norm_g, out):
    _, T, D = x.shape
    M = meta_tokens.shape[0]
    L = T + M
    KT = D // P
    NT = T // P
    CW = 348
    LP = 3 * CW
    NH = KT
    HD = P // 2
    QW = 512
    SCALE = HD ** -0.5
    assert L <= LP and T == 2 * QW and NH * P == D and a_conv_w.shape[1] == 3

    x_rows = x[0]
    out_rows = out[0]
    w_in_a = a_w_in[0].rearrange("(k p) n -> p k n", p=P)
    w_out_a = a_w_out[0].rearrange("(k p) n -> p k n", p=P)
    w_kv_v = w_kv.rearrange("(k p) n -> p k n", p=P)
    w_in_b = b_w_in[0].rearrange("(k p) n -> p k n", p=P)
    w_out_b = b_w_out[0].rearrange("(k p) n -> p k n", p=P)
    h1_dram = nc.dram_tensor("h1_scratch", [T, D], F32, kind="Internal").ap()
    y_dram = nc.dram_tensor("y_scratch", [P, NH - 1, T], F32, kind="Internal").ap()

    with ExitStack() as ctx:
        def sb(name, shape, dt):
            return ctx.enter_context(nc.sbuf_tensor(name, shape, dt))

        def sem(name):
            return ctx.enter_context(nc.semaphore(name))

        X_hi = sb("X_hi", [P, KT, LP], F32R)
        X_lo = sb("X_lo", [P, KT, LP], F32R)
        ring = sb("ring", [P, 2, 2, KT, P], F32R)
        BIGW = 2 * KT * D
        big = sb("big", [P, BIGW], F32R)
        wo_hi = big[:, 0:KT * D].rearrange("p (k n) -> p k n", k=KT)
        wo_lo = big[:, KT * D:2 * KT * D].rearrange("p (k n) -> p k n", k=KT)
        keys = [big[:, 2 * LP * c:2 * LP * (c + 1)].rearrange("p (s n) -> p s n", s=2) for c in range(2)]
        at = 4 * LP
        queries = [big[:, at + T * c:at + T * (c + 1)] for c in range(2)]
        at += 2 * T
        NK = NT + 1
        V = big[:, at:at + 2 * NK * P].rearrange("p (s j v) -> p s j v", s=2, j=NK)
        at += 2 * NK * P
        attn_t = big[:, at:at + 2 * NK * 2 * P].rearrange("p (s j q) -> p s j q", s=2, j=NK)
        at += 4 * NK * P
        attn_d = big[:, at:at + 4 * P].rearrange("p (s q) -> p s q", s=2)
        assert at + 4 * P <= BIGW

        WORK = KT * LP + 2 * D + D + 3 * LP + 16
        work = sb("work", [P, WORK], F32)
        raw_at = KT * LP
        misc_at = raw_at + 2 * D
        raw = [work[:, raw_at + D * s:raw_at + D * (s + 1)].rearrange("p (k n) -> p k n", k=KT) for s in range(2)]
        X0S = 6
        x0 = [work[:, D * s:D * (s + 1)] for s in range(X0S)]
        squares0 = work[:, D * X0S:D * (X0S + 1)]
        Y = work[:, 0:KT * LP].rearrange("p (k n) -> p k n", k=KT)
        raw_o = work[:, misc_at:misc_at + D].rearrange("p (k n) -> p k n", k=KT)
        cz = work[:, misc_at + D:misc_at + D + LP]
        vpad = work[:, misc_at + D + LP:misc_at + D + 2 * LP + 2]
        conv = work[:, misc_at + D + 2 * LP + 2:misc_at + D + 3 * LP + 2]
        xt = [work[:, misc_at + D * s:misc_at + D * (s + 1)] for s in range(2)]
        ht = [work[:, misc_at + D * (2 + s):misc_at + D * (3 + s)] for s in range(2)]
        E = [[work[:, LP * (2 * s + c):LP * (2 * s + c + 1)] for c in range(2)] for s in range(2)]
        v_t = work[:, 4 * LP:5 * LP]
        raw_b = raw + [v_t[:, 0:D].rearrange("p (k n) -> p k n", k=KT)]
        NB = len(raw_b)
        z_act = work[:, 5 * LP:5 * LP + T]
        o_t = work[:, 6 * LP:6 * LP + T]
        r_o = work[:, 7 * LP:7 * LP + T]
        y_o = work[:, misc_at:misc_at + T]
        o_sq = work[:, misc_at + T:misc_at + T + 2 * P]
        y4_at = misc_at + T + 2 * P
        W4 = (NH - 1) * P
        y4 = [work[:, y4_at + W4 * s:y4_at + W4 * (s + 1)].rearrange("p (k n) -> p k n", k=NH - 1) for s in range(2)]
        assert y4_at + 2 * W4 <= WORK
        h4 = [work[:, raw_at + D * s:raw_at + D * (s + 1)] for s in range(2)]
        o4 = [work[:, D * s:D * (s + 1)] for s in range(2)]
        g_final = work[:, 2 * D:3 * D]
        HALF = D // 2
        BANK4 = (3, 1)

        ident = sb("ident", [P, P], F32)
        ones = sb("ones", [P, P], F32)
        mask_q = sb("mask_q", [P, P], BF16)
        mask_k = sb("mask_k", [P, HD + LP - L], BF16)
        gain_rows = work[:, misc_at + D:misc_at + D + P]
        gains = sb("gains", [P, 8 * KT], F32)
        g_a = gains[:, 0:KT]
        g_kv = gains[:, KT:2 * KT]
        g_b = gains[:, 2 * KT:3 * KT]
        conv_b = gains[:, 3 * KT:4 * KT]
        conv_w = gains[:, 4 * KT:7 * KT].rearrange("p (j k) -> p j k", j=3)
        g_sub = sb("g_sub", [P, 2], F32)
        lam_in = sb("lam_in", [P, 4, HD], F32)
        lam_s = sb("lam_s", [P, 8], F32)
        eps = sb("eps", [P, 1], F32)
        stat = sb("stat", [P, 2, 8], F32)
        end_sq = sb("end_sq", [P, 2], F32)
        neg_max = sb("neg_max", [P, 2, 2], F32)
        z_sum = sb("z_sum", [P, 2, 2], F32)
        z_inv = sb("z_inv", [P, 2, 3], F32)
        ps = ctx.enter_context(nc.psum_tensor("ps", [P, 8, 512], F32))

        def flat(bank, width):
            return ps[:].rearrange("p b n -> p (b n)")[:, bank * 512:bank * 512 + width]

        const_in = sem("const_in")
        lam_loaded = sem("lam_loaded")
        rows_zero = sem("rows_zero")
        gains_mm = sem("gains_mm")
        gains_done = sem("gains_done")
        ident_made = sem("ident_made")
        masks_made = sem("masks_made")
        pads_zero = sem("pads_zero")
        lam_step = sem("lam_step")
        lam_exp = sem("lam_exp")
        lam_done = sem("lam_done")
        x0_in = [sem(f"x0_in{s}") for s in range(X0S)]
        x_in = [sem(f"x_in{s}") for s in range(2)]
        sq_done = sem("sq_done")
        ln_done = sem("ln_done")
        r0_done = sem("r0_done")
        newton = sem("newton")
        xn_done = sem("xn_done")
        tr_done = sem("tr_done")
        xh_done = sem("xh_done")
        xl_done = sem("xl_done")
        raw_in = [sem(f"raw_in{s}") for s in range(2)]
        w_scaled = sem("w_scaled")
        w_hi = sem("w_hi")
        w_lo = sem("w_lo")
        c_done = sem("c_done")
        v_done = sem("v_done")
        conv_step = sem("conv_step")
        b_done = sem("b_done")
        z_done = sem("z_done")
        y_done = sem("y_done")
        o_in = sem("o_in")
        o_hi = sem("o_hi")
        o_lo = sem("o_lo")
        y0_hi = sem("y0_hi")
        y0_lo = sem("y0_lo")
        y_hi = sem("y_hi")
        y_lo = sem("y_lo")
        out_mm = sem("out_mm")
        h1_done = sem("h1_done")
        vpad_zero = sem("vpad_zero")
        v_zero = sem("v_zero")
        h1_stored = [sem(f"h1_stored{s}") for s in range(2)]
        unit_mm = sem("unit_mm")
        chunk_mm = sem("chunk_mm")
        chunk_hi = sem("chunk_hi")
        kq_out = sem("kq_out")
        vz_out = sem("vz_out")
        z_silu = sem("z_silu")
        keys_dup = sem("keys_dup")
        s_mm = sem("s_mm")
        s_out = sem("s_out")
        exp_done = sem("exp_done")
        recip_done = sem("recip_done")
        inv_done = sem("inv_done")
        e1_scaled = sem("e1_scaled")
        attn_done = sem("attn_done")
        round_mm = sem("round_mm")
        round_hi = sem("round_hi")
        round_lo = sem("round_lo")
        pv_mm = sem("pv_mm")
        o_copied = sem("o_copied")
        o_squared = sem("o_squared")
        ms_mm = sem("ms_mm")
        ms_ln = sem("ms_ln")
        r_done = sem("r_done")
        or_done = sem("or_done")
        y_head = sem("y_head")
        y_stored = sem("y_stored")
        wb_in = [sem(f"wb_in{s}") for s in range(NB)]
        wb_hi = sem("wb_hi")
        wb_lo = sem("wb_lo")
        y4_in = [sem(f"y4_in{s}") for s in range(2)]
        h4_in = [sem(f"h4_in{s}") for s in range(2)]
        gf_in = sem("gf_in")
        oz_done = sem("oz_done")
        y4e_hi = sem("y4e_hi")
        y4e_lo = sem("y4e_lo")
        y4_hi = sem("y4_hi")
        y4_lo = sem("y4_lo")
        out4_mm = sem("out4_mm")
        out4_half = sem("out4_half")
        h2_half = sem("h2_half")
        end_sq_done = sem("end_sq_done")
        end_mean = sem("end_mean")
        h2_done = sem("h2_done")
        o4_done = sem("o4_done")
        o4_stored = [sem(f"o4_stored{s}") for s in range(2)]

        U1 = 4 * KT
        UH = 4
        CHUNKS = 10
        CHUNK_OF = {"V": 0, "K": 3, "Q": 6, "Z": 8}
        RH = 18
        RP = 4
        SLOT = {"V": 1, "K": 0, "Q": 1, "Z": 0}

        def rounds_of(i):
            tiles = list(range(1, i + 2)) + [0]
            return [tiles[a:a + 4] for a in range(0, len(tiles), 4)]

        ROUND_AT = [sum(len(rounds_of(a)) for a in range(i)) for i in range(NT)]
        V_ROUNDS = [[1, 2, 3], [4, 5, 6], [7, 8], [0]]
        assert ROUND_AT[-1] + len(rounds_of(NT - 1)) + len(V_ROUNDS) == RH

        def round_bank(n):
            return 5 + n % 2

        def chunk_bank(kind, c):
            return 4 if kind == "V" else 3 + c % 2

        def s_bank(i, c):
            return 2 * c if s_shape(i)[0] <= 2 else 0

        def s_read(h, i, c):
            n = 2 * (NT * h + i) + c
            shares = s_shape(i)[0] == 3 or (c == 0 and s_shape((i - 1) % NT)[0] == 3)
            return n + 1 if shares or (i, c) == (0, 0) else n

        def tr_bank(slot):
            return 6 - 2 * slot

        def s_shape(i):
            n = M + P * (i + 1)
            if n <= 512:
                return 1, n
            if n <= 1024:
                return 2, n // 2
            return 3, CW

        FILL_AT = [None, 2, 3, 4, 5, None, 6, 7, 8, 9, 10, 11, 12, 13, 14, None]
        MS_AT = ((4, 1), (6, 0))
        WB_ORDER = (4, 5, 6, 7, 0, 1, 2, 3)
        WB_AT = [(), (), (0,), (1,), (2, 3), (4, 5), (6, 7), ()]

        def key_col(j):
            return 0 if j == 0 else M + P * (j - 1)

        block = ctx.enter_context(nc.Block())

        @block.sync
        def _(sp):
            def load_x(t, slot, dst, sems):
                if t is None:
                    sp.dma_start(dst[slot][0:M, :], meta_tokens).then_inc(sems[slot], 16)
                    sp.dma_start(dst[slot][M:P, :], x_rows[0:P - M, :]).then_inc(sems[slot], 16)
                else:
                    sp.dma_start(dst[slot], x_rows[bass.ds(t * P, P), :]).then_inc(sems[slot], 16)

            load_x(None, 0, x0, x0_in)
            load_x(0, 1, x0, x0_in)
            load_x(1, 2, x0, x0_in)
            for r, v in enumerate((a_norm_g[0], kv_norm_g, b_norm_g[0], a_conv_b[0])):
                sp.dma_start(gain_rows[KT * r:KT * (r + 1), :], v.rearrange("(k p) -> k p", p=P)).then_inc(const_in, 16)
            sp.dma_start(gain_rows[4 * KT:7 * KT, :],
                         a_conv_w[0].rearrange("j (k p) -> (j k) p", p=P)).then_inc(const_in, 16)
            sp.dma_start(gain_rows[7 * KT:8 * KT, :], b_subln_g[0:1, :].to_broadcast([KT, P])).then_inc(const_in, 16)

            def load_unit(u, slot, w, col):
                sp.wait_ge(w_hi, u - 1)
                sp.wait_ge(w_lo, u - 1)
                sp.dma_start(raw[slot], w[:, :, bass.ds(col, P)]).then_inc(raw_in[slot], 16)

            ORDER = (1, 2, 0, 3)
            for t in range(3, NT + 1):
                if t == 4:
                    sp.dma_start(raw[0], w_in_a[:, :, ORDER[0] * D:ORDER[0] * D + P]).then_inc(raw_in[0], 16)
                if t >= X0S:
                    sp.wait_ge(tr_done, t - X0S + 1)
                load_x(t - 1, t % X0S, x0, x0_in)
            sp.dma_start(raw[1], w_in_a[:, :, ORDER[1] * D:ORDER[1] * D + P]).then_inc(raw_in[1], 16)
            for j, v in enumerate((b_lambda_q1, b_lambda_k1, b_lambda_q2, b_lambda_k2)):
                sp.dma_start(lam_in[:, j, :], v[0:1, :].to_broadcast([P, HD])).then_inc(lam_loaded, 16)
            sp.dma_start(raw_o, w_out_a[:, :, 0:P]).then_inc(o_in, 16)
            for n in (2, 3):
                load_unit(n, n % 2, w_in_a, ORDER[n] * D)
            with sp.Fori(1, KT) as f:
                sp.wait_ge(o_hi, f)
                sp.wait_ge(o_lo, f)
                sp.dma_start(raw_o, w_out_a[:, :, bass.ds(f * P, P)]).then_inc(o_in, 16)
                for n in range(4):
                    load_unit(4 * f + n, n % 2, w_in_a, f * P + ORDER[n] * D)

            sp.wait_ge(o_hi, KT)
            sp.wait_ge(o_lo, KT)
            sp.wait_ge(y_done, KT)
            load_x(None, 0, xt, x_in)
            load_x(0, 1, xt, x_in)
            def load_head_unit(u, kind, h, ahead=0):
                slot = SLOT[kind]
                w, col = {"V": (w_kv_v, D), "K": (w_kv_v, 0), "Q": (w_in_b, 0), "Z": (w_in_b, D)}[kind]
                load_unit(u, slot, w, h * P + (col + ahead * P))

            sp.wait_ge(w_hi, U1)
            sp.wait_ge(w_lo, U1)
            load_head_unit(U1, "V", 0)
            sp.dma_start(raw[SLOT["K"]], w_kv_v[:, :, 0:P]).then_inc(raw_in[SLOT["K"]], 16)

            def store_h1(t, slot, stored=None):
                sp.wait_ge(h1_done, t + 1)
                sp.dma_start(h1_dram[bass.ds((t - 1) * P, P), :],
                             ht[slot]).then_inc(h1_stored[slot] if stored is None else stored, 16)

            def step2(t, slot):
                sp.wait_ge(tr_done, NT + 1 + t)
                load_x(t, 1 - slot, xt, x_in)
                store_h1(t, slot)

            with sp.Fori(0, (NT - 2) // 2) as i:
                step2(2 * i + 1, 1)
                step2(2 * i + 2, 0)
            step2(NT - 1, 1)
            store_h1(NT, 0, y_stored)

            def dup_keys(h):
                sp.wait_ge(kq_out, 5 * h + 3)
                sp.dma_start(keys[0][HD:P].bitcast(F32), keys[0][0:HD].bitcast(F32)).then_inc(keys_dup, 16)
                sp.dma_start(keys[1][0:HD].bitcast(F32), keys[1][HD:P].bitcast(F32)).then_inc(keys_dup, 16)

            load_head_unit(U1 + 2, "Q", 0)
            load_head_unit(U1 + 3, "Z", 0)

            def store_y(h):
                sp.wait_ge(y_head, h + 2)
                sp.dma_start(y_dram[:, bass.ds(h, 1), :], y_o.rearrange("p (a n) -> p a n", a=1)).then_inc(y_stored, 16)

            def head(h, ahead):
                u = U1 + 4 + UH * h
                load_head_unit(u + 2, "Q", h + 1)
                load_head_unit(u + 3, "Z", h + 1)
                if ahead:
                    load_head_unit(u + 4, "V", h + 1, 1)
                dup_keys(h + 1)
                store_y(h)
                if ahead:
                    load_head_unit(u + 5, "K", h + 1, 1)

            load_head_unit(U1 + 4, "V", 1)
            dup_keys(0)
            load_head_unit(U1 + 5, "K", 1)
            with sp.Fori(0, NH - 2) as h:
                head(h, True)
            head(NH - 2, False)

            def load_y4(t, slot):
                sp.dma_start(y4[slot], y_dram[:, :, bass.ds(t * P, P)]).then_inc(y4_in[slot], 16)

            def load_h4(t, slot):
                sp.dma_start(h4[slot], h1_dram[bass.ds(t * P, P), :]).then_inc(h4_in[slot], 16)

            def store4(t, slot):
                sp.wait_ge(o4_done, t + 1)
                sp.dma_start(out_rows[bass.ds(t * P, P), :], o4[slot]).then_inc(o4_stored[slot], 16)

            sp.wait_ge(y_stored, 16 * NH)
            load_y4(0, 0)
            load_y4(1, 1)
            UL = U1 + 4 + UH * (NH - 1)
            sp.wait_ge(w_hi, UL)
            sp.wait_ge(w_lo, UL)
            for n, j in enumerate(WB_ORDER):
                if n >= NB:
                    sp.wait_ge(wb_lo, n - NB + 1)
                elif n == 2:
                    sp.wait_ge(round_mm, RP + RH * (NH - 1))
                sp.dma_start(raw_b[n % NB], w_out_b[:, :, j * P:(j + 1) * P]).then_inc(wb_in[n % NB], 16)
            sp.wait_ge(y4e_lo, 2)
            for s in range(2):
                load_y4(2 + s, s)
            for s in range(2):
                sp.wait_ge(h1_stored[s], 16 * (NT // 2 - 1 + s))
                sp.wait_ge(wb_lo, KT - 1 + s)
                load_h4(s, s)
            sp.wait_ge(y_head, NH + 1)
            sp.dma_start(g_final, final_norm_g.rearrange("(a n) -> a n", a=1).to_broadcast([P, D])).then_inc(gf_in, 16)
            with sp.Fori(0, NT // 2 - 2) as i:
                for s in range(2):
                    t = 2 * i + s
                    sp.wait_ge(y4_lo, t + 3)
                    load_y4(t + 4, s)
                    store4(t, s)
                    load_h4(t + 2, s)
            for s in range(2):
                store4(NT - 4 + s, s)
                load_h4(NT - 2 + s, s)
            store4(NT - 2, 0)
            for c in range(2):
                sp.wait_ge(o4_done, NT + c)
                sp.dma_start(out_rows[(NT - 1) * P:NT * P, HALF * c:HALF * (c + 1)],
                             o4[1][:, HALF * c:HALF * (c + 1)]).then_inc(o4_stored[1], 16)
            for s in range(2):
                sp.wait_ge(o4_stored[s], 16 * (NT // 2 + s))

        @block.gpsimd
        def _(pool):
            nc.gpsimd.memset(ident[:], 0.0).then_inc(ident_made, 1)
            nc.gpsimd.memset(ones[:], 1.0).then_inc(ident_made, 1)
            nc.gpsimd.memset(eps[:], EPS).then_inc(ident_made, 1)
            pool.wait_ge(ident_made, 3)
            nc.gpsimd.affine_select(out=ident[:], in_=ident[:], compare_op=ALU.not_equal, fill=1.0, base=0,
                                    pattern=[[-1, P]], channel_multiplier=1).then_inc(ident_made, 1)
            pool.wait_ge(ident_made, 4)
            nc.gpsimd.memset(gain_rows[8 * KT:P, :], 0.0).then_inc(rows_zero, 1)
            pool.wait_ge(rows_zero, 1)
            nc.gpsimd.memset(X_hi[:, :, L:LP].bitcast(F32), 0.0).then_inc(pads_zero, 1)
            nc.gpsimd.memset(X_lo[:, :, L:LP].bitcast(F32), 0.0).then_inc(pads_zero, 1)
            nc.gpsimd.memset(mask_q[:], 0.0).then_inc(masks_made, 1)
            nc.gpsimd.memset(mask_k[:], 0.0).then_inc(masks_made, 1)
            pool.wait_ge(masks_made, 2)
            for n, (rows, value) in enumerate((
                    (mask_q[0:2, :], 1.0), (mask_k[0:2, HD:], MASKED), (mask_q[0:1, HD:P], 0.0),
                    (mask_k[0:1, 0:HD], MASKED), (mask_k[0:1, HD:], 0.0))):
                nc.gpsimd.memset(rows, value).then_inc(masks_made, 1)
                pool.wait_ge(masks_made, n + 3)

            def scale_unit(u, slot, count, g):
                pool.wait_ge(raw_in[slot], count)
                nc.gpsimd.tensor_tensor(raw[slot], raw[slot], g.unsqueeze(2).to_broadcast([P, KT, P]),
                                        ALU.mult).then_inc(w_scaled, 1)

            pool.wait_ge(gains_done, 1)
            with pool.Fori(0, KT) as f:
                for n in range(4):
                    scale_unit(4 * f + n, n % 2, 32 * f + 16 * (n // 2 + 1), g_a)
            R1 = 16 * (U1 // 2)
            scale_unit(U1, 1, R1 + 16, g_kv)
            scale_unit(U1 + 1, 0, R1 + 16, g_kv)
            scale_unit(U1 + 2, 1, R1 + 32, g_b)
            scale_unit(U1 + 3, 0, R1 + 32, g_b)

            def scale_e1(h, i):
                pool.wait_ge(inv_done, NT * h + i + 1)
                nb, w = s_shape(i)
                e1 = E[i % 2][1][:, 0:nb * w]
                nc.gpsimd.tensor_tensor(e1, e1, z_inv[:, i % 2, 2:3].to_broadcast([P, nb * w]),
                                        ALU.mult).then_inc(e1_scaled, 1)

            def head(h, last):
                for i in range(NT):
                    if not last:
                        u = U1 + 4 + UH * h
                        at = R1 + 32 + 32 * h
                        if i == 0:
                            scale_unit(u, 1, at + 16, g_kv)
                        if i == 2:
                            scale_unit(u + 1, 0, at + 16, g_kv)
                        if i == 5:
                            scale_unit(u + 2, 1, at + 32, g_b)
                        if i == 7:
                            scale_unit(u + 3, 0, at + 32, g_b)
                    if not last:
                        scale_e1(h, i)
                    if last and i in (1, 2):
                        pool.wait_ge(y4e_hi, i)
                        nc.gpsimd.tensor_tensor(ring[:, 2 - i, 1, 0:NH - 1], y4[2 - i], ring[:, 2 - i, 0, 0:NH - 1],
                                                ALU.subtract).then_inc(y4e_lo, 1)
                    for n in WB_AT[i] if last else ():
                        j = WB_ORDER[n]
                        pool.wait_ge(wb_hi, n + 1)
                        nc.gpsimd.tensor_tensor(X_lo[:, :, j * P:(j + 1) * P], raw_b[n % NB], X_hi[:, :, j * P:(j + 1) * P],
                                                ALU.subtract).then_inc(wb_lo, 1)
                if not last:
                    pool.wait_ge(r_done, h + 1)
                    nc.gpsimd.tensor_tensor(o_t, o_t, r_o, ALU.mult).then_inc(or_done, 1)

            with pool.Fori(0, NH - 1) as h:
                head(h, False)
            head(NH - 1, True)

        @block.scalar
        def _(act):
            def unit_hi(u, slot, sem_used, used):
                act.wait_ge(w_scaled, u + 1)
                if used is not None:
                    act.wait_ge(sem_used, used)
                nc.scalar.activation(ring[:, slot, 0], raw[slot], ACT.Copy).then_inc(w_hi, 1)

            def stats(n, slot, src, squares=None, offset=None):
                s = stat[:, slot]
                nc.scalar.activation(flat(tr_bank(slot), D) if squares is None else squares, src, ACT.Square,
                                     accum_out=s[:, 0:1]).then_inc(sq_done, 1)
                act.wait_ge(sq_done, n + 1)
                nc.scalar.activation(s[:, 2:3], s[:, 0:1], ACT.Ln, bias=eps[:] if offset is None else offset,
                                     scale=1.0 / D).then_inc(ln_done, 1)
                act.wait_ge(ln_done, n + 1)
                nc.scalar.activation(s[:, 3:4], s[:, 2:3], ACT.Exp, scale=-0.5).then_inc(r0_done, 1)

            def x_hi(n, slot, col, width):
                act.wait_ge(tr_done, n + 1)
                nc.scalar.activation(X_hi[:, :, bass.ds(col, width)],
                                     flat(tr_bank(slot), D).rearrange("p (k n) -> p k n", k=KT)[:, :, 0:width],
                                     ACT.Copy).then_inc(xh_done, 1)

            nc.scalar.preload_act_table_set("natural_log_exp_and_others")
            act.wait_ge(ident_made, 3)
            for t in range(NT + 1):
                act.wait_ge(x0_in[t % X0S], 32 + 16 * (t // X0S) if t % X0S == 0 else 16 * (t // X0S + 1))
                if t >= 2:
                    act.wait_ge(xn_done, t - 1)
                stats(t, t % 2, x0[t % X0S], squares0)
                if t >= 2:
                    x_hi(t - 2, t % 2, key_col(t - 2), M if t == 2 else P)
                if t == 3:
                    act.wait_ge(gains_mm, 1)
                    nc.scalar.activation(gains[:], ps[:, 3, 0:8 * KT], ACT.Copy).then_inc(gains_done, 1)
                if t == 5:
                    unit_hi(0, 0, None, None)
            for t in (NT - 1, NT):
                x_hi(t, t % 2, key_col(t), P)
            unit_hi(1, 1, None, None)
            act.wait_ge(lam_step, 4)
            nc.scalar.activation(lam_s[:, 2:4], lam_s[:, 0:2], ACT.Exp).then_inc(lam_exp, 1)

            nc.scalar.preload_act_table_set("silu_and_others")

            def feature(f, first=False, last=False):
                if not first:
                    unit_hi(4 * f + 1, 1, unit_mm, 4 * f)
                act.wait_ge(unit_mm, 4 * f + 1)
                if not first:
                    act.wait_ge(y_done, f)
                nc.scalar.activation(cz.rearrange("p (b n) -> p b n", b=3), ps[:, 0:3, 0:CW], ACT.Copy).then_inc(c_done, 1)
                unit_hi(4 * f + 2, 0, unit_mm, 4 * f + 1)
                act.wait_ge(o_in, 16 * f + 16)
                nc.scalar.activation(wo_hi[:, :, bass.ds(f * P, P)], raw_o, ACT.Copy).then_inc(o_hi, 1)
                unit_hi(4 * f + 3, 1, unit_mm, 4 * f + 2)
                if not last:
                    unit_hi(4 * f + 4, 0, unit_mm, 4 * f + 3)
                else:
                    act.wait_ge(y_done, KT - 1)
                    act.wait_ge(unit_mm, U1 - 1)
                    nc.scalar.activation(ring[:, 0, 0, 0:KT - 1], Y[:, 0:KT - 1, 0:P], ACT.Copy).then_inc(y0_hi, 1)
                act.wait_ge(unit_mm, 4 * f + 4)
                act.wait_ge(v_done, f + 1)
                nc.scalar.activation(cz.rearrange("p (b n) -> p b n", b=3), ps[:, 3:6, 0:CW], ACT.Silu).then_inc(z_done, 1)

            feature(0, first=True)
            with act.Fori(1, KT - 1) as f:
                feature(f)
            feature(KT - 1, last=True)


            def y_tile_hi(t, slot, col):
                act.wait_ge(y_done, KT)
                nc.scalar.activation(ring[:, slot, 0], Y[:, :, bass.ds(col, P)], ACT.Copy).then_inc(y_hi, 1)

            N2 = NT + 1

            def step2(t, par, nxt=True, prev=True, prev2=True, meta2=False):
                if nxt:
                    act.wait_ge(out_mm, t)
                    y_tile_hi(t + 1, 1 - par, M + t * P)
                if prev2:
                    x_hi(N2 + t - 2, par, 0 if meta2 else M + (t - 3) * P, M if meta2 else P)
                if prev:
                    act.wait_ge(h1_done, t)
                    act.wait_ge(xn_done, N2 + t - 2)
                    act.wait_ge(xl_done, N2 + t - 2)
                    stats(N2 + t - 1, 1 - par, ht[1 - par])

            act.wait_ge(y_done, KT)
            nc.scalar.activation(ring[:, 0, 0, KT - 1], Y[:, KT - 1, 0:P], ACT.Copy).then_inc(y_hi, 1)
            y_tile_hi(1, 1, M)
            nc.scalar.preload_act_table_set("natural_log_exp_and_others")
            step2(1, 1, prev2=False)
            step2(2, 0, meta2=True)
            with act.Fori(0, (NT - 4) // 2) as i:
                step2(2 * i + 3, 1)
                step2(2 * i + 4, 0)
            step2(NT - 1, 1)
            unit_hi(U1, SLOT["V"], out_mm, NT)
            step2(NT, 0, nxt=False)
            step2(NT + 1, 1, nxt=False)
            unit_hi(U1 + 1, SLOT["K"], out_mm, NT + 1)
            x_hi(N2 + NT, 0, M + (NT - 1) * P, P)

            def chunk(kind, h, c, bank=None, count=None):
                act.wait_ge(chunk_mm, CHUNKS * h + CHUNK_OF[kind] + c + 1 if count is None else count)
                return ps[:, chunk_bank(kind, c) if bank is None else bank, 0:CW if kind in "VK" else QW]

            def v_chunk(h, c, bank=None, count=None):
                b = chunk("V", h, c, bank, count)
                nc.scalar.activation(v_t[:, CW * c:CW * (c + 1)], b, ACT.Copy).then_inc(vz_out, 1)

            def k_chunk_hi(h, c, scores=None, count=None):
                b = chunk("K", h, c, None, count)
                if scores is not None:
                    act.wait_ge(s_mm, scores)
                nc.scalar.activation(keys[0][0:HD, 0, CW * c:CW * (c + 1)], b[0:HD], ACT.Copy)
                nc.scalar.activation(keys[1][HD:P, 0, CW * c:CW * (c + 1)], b[HD:P], ACT.Copy).then_inc(chunk_hi, 1)

            def q_chunk_hi(h, c):
                b = chunk("Q", h, c)
                nc.scalar.activation(queries[0][0:HD, QW * c:QW * (c + 1)], b[0:HD], ACT.Copy)
                nc.scalar.activation(queries[1][HD:P, QW * c:QW * (c + 1)], b[HD:P], ACT.Copy).then_inc(chunk_hi, 1)

            def z_copy(h):
                act.wait_ge(y_head, h + 1)
                act.wait_ge(chunk_mm, CHUNKS * h + CHUNK_OF["Z"] + 2)
                nc.scalar.activation(z_act.rearrange("p (c n) -> p c n", c=2), ps[:, 3:5, :], ACT.Copy).then_inc(vz_out, 1)

            def round_hi_v(n, par, tiles, pvs):
                act.wait_ge(round_mm, n + 1)
                if pvs is not None:
                    act.wait_ge(pv_mm, pvs)
                b = ps[:, round_bank(par), 0:P * len(tiles)]
                if tiles == [0]:
                    nc.scalar.activation(V[0:M, 0, 0, :], b[0:M], ACT.Copy).then_inc(round_hi, 1)
                else:
                    nc.scalar.activation(V[:, 0, tiles[0]:tiles[-1] + 1, :], b.rearrange("p (j v) -> p j v", v=P),
                                         ACT.Copy).then_inc(round_hi, 1)

            def round_hi_a(n, par, tiles, i, pvs):
                act.wait_ge(round_mm, n + 1)
                if pvs is not None:
                    act.wait_ge(pv_mm, pvs)
                b = ps[:, round_bank(par), 0:P * len(tiles)].rearrange("p (j q) -> p j q", q=P)
                half = i % 2
                qs = slice(P * half, P * half + P)
                full = [j for j in tiles if j]
                last = None
                if half and i + 1 in full:
                    full = full[:-1]
                    last = nc.scalar.activation(attn_d[:, 0, P:2 * P], b[:, len(full)], ACT.Copy)
                if full:
                    last = nc.scalar.activation(attn_t[:, 0, full[0]:full[-1] + 1, qs], b[:, 0:len(full)], ACT.Copy)
                if 0 in tiles:
                    last = nc.scalar.activation(attn_t[:, 0, 0:1, qs], b[:, len(tiles) - 1:len(tiles)], ACT.Copy)
                last.then_inc(round_hi, 1)

            def exp(h, i, c):
                n = 2 * (NT * h + i) + c
                act.wait_ge(s_out, n + 2)
                nb, w = s_shape(i)
                e = E[i % 2][c][:, 0:nb * w]
                nc.scalar.activation(e, e, ACT.Exp, bias=neg_max[:, i % 2, c:c + 1], scale=-1.0,
                                     accum_out=z_sum[:, i % 2, c:c + 1]).then_inc(exp_done, 1)

            def o_group(h, g):
                act.wait_ge(pv_mm, 4 * h + g + 1)
                nc.scalar.activation(o_t[:, 2 * P * g:2 * P * (g + 1)], ps[:, 7, 0:2 * P], ACT.Copy).then_inc(o_copied, 1)
                nc.scalar.activation(o_sq, ps[:, 7, 0:2 * P], ACT.Square).then_inc(o_squared, 1)

            def ln_group(h, g):
                act.wait_ge(ms_mm, 4 * h + g + 1)
                nc.scalar.activation(r_o[:, 2 * P * g:2 * P * (g + 1)], ps[:, 7, 0:2 * P], ACT.Ln, bias=eps[:],
                                     scale=1.0 / P).then_inc(ms_ln, 1)

            v_chunk(0, 0, 3, 1)
            v_chunk(0, 1, None, 2)
            k_chunk_hi(0, 0, None, 3)
            v_chunk(0, 2, None, 4)
            unit_hi(U1 + 2, SLOT["Q"], chunk_mm, 4)
            k_chunk_hi(0, 2, None, 5)
            k_chunk_hi(0, 1, None, 6)
            for r, tiles in enumerate(V_ROUNDS):
                round_hi_v(r, r, tiles, None)
            unit_hi(U1 + 3, SLOT["Z"], chunk_mm, 6)
            for c in range(2):
                q_chunk_hi(0, c)

            def wb_unit_hi(n):
                j = WB_ORDER[n]
                act.wait_ge(wb_in[n % NB], 16 * (n // NB + 1))
                act.wait_ge(chunk_mm, CHUNKS * NH)
                nc.scalar.activation(X_hi[:, :, j * P:(j + 1) * P], raw_b[n % NB], ACT.Copy).then_inc(wb_hi, 1)

            def y4_hi_heads(t, slot, done=None):
                act.wait_ge(y4_in[slot], (t // 2 + 1) * 16)
                ins = nc.scalar.activation(ring[:, slot, 0, 0:NH - 1], y4[slot], ACT.Copy)
                if done is not None:
                    ins.then_inc(done, 1)

            def y4_hi_last(t, slot):
                nc.scalar.activation(ring[:, slot, 0, NH - 1], y_o[:, t * P:(t + 1) * P], ACT.Copy).then_inc(y4_hi, 1)

            def silu(h):
                act.wait_ge(vz_out, 4 * h + 4)
                nc.scalar.activation(z_act, z_act, ACT.Silu).then_inc(z_silu, 1)
                nc.scalar.preload_act_table_set("natural_log_exp_and_others")

            def head(h, last):
                R0 = RP + RH * h
                u = U1 + 4 + UH * h
                for i in range(NT):
                    if not last and i == 4:
                        v_chunk(h + 1, 0)
                    if i == 2:
                        z_copy(h)
                    exp(h, i, 0)
                    if not last:
                        if i == 3:
                            unit_hi(u + 1, SLOT["K"], chunk_mm, CHUNKS * h + 10)
                        if i == 5:
                            v_chunk(h + 1, 1)
                        if i == 7:
                            v_chunk(h + 1, 2)
                    if (i, 0) in MS_AT:
                        ln_group(h, (i - 4) // 2)
                    exp(h, i, 1)
                    if (i, 1) in MS_AT:
                        ln_group(h, (i - 4) // 2)
                    if i >= 1:
                        attn_rounds(h, i - 1, R0)
                    if i >= 3 and i % 2 == 1:
                        o_group(h, (i - 3) // 2)
                    if not last:
                        if i == 0:
                            unit_hi(u, SLOT["V"], chunk_mm, CHUNKS * h + 8)
                    if last and i in (1, 2):
                        act.wait_ge(chunk_mm, CHUNKS * NH - 2 * (i == 1))
                        y4_hi_heads(2 - i, 2 - i, y4e_hi)
                    for n in WB_AT[i] if last else ():
                        wb_unit_hi(n)
                if not last:
                    unit_hi(u + 2, SLOT["Q"], chunk_mm, CHUNKS * (h + 1) + 3)
                    k_chunk_hi(h + 1, 0, 2 * NT * (h + 1))
                ln_group(h, 2)
                if not last:
                    k_chunk_hi(h + 1, 1)
                attn_round(h, NT - 1, R0, 0)
                attn_round(h, NT - 1, R0, 1)
                attn_round(h, NT - 1, R0, 2)
                if not last:
                    k_chunk_hi(h + 1, 2)
                if last:
                    silu(h)
                o_group(h, 3)
                if not last:
                    for r, tiles in enumerate(V_ROUNDS):
                        round_hi_v(R0 + 14 + r, 14 + r, tiles, 4 * (h + 1))
                        if r == 1:
                            unit_hi(u + 3, SLOT["Z"], chunk_mm, CHUNKS * (h + 1) + 6)
                ln_group(h, 3)
                act.wait_ge(ms_ln, 4 * (h + 1))
                nc.scalar.activation(r_o[:, 0:T], r_o[:, 0:T], ACT.Exp, scale=-0.5).then_inc(r_done, 1)
                if not last:
                    silu(h)
                    q_chunk_hi(h + 1, 0)
                    q_chunk_hi(h + 1, 1)

            def attn_rounds(h, i, R0):
                for r in range(len(rounds_of(i))):
                    attn_round(h, i, R0, r)

            def attn_round(h, i, R0, r):
                n = ROUND_AT[i] + r
                pvs = 4 * h + i // 2 if i % 2 == 0 and i > 0 else None
                round_hi_a(R0 + n, n, rounds_of(i)[r], i, pvs)

            with act.Fori(0, NH - 1) as h:
                head(h, False)
            head(NH - 1, True)

            N4 = 2 * N2
            act.wait_ge(y_head, NH + 1)
            for t in range(2):
                y4_hi_last(t, t)
            for t in range(NT):
                if t + 2 < NT:
                    act.wait_ge(out4_mm, t + 1)
                    y4_hi_heads(t + 2, t % 2)
                    y4_hi_last(t + 2, t % 2)
                if t >= 2:
                    act.wait_ge(o4_done, t - 1)
                if t < NT - 1:
                    act.wait_ge(h2_done, t + 1)
                    stats(N4 + t, t % 2, h4[t % 2], flat(5, D))
            act.wait_ge(h2_half, 1)
            nc.scalar.activation(ps[:, 5, :], h4[1][:, 0:HALF], ACT.Square, accum_out=end_sq[:, 0:1]).then_inc(end_sq_done, 1)
            act.wait_ge(h2_done, NT)
            act.wait_ge(end_mean, 1)
            stats(N4 + NT - 1, 1, h4[1][:, HALF:D], ps[:, 6, :], end_sq[:, 1:2])

        @block.tensor
        def _(pe):
            N2 = NT + 1

            def three(out_ap, wh, wl, xh, xl, start, stop):
                pe.matmul(out_ap, wh, xh, start=start, stop=False)
                pe.matmul(out_ap, wh, xl, start=False, stop=False)
                return pe.matmul(out_ap, wl, xh, start=False, stop=stop)

            def transpose_tile(n, slot, src, reused=True):
                pe.wait_ge(xn_done, n + 1)
                if reused:
                    pe.wait_ge(xh_done, n - 1)
                    pe.wait_ge(xl_done, n - 1)
                for k in range(KT):
                    mm = pe.transpose(ps[:, tr_bank(slot) + k // 4, P * (k % 4):P * (k % 4) + P],
                                      src[:, k * P:(k + 1) * P], ident[:])
                mm.then_inc(tr_done, 1)

            pe.wait_ge(ident_made, 4)
            def unit_part(slot, bank, c, k0=0, k1=KT):
                for k in range(k0, k1):
                    mm = three(ps[:, bank + c, 0:CW], ring[:, slot, 0, k], ring[:, slot, 1, k],
                               X_hi[:, k, CW * c:CW * (c + 1)], X_lo[:, k, CW * c:CW * (c + 1)],
                               k == 0, k == KT - 1)
                return mm

            for t in range(NT + 1):
                transpose_tile(t, t % 2, x0[t % X0S], reused=t >= 2)
                if t == 2:
                    pe.wait_ge(const_in, 16 * 6)
                    pe.wait_ge(rows_zero, 1)
                    pe.transpose(ps[:, 3, 0:P], gain_rows, ident[:]).then_inc(gains_mm, 1)
                if t == 5:
                    pe.wait_ge(xl_done, 4)
                    pe.wait_ge(w_lo, 1)
                    unit_part(0, 0, 0, 0, 3)
                if t == 6:
                    unit_part(0, 0, 0, 3, 6)
                if t == 7:
                    unit_part(0, 0, 0, 6, KT)
            pe.wait_ge(xl_done, 7)
            unit_part(0, 0, 1)
            pe.wait_ge(pads_zero, 2)
            pe.wait_ge(xl_done, NT + 1)
            unit_part(0, 0, 2).then_inc(unit_mm, 1)

            def unit(u, slot, bank, read=None, count=0):
                pe.wait_ge(w_lo, u + 1)
                if read is not None:
                    pe.wait_ge(read, count)
                for c in range(3):
                    mm = unit_part(slot, bank, c)
                mm.then_inc(unit_mm, 1)

            def second_half(f):
                unit(4 * f + 2, 0, 0, c_done, f + 1)
                unit(4 * f + 3, 1, 3, v_done, f + 1)

            pe.wait_ge(gains_done, 1)
            unit(1, 1, 3)
            with pe.Fori(0, KT - 1) as f:
                second_half(f)
                unit(4 * f + 4, 0, 0, b_done, f + 1)
                unit(4 * f + 5, 1, 3, z_done, f + 1)
            second_half(KT - 1)

            def out_tile(t, slot, hi_sem, lo_sem, wh, wl, read, count, done, early=None):
                if early is not None:
                    pe.wait_ge(early[0], 1)
                    pe.wait_ge(early[1], 1)
                if count is not None:
                    pe.wait_ge(read, count)
                for c in range(2):
                    for k in range(KT):
                        if c == 0 and k == (0 if early is None else KT - 1):
                            pe.wait_ge(hi_sem, t + 1)
                            pe.wait_ge(lo_sem, t + 1)
                        mm = three(ps[:, 2 * slot + c, :], ring[:, slot, 0, k], ring[:, slot, 1, k],
                                   wh[:, k, 512 * c:512 * (c + 1)], wl[:, k, 512 * c:512 * (c + 1)],
                                   k == 0, k == KT - 1)
                mm.then_inc(done, 1)

            def out2(t, slot, count, early=None):
                out_tile(t, slot, y_hi, y_lo, wo_hi, wo_lo, h1_done, count, out_mm, early)

            pe.wait_ge(o_hi, KT)
            pe.wait_ge(o_lo, KT)
            pe.wait_ge(b_done, KT)
            out2(0, 0, None, (y0_hi, y0_lo))
            pe.wait_ge(z_done, KT)
            out2(1, 1, None)
            transpose_tile(N2, 0, xt[0])
            with pe.Fori(0, (NT - 2) // 2) as i:
                t = 2 * i + 2
                out2(t, 0, t - 1)
                transpose_tile(N2 + t - 1, 1, xt[1])
                out2(t + 1, 1, t)
                transpose_tile(N2 + t, 0, xt[0])
            out2(NT, 0, NT - 1)
            transpose_tile(N2 + NT - 1, 1, xt[1])

            def chunk(kind, h, c, read=None, count=0, k0=0, k1=KT, bank=None):
                slot = SLOT[kind]
                width, first = (CW, 0) if kind in "VK" else (QW, M)
                if k0 == 0:
                    pe.wait_ge(w_lo, U1 + UH * h + "VKQZ".index(kind) + 1)
                    if read is not None:
                        pe.wait_ge(read, count)
                o = ps[:, chunk_bank(kind, c) if bank is None else bank, 0:width]
                for k in range(k0, k1):
                    cols = slice(first + width * c, first + width * (c + 1))
                    mm = three(o, ring[:, slot, 0, k], ring[:, slot, 1, k], X_hi[:, k, cols], X_lo[:, k, cols],
                               k == 0, k == KT - 1)
                if k1 == KT:
                    mm.then_inc(chunk_mm, 1)

            def v_rounds(h, n0, rounds=range(len(V_ROUNDS))):
                pe.wait_ge(vz_out, 4 * h + 3)
                for r, tiles in [(r, V_ROUNDS[r]) for r in rounds]:
                    if n0 is not None:
                        pe.wait_ge(round_hi, n0 + r - 1)
                        pe.wait_ge(round_lo, n0 + r - 1)
                    elif r >= 2:
                        pe.wait_ge(round_hi, r - 1)
                        pe.wait_ge(round_lo, r - 1)
                    for q, j in enumerate(tiles):
                        mm = pe.transpose(ps[:, round_bank(r), P * q:P * (q + 1)],
                                          v_t[:, key_col(j):key_col(j) + P], ident[:])
                    mm.then_inc(round_mm, 1)

            pe.wait_ge(h1_done, NT)
            chunk("V", 0, 0, bank=3)
            pe.wait_ge(xh_done, N2 + NT)
            pe.wait_ge(xl_done, N2 + NT)
            chunk("V", 0, 1)
            transpose_tile(N2 + NT, 0, xt[0])
            chunk("K", 0, 0, vz_out, 1)
            pe.wait_ge(xh_done, N2 + NT + 1)
            pe.wait_ge(xl_done, N2 + NT + 1)
            chunk("V", 0, 2, vz_out, 2)
            chunk("K", 0, 2, kq_out, 1)
            chunk("K", 0, 1, vz_out, 3)
            v_rounds(0, None, (0, 1))
            chunk("Q", 0, 0, kq_out, 2, 0, 3)
            v_rounds(0, None, (2, 3))
            chunk("Q", 0, 0, k0=3)
            chunk("Q", 0, 1, kq_out, 3)

            def scores(h, i, c):
                pe.wait_ge(s_out, s_read(h, i, c))
                nb, w = s_shape(i)
                q = queries[c][:, P * i:P * (i + 1)]
                bank = s_bank(i, c)
                wide = max(w, 256)
                for b in range(nb):
                    o = ps[:, bank + b, 0:wide]
                    pe.matmul(o, q, keys[c][:, 0, b * w:b * w + wide], start=True, stop=False)
                    pe.matmul(o, q, keys[c][:, 1, b * w:b * w + wide], start=False, stop=b < nb - 1)
                hidden = HD + (nb * w - (M + P * (i + 1)))
                pe.matmul(ps[:, bank + nb - 1, w - hidden:w], mask_q[:], mask_k[:, 0:hidden], start=False,
                          stop=True).then_inc(s_mm, 1)

            def attn_rounds(h, i, rounds=None):
                pe.wait_ge(attn_done, NT * h + i + 1)
                for r in range(len(rounds_of(i))) if rounds is None else rounds:
                    tiles = rounds_of(i)[r]
                    n = ROUND_AT[i] + r
                    pe.wait_ge(round_hi, RP + RH * h + n - 1)
                    pe.wait_ge(round_lo, RP + RH * h + n - 1)
                    for q, j in enumerate(tiles):
                        mm = pe.transpose(ps[:, round_bank(n), P * q:P * (q + 1)],
                                          E[i % 2][0][:, key_col(j):key_col(j) + P], ident[:])
                    mm.then_inc(round_mm, 1)

            def products(h, g):
                n = RP + RH * h + ROUND_AT[2 * g + 1] + len(rounds_of(2 * g + 1))
                pe.wait_ge(round_hi, n)
                pe.wait_ge(round_lo, n)
                if g:
                    pe.wait_ge(ms_ln, 4 * h + g)
                for j in range(2 * g + 3):
                    hi, lo = (attn_t[:, part, j] if j < 2 * g + 2 else attn_d[:, part] for part in range(2))
                    mm = three(ps[:, 7, 0:2 * P], V[:, 0, j], V[:, 1, j], hi, lo, j == 0, j == 2 * g + 2)
                mm.then_inc(pv_mm, 1)

            def mean_squares(h, g):
                pe.wait_ge(o_squared, 4 * h + g + 1)
                pe.matmul(ps[:, 7, 0:2 * P], ones[:], o_sq, start=True, stop=True).then_inc(ms_mm, 1)

            PARTS = ((0, 3), (3, 6), (6, KT))

            def out4_part(t, c, k0, k1):
                slot = t % 2
                if k0 == 0 and t < 2:
                    pe.wait_ge(y4e_lo, 2)
                    pe.wait_ge(wb_lo, 4 if c else KT)
                for k in range(k0, k1):
                    mm = three(ps[:, BANK4[slot] + c, :], ring[:, slot, 0, k], ring[:, slot, 1, k],
                               X_hi[:, k, 512 * c:512 * (c + 1)], X_lo[:, k, 512 * c:512 * (c + 1)], k == 0, k == NH - 1)
                return mm

            def filler(h, p, last):
                k0, k1 = PARTS[p % 3]
                c = p // 3
                if c < 2:
                    chunk("Z", h, c, kq_out, 5 * h + 4 + c, k0, k1)
                elif not last:
                    chunk("V", h + 1, c - 2, vz_out, 4 * h + 4 + c - 2, k0, k1)

            pe.wait_ge(masks_made, 7)
            pe.wait_ge(v_zero, 4)

            def head(h, last):
                filler(h, 0, last)
                filler(h, 1, last)
                pe.wait_ge(keys_dup, 32 * h + 32)
                pe.wait_ge(kq_out, 5 * h + 5)
                for i in range(NT):
                    for c in range(2):
                        if (i, c) == (3, 1):
                            pe.wait_ge(vz_out, 4 * h + 4)
                        scores(h, i, c)
                        p = 2 * i + c
                        if FILL_AT[p] is not None:
                            filler(h, FILL_AT[p], last)
                        if last and 12 <= p < 16:
                            out4_part(0, 1, 2 * (p - 12), min(2 * (p - 12) + 2, NH - 1))
                        if (i, c) in MS_AT:
                            mean_squares(h, (i - 4) // 2)
                        if c == 0 and i == NT - 1:
                            products(h, 2)
                    if 3 <= i < NT - 1 and i % 2 == 1:
                        products(h, (i - 3) // 2)
                    if i >= 1:
                        attn_rounds(h, i - 1)
                if last:
                    pe.wait_ge(s_out, 2 * NT * NH)
                    out4_part(0, 0, 0, NH - 1)
                else:
                    chunk("K", h + 1, 0, s_out, 2 * NT * (h + 1))
                mean_squares(h, 2)
                if not last:
                    chunk("K", h + 1, 1, vz_out, 4 * (h + 1) + 3)
                attn_rounds(h, NT - 1, (0, 1))
                if last:
                    pe.wait_ge(s_out, 2 * NT * NH + 1)
                    out4_part(1, 0, 0, 4)
                else:
                    chunk("K", h + 1, 2, kq_out, 5 * (h + 1) + 1, 0, 4)
                attn_rounds(h, NT - 1, (2,))
                if last:
                    out4_part(1, 0, 4, NH - 1)
                else:
                    chunk("K", h + 1, 2, k0=4)
                if not last:
                    v_rounds(h + 1, RP + RH * h + 14, (0,))
                products(h, 3)
                if last:
                    out4_part(1, 1, 0, 2)
                    mean_squares(h, 3)
                    out4_part(1, 1, 2, NH - 1)
                else:
                    v_rounds(h + 1, RP + RH * h + 14, (1,))
                    chunk("Q", h + 1, 0, kq_out, 5 * (h + 1) + 3, 0, 3)
                    v_rounds(h + 1, RP + RH * h + 14, (2, 3))
                    mean_squares(h, 3)
                    chunk("Q", h + 1, 0, k0=3)
                    chunk("Q", h + 1, 1, kq_out, 5 * (h + 1) + 2)

            with pe.Fori(0, NH - 1) as h:
                head(h, False)
            head(NH - 1, True)

            for t in range(2):
                pe.wait_ge(y4_lo, t + 1)
                for c in range(2):
                    mm = out4_part(t, c, NH - 1, NH)
                mm.then_inc(out4_mm, 1)

            def out4(t, s):
                pe.wait_ge(y4_lo, t + 1)
                pe.wait_ge(h2_done, t - 1)
                out4_part(2 + s, 0, 0, NH).then_inc(out4_half, 1)
                out4_part(2 + s, 1, 0, NH).then_inc(out4_mm, 1)

            with pe.Fori(1, NT // 2) as i:
                for s in range(2):
                    out4(2 * i + s, s)

        @block.vector
        def _(dve):
            N2 = NT + 1
            N4 = 2 * N2

            def unit_lo(u, slot):
                dve.wait_ge(w_hi, u + 1)
                nc.vector.tensor_tensor(ring[:, slot, 1], raw[slot], ring[:, slot, 0], ALU.subtract).then_inc(w_lo, 1)

            def inverse_root(n, slot, offset=EPS):
                s = stat[:, slot]
                dve.wait_ge(r0_done, n + 1)
                nc.vector.tensor_scalar(s[:, 1:2], s[:, 0:1], 1.0 / D, offset, ALU.mult, ALU.add).then_inc(newton, 1)
                dve.wait_ge(newton, 4 * n + 1)
                nc.vector.tensor_scalar(s[:, 4:5], s[:, 3:4], s[:, 3:4], s[:, 1:2], ALU.mult, ALU.mult).then_inc(newton, 1)
                dve.wait_ge(newton, 4 * n + 2)
                nc.vector.tensor_scalar(s[:, 5:6], s[:, 4:5], -0.5, 1.5, ALU.mult, ALU.add).then_inc(newton, 1)
                dve.wait_ge(newton, 4 * n + 3)
                nc.vector.tensor_tensor(s[:, 6:7], s[:, 3:4], s[:, 5:6], ALU.mult).then_inc(newton, 1)
                dve.wait_ge(newton, 4 * n + 4)
                return s[:, 6:7]

            def x_lo(n, slot, col, width):
                dve.wait_ge(xh_done, n + 1)
                nc.vector.tensor_tensor(X_lo[:, :, bass.ds(col, width)],
                                        flat(tr_bank(slot), D).rearrange("p (k n) -> p k n", k=KT)[:, :, 0:width],
                                        X_hi[:, :, bass.ds(col, width)], ALU.subtract).then_inc(xl_done, 1)

            for t in range(NT + 1):
                r = inverse_root(t, t % 2)
                nc.vector.tensor_scalar(x0[t % X0S], x0[t % X0S], r, None, ALU.mult).then_inc(xn_done, 1)
                if t >= 2:
                    x_lo(t - 2, t % 2, key_col(t - 2), M if t == 2 else P)
                if t == 5:
                    unit_lo(0, 0)
            for t in (NT - 1, NT):
                x_lo(t, t % 2, key_col(t), P)
            unit_lo(1, 1)

            dve.wait_ge(lam_loaded, 16 * 4)
            for j in range(2):
                nc.vector.tensor_tensor(lam_in[:, 2 * j], lam_in[:, 2 * j], lam_in[:, 2 * j + 1], ALU.mult).then_inc(lam_step, 1)
            for j in range(2):
                dve.wait_ge(lam_step, j + 1)
                nc.vector.tensor_reduce(lam_s[:, j:j + 1], lam_in[:, 2 * j], AX_X, ALU.add).then_inc(lam_step, 1)
            dve.wait_ge(gains_done, 1)
            nc.vector.tensor_scalar(g_sub[:, 1:2], gains[:, 7 * KT:7 * KT + 1], 1.0 - LAMBDA_INIT, None, ALU.mult).then_inc(lam_step, 1)
            dve.wait_ge(lam_exp, 1)
            nc.vector.tensor_scalar(lam_s[:, 7:8], lam_s[:, 2:3], lam_s[:, 3:4], LAMBDA_INIT, ALU.subtract,
                                    ALU.add).then_inc(lam_done, 1)

            cz3 = cz.rearrange("p (b n) -> p b n", b=3)
            conv3 = conv.rearrange("p (b n) -> p b n", b=3)
            nc.vector.memset(vpad[:, 0:2], 0.0).then_inc(vpad_zero, 1)

            def feature(f, first=False, last=False):
                if not first:
                    unit_lo(4 * f + 1, 1)
                unit_lo(4 * f + 2, 0)
                dve.wait_ge(o_hi, f + 1)
                nc.vector.tensor_tensor(wo_lo[:, :, bass.ds(f * P, P)], raw_o, wo_hi[:, :, bass.ds(f * P, P)],
                                        ALU.subtract).then_inc(o_lo, 1)
                dve.wait_ge(unit_mm, 4 * f + 2)
                dve.wait_ge(c_done, f + 1)
                nc.vector.tensor_tensor(vpad[:, 2:2 + LP].rearrange("p (b n) -> p b n", b=3), ps[:, 3:6, 0:CW], cz3,
                                        ALU.mult).then_inc(v_done, 1)
                dve.wait_ge(v_done, f + 1)
                nc.vector.tensor_scalar(conv, vpad[:, 0:LP], conv_w[:, 0, bass.ds(f, 1)], conv_b[:, bass.ds(f, 1)],
                                        ALU.mult, ALU.add).then_inc(conv_step, 1)
                for j in (1, 2):
                    dve.wait_ge(conv_step, 3 * f + j)
                    nc.vector.scalar_tensor_tensor(out=conv, in0=vpad[:, j:j + LP], scalar=conv_w[:, j, bass.ds(f, 1)],
                                                   in1=conv, op0=ALU.mult, op1=ALU.add).then_inc(conv_step, 1)
                unit_lo(4 * f + 3, 1)
                dve.wait_ge(unit_mm, 4 * f + 3)
                dve.wait_ge(conv_step, 3 * f + 3)
                nc.vector.tensor_tensor(conv3, ps[:, 0:3, 0:CW], conv3, ALU.mult).then_inc(b_done, 1)
                if not last:
                    unit_lo(4 * f + 4, 0)
                else:
                    dve.wait_ge(y0_hi, 1)
                    nc.vector.tensor_tensor(ring[:, 0, 1, 0:KT - 1], Y[:, 0:KT - 1, 0:P], ring[:, 0, 0, 0:KT - 1],
                                            ALU.subtract).then_inc(y0_lo, 1)
                dve.wait_ge(z_done, f + 1)
                dve.wait_ge(b_done, f + 1)
                nc.vector.tensor_tensor(Y[:, bass.ds(f, 1), :], conv.rearrange("p (a n) -> p a n", a=1),
                                        cz.rearrange("p (a n) -> p a n", a=1), ALU.mult).then_inc(y_done, 1)

            dve.wait_ge(vpad_zero, 1)
            feature(0, first=True)
            with dve.Fori(1, KT - 1) as f:
                feature(f)
            feature(KT - 1, last=True)

            def y_tile_lo(t, slot, col):
                dve.wait_ge(y_hi, t + 1)
                dve.wait_ge(y_done, KT)
                nc.vector.tensor_tensor(ring[:, slot, 1], Y[:, :, bass.ds(col, P)], ring[:, slot, 0],
                                        ALU.subtract).then_inc(y_lo, 1)

            def h1_tile(t, slot, x_count, reused=True):
                dve.wait_ge(out_mm, t + 1)
                dve.wait_ge(x_in[slot], x_count)
                if reused:
                    dve.wait_ge(h1_stored[slot], stored_before(t, slot))
                nc.vector.tensor_tensor(ht[slot], flat(2 * slot, D), xt[slot], ALU.add).then_inc(h1_done, 1)

            def stored_before(t, slot):
                return 8 * (t - 2) if slot == 0 else 8 * (t - 1)

            def x2_count(t, slot):
                return 32 + 8 * t if slot == 0 else 8 * (t + 1)

            def step2(t, par, nxt=True, prev=True, prev2=True, first=False, meta2=False):
                if prev:
                    h1_tile(t - 1, 1 - par, x2_count(t - 1, 1 - par), reused=not first)
                if nxt:
                    y_tile_lo(t + 1, 1 - par, M + t * P)
                if prev2:
                    x_lo(N2 + t - 2, par, 0 if meta2 else M + (t - 3) * P, M if meta2 else P)
                if prev:
                    r = inverse_root(N2 + t - 1, 1 - par)
                    nc.vector.tensor_scalar(xt[1 - par], ht[1 - par], r, None, ALU.mult).then_inc(xn_done, 1)

            dve.wait_ge(y_hi, 1)
            dve.wait_ge(y_done, KT)
            nc.vector.tensor_tensor(ring[:, 0, 1, KT - 1], Y[:, KT - 1, 0:P], ring[:, 0, 0, KT - 1],
                                    ALU.subtract).then_inc(y_lo, 1)
            y_tile_lo(1, 1, M)
            step2(1, 1, prev2=False, first=True)
            step2(2, 0, first=True, meta2=True)
            with dve.Fori(0, (NT - 4) // 2) as i:
                step2(2 * i + 3, 1)
                step2(2 * i + 4, 0)
            step2(NT - 1, 1)
            unit_lo(U1, SLOT["V"])
            step2(NT, 0, nxt=False)
            step2(NT + 1, 1, nxt=False)
            unit_lo(U1 + 1, SLOT["K"])
            x_lo(N2 + NT, 0, M + (NT - 1) * P, P)

            def k_chunk_lo(h, c, count=None):
                dve.wait_ge(chunk_hi, 5 * h + c + 1 if count is None else count)
                b = ps[:, chunk_bank("K", c), 0:CW]
                for q, rows in enumerate((slice(0, HD), slice(HD, P))):
                    ins = nc.vector.tensor_tensor(keys[q][rows, 1, CW * c:CW * (c + 1)], b[rows],
                                                  keys[q][rows, 0, CW * c:CW * (c + 1)], ALU.subtract)
                ins.then_inc(kq_out, 1)

            def q_chunk_lo(h, c):
                dve.wait_ge(chunk_hi, 5 * h + 3 + c + 1)
                b = ps[:, chunk_bank("Q", c), :]
                cols = slice(QW * c, QW * (c + 1))
                nc.vector.tensor_tensor(queries[0][HD:P, cols], b[0:HD], queries[0][0:HD, cols], ALU.subtract)
                nc.vector.tensor_tensor(queries[1][0:HD, cols], b[HD:P], queries[1][HD:P, cols],
                                        ALU.subtract).then_inc(kq_out, 1)

            def round_lo_v(n, par, tiles):
                dve.wait_ge(round_hi, n + 1)
                b = ps[:, round_bank(par), 0:P * len(tiles)]
                if tiles == [0]:
                    nc.vector.tensor_tensor(V[0:M, 1, 0, :], b[0:M], V[0:M, 0, 0, :], ALU.subtract).then_inc(round_lo, 1)
                else:
                    js = slice(tiles[0], tiles[-1] + 1)
                    nc.vector.tensor_tensor(V[:, 1, js, :], b.rearrange("p (j v) -> p j v", v=P), V[:, 0, js, :],
                                            ALU.subtract).then_inc(round_lo, 1)

            def attn_rounds(h, i):
                for r in range(len(rounds_of(i))):
                    attn_round(h, i, r)

            def attn_round(h, i, r):
                tiles = rounds_of(i)[r]
                n = ROUND_AT[i] + r
                dve.wait_ge(round_hi, RP + RH * h + n + 1)
                b = ps[:, round_bank(n), 0:P * len(tiles)].rearrange("p (j q) -> p j q", q=P)
                qs = slice(P * (i % 2), P * (i % 2) + P)
                full = [j for j in tiles if j]
                if i % 2 and i + 1 in full:
                    full = full[:-1]
                    ins = nc.vector.tensor_tensor(attn_d[:, 1, P:2 * P], b[:, len(full)], attn_d[:, 0, P:2 * P],
                                                  ALU.subtract)
                if full:
                    js = slice(full[0], full[-1] + 1)
                    ins = nc.vector.tensor_tensor(attn_t[:, 1, js, qs], b[:, 0:len(full)], attn_t[:, 0, js, qs],
                                                  ALU.subtract)
                if 0 in tiles:
                    ins = nc.vector.tensor_tensor(attn_t[:, 1, 0:1, qs], b[:, len(tiles) - 1:len(tiles)],
                                                  attn_t[:, 0, 0:1, qs], ALU.subtract)
                ins.then_inc(round_lo, 1)

            def scores_out(h, i, c):
                n = 2 * (NT * h + i) + c
                dve.wait_ge(s_mm, n + 1)
                nb, w = s_shape(i)
                e = E[i % 2][c][:, 0:nb * w].rearrange("p (b n) -> p b n", b=nb)
                bank = s_bank(i, c)
                nc.vector.tensor_scalar(e, ps[:, bank:bank + nb, 0:w], -SCALE, None, ALU.mult, ALU.min,
                                        accum_out=neg_max[:, i % 2, c:c + 1]).then_inc(s_out, 1)

            def inverse_sums(h, i):
                dve.wait_ge(exp_done, 2 * (NT * h + i) + 2)
                nc.vector.reciprocal(z_inv[:, i % 2, 0:2], z_sum[:, i % 2, :]).then_inc(recip_done, 1)
                dve.wait_ge(recip_done, NT * h + i + 1)
                nc.vector.tensor_tensor(z_inv[:, i % 2, 2:3], z_inv[:, i % 2, 1:2], lam_s[:, 7:8],
                                        ALU.mult).then_inc(inv_done, 1)

            def combine(h, i):
                dve.wait_ge(e1_scaled, NT * h + i + 1)
                nb, w = s_shape(i)
                nc.vector.scalar_tensor_tensor(out=E[i % 2][0][:, 0:nb * w], in0=E[i % 2][0][:, 0:nb * w],
                                               scalar=z_inv[:, i % 2, 0:1], in1=E[i % 2][1][:, 0:nb * w],
                                               op0=ALU.mult, op1=ALU.subtract).then_inc(attn_done, 1)

            def y_out(h):
                dve.wait_ge(or_done, h + 1)
                dve.wait_ge(z_silu, h + 1)
                dve.wait_ge(y_stored, 16 * (h + 1))
                nc.vector.scalar_tensor_tensor(out=y_o, in0=o_t, scalar=g_sub[:, 1:2], in1=z_act, op0=ALU.mult,
                                               op1=ALU.mult).then_inc(y_head, 1)

            def y_out_last():
                dve.wait_ge(o_copied, 4 * NH)
                dve.wait_ge(z_silu, NH)
                dve.wait_ge(y_stored, 16 * NH)
                nc.vector.scalar_tensor_tensor(out=y_o, in0=o_t, scalar=g_sub[:, 1:2], in1=z_act, op0=ALU.mult,
                                               op1=ALU.mult).then_inc(oz_done, 1)
                dve.wait_ge(oz_done, 1)
                dve.wait_ge(r_done, NH)
                nc.vector.tensor_tensor(y_o, y_o, r_o[:, 0:T], ALU.mult).then_inc(y_head, 1)

            def y4_lo_heads(slot):
                return nc.vector.tensor_tensor(ring[:, slot, 1, 0:NH - 1], y4[slot], ring[:, slot, 0, 0:NH - 1],
                                               ALU.subtract)

            dve.wait_ge(lam_done, 1)
            dve.wait_ge(out_mm, NT + 1)
            for part in range(2):
                nc.vector.memset(V[:, part, 0, :].bitcast(F32), 0.0).then_inc(v_zero, 1)
                nc.vector.memset(attn_d[:, part, 0:P].bitcast(F32), 0.0).then_inc(v_zero, 1)
            nc.vector.memset(neg_max[:], 0.0).then_inc(s_out, 1)
            nc.vector.memset(z_inv[:], 0.0).then_inc(y_head, 1)
            k_chunk_lo(0, 0)
            unit_lo(U1 + 2, SLOT["Q"])
            k_chunk_lo(0, 2, 2)
            k_chunk_lo(0, 1, 3)
            for r, tiles in enumerate(V_ROUNDS):
                round_lo_v(r, r, tiles)
            unit_lo(U1 + 3, SLOT["Z"])
            for c in range(2):
                q_chunk_lo(0, c)

            def scale_e1(h, i):
                dve.wait_ge(inv_done, NT * h + i + 1)
                e1 = E[i % 2][1][:, 0:s_shape(i)[0] * s_shape(i)[1]]
                nc.vector.tensor_scalar(e1, e1, z_inv[:, i % 2, 2:3], None, ALU.mult).then_inc(e1_scaled, 1)

            def head(h, last):
                u = U1 + 4 + UH * h
                for i in range(NT):
                    scores_out(h, i, 0)
                    if i >= 1:
                        combine(h, i - 1)
                    scores_out(h, i, 1)
                    if i:
                        inverse_sums(h, i)
                        if last:
                            scale_e1(h, i)
                    if not last and i == 3:
                        unit_lo(u + 1, SLOT["K"])
                    if i >= 1:
                        attn_rounds(h, i - 1)
                    if not last and i == 0:
                        unit_lo(u, SLOT["V"])
                    if i == 0:
                        inverse_sums(h, i)
                        if last:
                            scale_e1(h, i)
                combine(h, NT - 1)
                if not last:
                    unit_lo(u + 2, SLOT["Q"])
                    k_chunk_lo(h + 1, 0)
                if not last:
                    k_chunk_lo(h + 1, 1)
                attn_round(h, NT - 1, 0)
                attn_round(h, NT - 1, 1)
                attn_round(h, NT - 1, 2)
                if not last:
                    k_chunk_lo(h + 1, 2)
                    for r, tiles in enumerate(V_ROUNDS):
                        round_lo_v(RP + RH * h + 14 + r, 14 + r, tiles)
                        if r == 1:
                            unit_lo(u + 3, SLOT["Z"])
                    q_chunk_lo(h + 1, 0)
                if last:
                    y_out_last()
                else:
                    y_out(h)
                    q_chunk_lo(h + 1, 1)

            with dve.Fori(0, NH - 1) as h:
                head(h, False)
            head(NH - 1, True)

            def y4_lo_last(t, slot):
                nc.vector.tensor_tensor(ring[:, slot, 1, NH - 1], y_o[:, t * P:(t + 1) * P], ring[:, slot, 0, NH - 1],
                                        ALU.subtract).then_inc(y4_lo, 1)

            for t in range(2):
                dve.wait_ge(y4_hi, t + 1)
                y4_lo_last(t, t)
            for t in range(NT - 1):
                s = t % 2
                dve.wait_ge(out4_mm, t + 1)
                dve.wait_ge(h4_in[s], 16 * (t // 2 + 1))
                nc.vector.tensor_tensor(h4[s], flat(BANK4[s], D), h4[s], ALU.add).then_inc(h2_done, 1)
                if t + 2 < NT:
                    dve.wait_ge(y4_hi, t + 3)
                    y4_lo_heads(s)
                    y4_lo_last(t + 2, s)
                r = inverse_root(N4 + t, s)
                if t == 0:
                    dve.wait_ge(gf_in, 16)
                if t >= 2:
                    dve.wait_ge(o4_stored[s], 16 * (t // 2))
                nc.vector.scalar_tensor_tensor(out=o4[s], in0=h4[s], scalar=r, in1=g_final, op0=ALU.mult,
                                               op1=ALU.mult).then_inc(o4_done, 1)
            halves = [slice(HALF * c, HALF * (c + 1)) for c in range(2)]
            dve.wait_ge(out4_half, NT - 2)
            dve.wait_ge(h4_in[1], 16 * (NT // 2))
            nc.vector.tensor_tensor(h4[1][:, halves[0]], ps[:, BANK4[1], :], h4[1][:, halves[0]], ALU.add).then_inc(h2_half, 1)
            dve.wait_ge(end_sq_done, 1)
            nc.vector.tensor_scalar(end_sq[:, 1:2], end_sq[:, 0:1], 1.0 / D, EPS, ALU.mult, ALU.add).then_inc(end_mean, 1)
            dve.wait_ge(out4_mm, NT)
            nc.vector.tensor_tensor(h4[1][:, halves[1]], ps[:, BANK4[1] + 1, :], h4[1][:, halves[1]],
                                    ALU.add).then_inc(h2_done, 1)
            dve.wait_ge(end_mean, 1)
            r = inverse_root(N4 + NT - 1, 1, end_sq[:, 1:2])
            dve.wait_ge(o4_stored[1], 16 * (NT // 2 - 1))
            for half in halves:
                nc.vector.scalar_tensor_tensor(out=o4[1][:, half], in0=h4[1][:, half], scalar=r, in1=g_final[:, half],
                                               op0=ALU.mult, op1=ALU.mult).then_inc(o4_done, 1)


_INS = ['x', 'meta_tokens', 'a_norm_g', 'a_w_in', 'a_conv_w', 'a_conv_b', 'a_w_out', 'kv_norm_g', 'w_kv', 'b_norm_g',
        'b_w_in', 'b_lambda_q1', 'b_lambda_k1', 'b_lambda_q2', 'b_lambda_k2', 'b_subln_g', 'b_w_out', 'final_norm_g']


def kernel(**inputs):
    import numpy as _np
    import concourse.bacc as _bacc
    from concourse import mybir as _mybir
    from concourse.bass_utils import run_bass_kernel_spmd as _run

    nc = _bacc.Bacc("TRN2", target_bir_lowering=False, num_devices=1)
    arrays, args = {}, []
    for name in _INS:
        a = _np.ascontiguousarray(inputs[name])
        arrays[f"in_{name}_dram"] = a
        args.append(nc.dram_tensor(f"in_{name}_dram", a.shape, _mybir.dt.from_np(a.dtype), kind="ExternalInput").ap())
    args.append(nc.dram_tensor("out_0_dram", inputs["x"].shape, _mybir.dt.float32, kind="ExternalOutput").ap())
    yoco_kernel(nc, *args)
    r = _run(nc, [arrays], core_ids=[0])
    return r.results[0]["out_0_dram"]
```
